# Optimizing a Trainium2 kernel written in Bass

```python
import jax, jax.numpy as jnp
from jax import lax
import numpy as np
import math

D_MODEL = 1024
BATCH = 1
SEQ = 512
DEPTH = 1

CHUNK = 64
BAND_CHUNKS = 9
ATTN_HEADS = 8
HEAD_DIM = 64
ATTN_WIDTH = ATTN_HEADS * HEAD_DIM
POOL_WINDOWS = (2, 4, 8, 16)
POOL_GROUPS = len(POOL_WINDOWS)
POOL_WIDTH = D_MODEL // 2
POOL_GROUP_DIM = POOL_WIDTH // POOL_GROUPS
MAX_REL_DIST = 256
N_REL = 2 * MAX_REL_DIST + 1
D_FF = 2816
CONV_WIDTH = 3
N_BRANCH = 2
IN_WIDTH = 3 * ATTN_WIDTH + POOL_WIDTH + N_BRANCH * D_MODEL
EPS = 1e-6


def rms_norm(x, g):
    xf = x.astype(jnp.float32)
    y = xf * lax.rsqrt(jnp.mean(xf * xf, axis=-1, keepdims=True) + EPS)
    return (y * g.astype(jnp.float32)).astype(x.dtype)

def chunk_band_attention(q, k, v, rel_bias):
    b, s, h, dh = q.shape
    n_chunks = s // CHUNK
    band = BAND_CHUNKS * CHUNK
    lead = (BAND_CHUNKS - 1) * CHUNK
    pad = ((0, 0), (lead, 0), (0, 0), (0, 0))
    k_pad = jnp.pad(k, pad)
    v_pad = jnp.pad(v, pad)
    dist = jnp.arange(CHUNK)[:, None] + lead - jnp.arange(band)[None, :]
    idx = jnp.clip(dist, -MAX_REL_DIST, MAX_REL_DIST) + MAX_REL_DIST
    bias = rel_bias.astype(jnp.float32)[:, idx]
    scale = HEAD_DIM ** -0.5
    key_offsets = jnp.arange(band)

    def one_chunk(c):
        start = c * CHUNK
        q_c = lax.dynamic_slice_in_dim(q, start, CHUNK, axis=1)
        k_c = lax.dynamic_slice_in_dim(k_pad, start, band, axis=1)
        v_c = lax.dynamic_slice_in_dim(v_pad, start, band, axis=1)
        sc = jnp.einsum('bqhd,bkhd->bhqk', q_c, k_c,
                        preferred_element_type=jnp.float32) * scale + bias
        valid = (start - lead + key_offsets) >= 0
        sc = jnp.where(valid[None, None, None, :], sc, -1e30)
        p = jax.nn.softmax(sc, axis=-1).astype(v.dtype)
        return jnp.einsum('bhqk,bkhd->bqhd', p, v_c)

    out = lax.map(one_chunk, jnp.arange(n_chunks))
    return jnp.moveaxis(out, 0, 1).reshape(b, s, h * dh)

def multiscale_pool(u, w_group, scale):
    b, s, c = u.shape
    uf = u.astype(jnp.float32)
    max_w = max(POOL_WINDOWS)
    cs = jnp.pad(jnp.cumsum(uf, axis=1), ((0, 0), (max_w, 0), (0, 0)))
    t = jnp.arange(s)
    outs = []
    for g, w in enumerate(POOL_WINDOWS):
        sl = slice(g * POOL_GROUP_DIM, (g + 1) * POOL_GROUP_DIM)
        win = cs[:, max_w:, sl] - cs[:, max_w - w:max_w - w + s, sl]
        cnt = jnp.minimum(t + 1, w).astype(jnp.float32)[None, :, None]
        outs.append(win / cnt - uf[:, :, sl])
    pooled = jnp.stack(outs, axis=2).astype(u.dtype)
    mixed = jnp.einsum('bsgc,gcd->bsgd', pooled, w_group).reshape(b, s, c)
    return mixed * scale

def conv_gated_ffn(x, w_up, conv_w, conv_b, w_down):
    hu = x @ w_up
    s = hu.shape[1]
    hp = jnp.pad(hu, ((0, 0), (CONV_WIDTH - 1, 0), (0, 0)))
    hc = conv_b + conv_w[CONV_WIDTH - 1] * hu
    for i in range(CONV_WIDTH - 1):
        hc = hc + conv_w[i] * hp[:, i:i + s]
    val, gate = jnp.split(hc, 2, axis=-1)
    return (jax.nn.gelu(gate, approximate=True) * val) @ w_down

def first_inputs(seed: int = 0) -> dict:
    key = jax.random.key(seed)
    ks = jax.random.split(key, 20)
    f32 = jnp.float32

    def nrm(k, shape, s):
        return jax.random.normal(k, shape, f32) * s

    return {
        "x": jax.random.normal(ks[0], (BATCH, SEQ, D_MODEL), f32),
        "norm_mix_pre": 1.0 + nrm(ks[1], (DEPTH, D_MODEL), 0.05),
        "w_in": nrm(ks[2], (DEPTH, D_MODEL, IN_WIDTH), D_MODEL ** -0.5),
        "b_gate": nrm(ks[3], (DEPTH, N_BRANCH * D_MODEL), 0.01),
        "rel_bias": nrm(ks[4], (DEPTH, ATTN_HEADS, N_REL), 0.1),
        "w_attn_out": nrm(ks[5], (DEPTH, ATTN_WIDTH, D_MODEL), ATTN_WIDTH ** -0.5),
        "w_pool_group": nrm(ks[6], (DEPTH, POOL_GROUPS, POOL_GROUP_DIM, POOL_GROUP_DIM), POOL_GROUP_DIM ** -0.5),
        "pool_scale": 1.0 + nrm(ks[7], (DEPTH, POOL_WIDTH), 0.1),
        "w_pool_out": nrm(ks[8], (DEPTH, POOL_WIDTH, D_MODEL), POOL_WIDTH ** -0.5),
        "w_o": nrm(ks[9], (DEPTH, D_MODEL, D_MODEL), D_MODEL ** -0.5),
        "norm_mix_post": 1.0 + nrm(ks[10], (DEPTH, D_MODEL), 0.05),
        "norm_ffn_pre": 1.0 + nrm(ks[11], (DEPTH, D_MODEL), 0.05),
        "w_up": nrm(ks[12], (DEPTH, D_MODEL, 2 * D_FF), D_MODEL ** -0.5),
        "conv_w": nrm(ks[13], (DEPTH, CONV_WIDTH, 2 * D_FF), CONV_WIDTH ** -0.5),
        "conv_b": nrm(ks[14], (DEPTH, 2 * D_FF), 0.01),
        "w_down": nrm(ks[15], (DEPTH, D_FF, D_MODEL), D_FF ** -0.5),
        "norm_ffn_post": 1.0 + nrm(ks[16], (DEPTH, D_MODEL), 0.05),
    }

def first_block(x, norm_mix_pre, w_in, b_gate, rel_bias, w_attn_out, w_pool_group, pool_scale,
              w_pool_out, w_o, norm_mix_post, norm_ffn_pre, w_up, conv_w, conv_b, w_down,
              norm_ffn_post):
    b, s, _ = x.shape
    splits = [ATTN_WIDTH, 2 * ATTN_WIDTH, 3 * ATTN_WIDTH, 3 * ATTN_WIDTH + POOL_WIDTH]
    for l in range(DEPTH):
        h = rms_norm(x, norm_mix_pre[l])
        proj = h @ w_in[l]
        q, k, v, u, gates = jnp.split(proj, splits, axis=-1)
        q = q.reshape(b, s, ATTN_HEADS, HEAD_DIM)
        k = k.reshape(b, s, ATTN_HEADS, HEAD_DIM)
        v = v.reshape(b, s, ATTN_HEADS, HEAD_DIM)
        y_a = chunk_band_attention(q, k, v, rel_bias[l]) @ w_attn_out[l]
        y_b = multiscale_pool(u, w_pool_group[l], pool_scale[l]) @ w_pool_out[l]
        g_a, g_b = jnp.split(jax.nn.sigmoid(gates + b_gate[l]), N_BRANCH, axis=-1)
        mix = (g_a * y_a + g_b * y_b) @ w_o[l]
        x = x + rms_norm(mix, norm_mix_post[l])
        f = conv_gated_ffn(rms_norm(x, norm_ffn_pre[l]), w_up[l], conv_w[l], conv_b[l], w_down[l])
        x = x + rms_norm(f, norm_ffn_post[l])
    return x


D_MIX = D_MODEL
D_PLE = 256
DA = D_MIX // 2
HA = 4
DA_V = DA // HA
DA_QK = DA_V // 2
DB = D_MIX - DA
HB = 16
DB_H = DB // HB
D_IN = 3 * DA + 3 * DB
GRID_W = 64
WIN_R = 8
WIN_C = 16
Q_COLS = 16
K_COLS = 32
ROPE_THETA = 10000.0
Q_BLOCK = 128
NEG = -1e30
N_GROUPS = 4
EXPERTS_PER_GROUP = 8
N_EXPERTS = N_GROUPS * EXPERTS_PER_GROUP
TOP_K = 2
D_EXPERT = 512
MOE_BLOCK = 128


def rms_norm_2(x, g):
    xf = x.astype(jnp.float32)
    y = xf * lax.rsqrt(jnp.mean(xf * xf, axis=-1, keepdims=True) + EPS)
    return (y * g.astype(jnp.float32)).astype(x.dtype)

def rope_tables(seq, dim):
    inv = ROPE_THETA ** (-jnp.arange(0, dim, 2, dtype=jnp.float32) / dim)
    ang = jnp.arange(seq, dtype=jnp.float32)[:, None] * inv[None, :]
    return jnp.cos(ang), jnp.sin(ang)

def apply_rope(x, cos, sin):
    s = x.shape[1]
    bshape = (s,) + (1,) * (x.ndim - 3) + (-1,)
    c = cos.reshape(bshape)
    sn = sin.reshape(bshape)
    x1, x2 = jnp.split(x.astype(jnp.float32), 2, axis=-1)
    return jnp.concatenate([x1 * c - x2 * sn, x2 * c + x1 * sn], axis=-1).astype(x.dtype)

def diff_attention(q, k, v, g_q, g_k, lam_q1, lam_k1, lam_q2, lam_k2, g_sub, lam_init):
    b, s = q.shape[:2]
    cos, sin = rope_tables(s, DA_QK)
    q = apply_rope(rms_norm_2(q, g_q), cos, sin)
    k = apply_rope(rms_norm_2(k, g_k), cos, sin)
    lam = (jnp.exp(jnp.sum(lam_q1.astype(jnp.float32) * lam_k1.astype(jnp.float32)))
           - jnp.exp(jnp.sum(lam_q2.astype(jnp.float32) * lam_k2.astype(jnp.float32)))
           + lam_init)
    scale = DA_QK ** -0.5
    qt = q.transpose(0, 2, 1, 3, 4)
    kt = k.transpose(0, 2, 1, 3, 4)
    vt = v.transpose(0, 2, 1, 3)
    k1, k2 = kt[..., 0, :], kt[..., 1, :]
    nqb = s // Q_BLOCK
    qb = qt.reshape(b, HA, nqb, Q_BLOCK, 2, DA_QK).transpose(2, 0, 1, 3, 4, 5)

    def block(qblk):
        s1 = jnp.einsum('bhqd,bhkd->bhqk', qblk[..., 0, :], k1).astype(jnp.float32) * scale
        s2 = jnp.einsum('bhqd,bhkd->bhqk', qblk[..., 1, :], k2).astype(jnp.float32) * scale
        w = (jax.nn.softmax(s1, axis=-1) - lam * jax.nn.softmax(s2, axis=-1)).astype(vt.dtype)
        return jnp.einsum('bhqk,bhkd->bhqd', w, vt)

    o = lax.map(block, qb)
    o = o.transpose(1, 0, 3, 2, 4).reshape(b, s, HA, DA_V)
    o = rms_norm_2(o, g_sub) * (1.0 - lam_init)
    return o.reshape(b, s, HA * DA_V)

def neighbourhood_attention(q, k, v, g_q, g_k, rpb):
    b, s, h, d = q.shape
    rows = s // GRID_W
    kr = min(WIN_R, rows)
    ncb = GRID_W // Q_COLS
    q = rms_norm_2(q, g_q)
    k = rms_norm_2(k, g_k)
    r = np.arange(rows)
    rs = np.clip(r - kr // 2, 0, rows - kr)
    key_rows = rs[:, None] + np.arange(kr)[None, :]
    row_off = (key_rows - r[:, None] + (WIN_R - 1)).astype(np.int32)
    c = np.arange(GRID_W).reshape(ncb, Q_COLS)
    cs = np.clip(c - WIN_C // 2, 0, GRID_W - WIN_C)
    kb = np.minimum(cs[:, 0], GRID_W - K_COLS)
    key_cols = kb[:, None] + np.arange(K_COLS)[None, :]
    col_valid = ((key_cols[:, None, :] >= cs[:, :, None])
                 & (key_cols[:, None, :] < cs[:, :, None] + WIN_C))
    col_off = np.clip(key_cols[:, None, :] - c[:, :, None] + (WIN_C - 1), 0, 2 * WIN_C - 2)
    key_idx = (key_rows[:, None, :, None] * GRID_W + key_cols[None, :, None, :])
    key_idx = key_idx.reshape(rows, ncb * kr * K_COLS).astype(np.int32)
    bias_cols = rpb.astype(jnp.float32)[:, :, col_off]
    bias_cols = jnp.where(col_valid, bias_cols, NEG)
    scale = d ** -0.5
    q_rows = q.reshape(b, rows, GRID_W, h, d).transpose(1, 0, 2, 3, 4)

    def row_step(args):
        q_row, idx, roff = args
        qb = q_row.reshape(b, ncb, Q_COLS, h, d)
        kg = k[:, idx].reshape(b, ncb, kr * K_COLS, h, d)
        vg = v[:, idx].reshape(b, ncb, kr * K_COLS, h, d)
        bias = bias_cols[:, roff]
        bias = bias.transpose(0, 2, 3, 1, 4).reshape(h, ncb, Q_COLS, kr * K_COLS)
        sc = jnp.einsum('bjqhd,bjkhd->bhjqk', qb, kg).astype(jnp.float32) * scale + bias
        pr = jax.nn.softmax(sc, axis=-1).astype(vg.dtype)
        o = jnp.einsum('bhjqk,bjkhd->bjqhd', pr, vg)
        return o.reshape(b, GRID_W, h, d)

    o = lax.map(row_step, (q_rows, jnp.asarray(key_idx), jnp.asarray(row_off)))
    return o.transpose(1, 0, 2, 3, 4).reshape(b, s, h * d)

def hier_moe(x, w_rg, w_re, w1, w3, w2):
    b, s, dm = x.shape
    t = b * s
    xf = x.reshape(t, dm)
    g_prob = jax.nn.softmax((xf @ w_rg).astype(jnp.float32), axis=-1)
    g_gate, g_idx = lax.top_k(g_prob, 1)
    e_logits = (xf @ w_re).astype(jnp.float32).reshape(t, N_GROUPS, EXPERTS_PER_GROUP)
    e_logits = jnp.take_along_axis(e_logits, g_idx[:, :, None], axis=1)[:, 0]
    e_w, e_i = lax.top_k(jax.nn.softmax(e_logits, axis=-1), TOP_K)
    weights = g_gate * (e_w / jnp.sum(e_w, axis=-1, keepdims=True))
    experts = (g_idx * EXPERTS_PER_GROUP + e_i).astype(jnp.int32)
    n = t * TOP_K
    slot_e = experts.reshape(n)
    slot_tok = jnp.repeat(jnp.arange(t, dtype=jnp.int32), TOP_K)
    slot_w = weights.reshape(n)
    order = jnp.argsort(slot_e)
    se = slot_e[order]
    counts = jnp.zeros((N_EXPERTS,), jnp.int32).at[slot_e].add(1)
    starts = jnp.cumsum(counts) - counts
    padded = (counts + MOE_BLOCK - 1) // MOE_BLOCK * MOE_BLOCK
    pad_end = jnp.cumsum(padded)
    pad_start = pad_end - padded
    dest = pad_start[se] + jnp.arange(n, dtype=jnp.int32) - starts[se]
    n_blocks = n // MOE_BLOCK + N_EXPERTS
    p_len = n_blocks * MOE_BLOCK
    pad_tok = jnp.full((p_len,), t, jnp.int32).at[dest].set(slot_tok[order])
    pad_w = jnp.zeros((p_len,), jnp.float32).at[dest].set(slot_w[order])
    block_e = jnp.minimum(jnp.searchsorted(pad_end, jnp.arange(n_blocks, dtype=jnp.int32) * MOE_BLOCK,
                                           side='right'), N_EXPERTS - 1).astype(jnp.int32)
    xf_pad = jnp.concatenate([xf, jnp.zeros((1, dm), xf.dtype)], axis=0)
    xs = xf_pad[pad_tok].reshape(n_blocks, MOE_BLOCK, dm)

    def expert_block(args):
        xb, e = args
        hdn = jax.nn.silu(xb @ w1[e]) * (xb @ w3[e])
        return hdn @ w2[e]

    ys = lax.map(expert_block, (xs, block_e)).reshape(p_len, dm)
    out = jnp.zeros((t + 1, dm), ys.dtype).at[pad_tok].add(ys * pad_w[:, None].astype(ys.dtype))
    return out[:t].reshape(b, s, dm).astype(x.dtype)

def second_inputs(seed: int = 0) -> dict:
    key = jax.random.key(seed)
    ks = jax.random.split(key, 25)
    f = jnp.float32

    def nrm(k, shape, scale):
        return jax.random.normal(k, shape, f) * scale

    return {
        'x': nrm(ks[0], (BATCH, SEQ, D_MODEL), 1.0),
        'p': nrm(ks[1], (DEPTH, BATCH, SEQ, D_PLE), 1.0),
        'g_mix': 1.0 + nrm(ks[2], (DEPTH, D_MODEL), 0.02),
        'w_in': nrm(ks[3], (DEPTH, D_MODEL, D_IN), D_MODEL ** -0.5),
        'g_qa': 1.0 + nrm(ks[4], (DEPTH, DA_QK), 0.02),
        'g_ka': 1.0 + nrm(ks[5], (DEPTH, DA_QK), 0.02),
        'lam_q1': nrm(ks[6], (DEPTH, DA_QK), 0.1),
        'lam_k1': nrm(ks[7], (DEPTH, DA_QK), 0.1),
        'lam_q2': nrm(ks[8], (DEPTH, DA_QK), 0.1),
        'lam_k2': nrm(ks[9], (DEPTH, DA_QK), 0.1),
        'g_sub': 1.0 + nrm(ks[10], (DEPTH, DA_V), 0.02),
        'g_qb': 1.0 + nrm(ks[11], (DEPTH, DB_H), 0.02),
        'g_kb': 1.0 + nrm(ks[12], (DEPTH, DB_H), 0.02),
        'rpb': nrm(ks[13], (DEPTH, HB, 2 * WIN_R - 1, 2 * WIN_C - 1), 0.1),
        'w_out': nrm(ks[14], (DEPTH, D_MIX, D_MODEL), D_MIX ** -0.5),
        'g_ffn': 1.0 + nrm(ks[15], (DEPTH, D_MODEL), 0.02),
        'w_rg': nrm(ks[16], (DEPTH, D_MODEL, N_GROUPS), D_MODEL ** -0.5),
        'w_re': nrm(ks[17], (DEPTH, D_MODEL, N_EXPERTS), D_MODEL ** -0.5),
        'w1': nrm(ks[18], (DEPTH, N_EXPERTS, D_MODEL, D_EXPERT), D_MODEL ** -0.5),
        'w3': nrm(ks[19], (DEPTH, N_EXPERTS, D_MODEL, D_EXPERT), D_MODEL ** -0.5),
        'w2': nrm(ks[20], (DEPTH, N_EXPERTS, D_EXPERT, D_MODEL), D_EXPERT ** -0.5),
        'g_plg': 1.0 + nrm(ks[21], (DEPTH, D_MODEL), 0.02),
        'w_plg': nrm(ks[22], (DEPTH, D_MODEL, D_MODEL), D_MODEL ** -0.5),
        'w_ple': nrm(ks[23], (DEPTH, D_PLE, D_MODEL), D_PLE ** -0.5),
        'g_ple': 1.0 + nrm(ks[24], (DEPTH, D_MODEL), 0.02),
    }

def second_block(x, p, g_mix, w_in, g_qa, g_ka, lam_q1, lam_k1, lam_q2, lam_k2, g_sub, g_qb, g_kb,
              rpb, w_out, g_ffn, w_rg, w_re, w1, w3, w2, g_plg, w_plg, w_ple, g_ple):
    b, s, _ = x.shape
    h = x
    for i in range(DEPTH):
        lam_init = 0.8 - 0.6 * math.exp(-0.3 * i)
        a = rms_norm_2(h, g_mix[i])
        proj = a @ w_in[i]
        qa, ka, va, qb, kb, vb = jnp.split(proj, np.cumsum([DA, DA, DA, DB, DB])[:5].tolist(), axis=-1)
        oa = diff_attention(qa.reshape(b, s, HA, 2, DA_QK), ka.reshape(b, s, HA, 2, DA_QK),
                            va.reshape(b, s, HA, DA_V), g_qa[i], g_ka[i],
                            lam_q1[i], lam_k1[i], lam_q2[i], lam_k2[i], g_sub[i], lam_init)
        ob = neighbourhood_attention(qb.reshape(b, s, HB, DB_H), kb.reshape(b, s, HB, DB_H),
                                     vb.reshape(b, s, HB, DB_H), g_qb[i], g_kb[i], rpb[i])
        h = h + jnp.concatenate([oa, ob], axis=-1) @ w_out[i]
        h = h + hier_moe(rms_norm_2(h, g_ffn[i]), w_rg[i], w_re[i], w1[i], w3[i], w2[i])
        h = h + rms_norm_2(p[i] @ w_ple[i], g_ple[i]) * jax.nn.sigmoid(rms_norm_2(h, g_plg[i]) @ w_plg[i])
    return h


def setup_inputs(seed=0):
    out = dict(first_inputs(seed))
    for name, value in second_inputs(seed + 1).items():
        if name != "x":
            out[name + "_2"] = value
    return out


def reference(
    x, norm_mix_pre, w_in, b_gate, rel_bias, w_attn_out, w_pool_group, pool_scale, w_pool_out,
    w_o, norm_mix_post, norm_ffn_pre, w_up, conv_w, conv_b, w_down, norm_ffn_post, p_2, g_mix_2,
    w_in_2, g_qa_2, g_ka_2, lam_q1_2, lam_k1_2, lam_q2_2, lam_k2_2, g_sub_2, g_qb_2, g_kb_2,
    rpb_2, w_out_2, g_ffn_2, w_rg_2, w_re_2, w1_2, w3_2, w2_2, g_plg_2, w_plg_2, w_ple_2,
    g_ple_2,
):
    x = first_block(
        x, norm_mix_pre, w_in, b_gate, rel_bias, w_attn_out, w_pool_group, pool_scale,
        w_pool_out, w_o, norm_mix_post, norm_ffn_pre, w_up, conv_w, conv_b, w_down,
        norm_ffn_post,
    )
    return second_block(
        x, p_2, g_mix_2, w_in_2, g_qa_2, g_ka_2, lam_q1_2, lam_k1_2, lam_q2_2, lam_k2_2,
        g_sub_2, g_qb_2, g_kb_2, rpb_2, w_out_2, g_ffn_2, w_rg_2, w_re_2, w1_2, w3_2, w2_2,
        g_plg_2, w_plg_2, w_ple_2, g_ple_2,
    )


_drawn_inputs = setup_inputs


def setup_inputs(seed=0):
    import zlib

    import numpy as np

    out = dict(_drawn_inputs(seed))
    spreads = {}
    factors = {'b_gate': 7.363,
     'rel_bias': 3.162,
     'conv_b': 3.314,
     'g_mix_2': 3.873,
     'g_qa_2': 4.955,
     'g_ka_2': 4.646,
     'lam_q1_2': 3.019,
     'g_sub_2': 5.012,
     'g_qb_2': 8.0,
     'g_kb_2': 8.0,
     'rpb_2': 5.716,
     'g_ffn_2': 3.219,
     'g_plg_2': 32.985,
     'g_ple_2': 35.725}
    for name, (base, spread) in spreads.items():
        noise = np.random.default_rng([zlib.crc32(name.encode()), seed]).standard_normal(out[name].shape)
        drawn = base * np.exp(spread * noise) if base else spread * noise
        out[name] = __import__('jax').numpy.asarray(drawn.astype(out[name].dtype))
    for name, factor in factors.items():
        out[name] = (out[name] * factor).astype(out[name].dtype)
    return out
```

```python
from collections import deque
from contextlib import ExitStack

import numpy as np

import concourse.bass as bass
from concourse import mybir

F32 = mybir.dt.float32
I32 = mybir.dt.int32
ACT = mybir.ActivationFunctionType
ALU = mybir.AluOpType
AX = mybir.AxisListType.X

NTOK, D = 512, 1024
TT, KD = 4, 8
FF = 2816
NP_FF = FF // 128
CHUNKS = [6, 6, 6, 4]
UNIT = 2048
NS = 6
NS_MOE = 8
NE = 32
NPAIR = NE // 2
C = 64
EPS = 1e-6
NEG = -1e30

COLS = {}
_o = 0
for _n, _w in (("mix_pre", 8), ("ffn_pre", 8), ("mix2", 8), ("ffn2", 8), ("plg", 8), ("b_gate", 16),
               ("pool_scale", 4), ("conv_w", 132), ("conv_b", 44), ("g_sub", 1)):
    COLS[_n] = (_o, _w)
    _o += _w
NCOLS = _o
ROWS = {}
_o = 0
for _n, _w in (("mix_post", 1024), ("ffn_post", 1024), ("ple", 1024), ("qa", 64), ("ka", 64), ("qb", 32),
               ("kb", 32), ("lq1", 64), ("lk1", 64), ("lq2", 64), ("lk2", 64)):
    ROWS[_n] = (_o, _w)
    _o += _w
NROWS = _o
CST = {}
_o = 0
for _n, _w in (("ident", 128), ("tri", 128), ("ones", 128), ("iota", 64), ("thr", 8), ("cnt", 64),
               ("cos", 128), ("sin", 128)):
    CST[_n] = (_o, _w)
    _o += _w
NCST = _o


class Queue:

    def __init__(self, sem):
        self.sem, self.n, self.items, self.waited = sem, 0, [], {}

    def wait(self, *after):
        for t in after:
            if t is None:
                continue
            if isinstance(t, list):
                self.wait(*t)
                continue
            sem, v = t
            if self.waited.get(sem.name, 0) < v:
                self.waited[sem.name] = v
                self.items.append(lambda e, sem=sem, v=v: e.wait_ge(sem, v))

    def __call__(self, fn, *after, sig=True):
        self.wait(*after)
        if not sig:
            self.items.append(fn)
            return None
        self.n += 1
        self.items.append(lambda e: fn(e).then_inc(self.sem, 1))
        return (self.sem, self.n)

    def dma(self, out, in_, sem, n, *after):
        self.wait(*after)
        self.items.append(lambda e: e.dma_start(out, in_).then_inc(sem, 16))
        return (sem, 16 * n)

    def run(self, e):
        for f in self.items:
            f(e)


class Ring:

    def __init__(self, bufs, after=None):
        self.free = deque((b, after) for b in bufs)

    def take(self):
        return self.free.popleft()

    def give(self, b, tok):
        self.free.append((b, tok))


def build(nc, x_d, wd, w1_d, w3_d, w2_d, cols_d, rows_d, cst_d, wr_d, wpg_d, pT_d, tb_d, nb_d, out_d):
    with ExitStack() as ctx:
        def sb(name, shape, dt=F32):
            return ctx.enter_context(nc.sbuf_tensor(name, shape, dt))

        def sem(name):
            return ctx.enter_context(nc.semaphore(name))

        ring_t = sb("ring", [128, NS * UNIT])
        X = sb("X", [128, TT, D])
        HT = sb("HT", [128, KD, NTOK])
        cols = sb("cols", [128, NCOLS])
        rows = sb("rows", [128, NROWS])
        cst = sb("cst", [128, NCST])
        wr = sb("wr", [128, KD, 36])
        wpg = sb("wpg", [128, 4, 128])
        st = sb("st", [128, 1600])
        route = sb("route", [128, 1600])
        nex_i = sb("nex_i", [1, 1], I32)
        NA_SZ = 22528
        arena = sb("arena", [128, NA_SZ])
        bank = [ctx.enter_context(nc.psum_tensor(f"bank{i}", [128, 512], F32)) for i in range(8)]

        def col(name, i=0, n=1):
            o = COLS[name][0]
            return cols[:, o + i:o + i + n]

        def row(name):
            o, w = ROWS[name]
            return rows[:, o:o + w]

        def con(name):
            o, w = CST[name]
            return cst[:, o:o + w]

        ident = con("ident")

        def region(o, *shape):
            n = int(np.prod(shape))
            assert o + n <= NA_SZ, (o, shape)
            v = arena[:, o:o + n]
            if len(shape) == 2:
                v = v.rearrange("p (a b) -> p a b", a=shape[0])
            if len(shape) == 3:
                v = v.rearrange("p (a b c) -> p a b c", a=shape[0], b=shape[1])
            return v

        s_pe, s_act, s_dve, s_pool, s_sp = (sem(n) for n in ("s_pe", "s_act", "s_dve", "s_pool", "s_sp"))
        pe, act, dve, pool, sp = Queue(s_pe), Queue(s_act), Queue(s_dve), Queue(s_pool), Queue(s_sp)
        engines = (pe, act, dve, pool)

        def everything():
            return [(q.sem, q.n) for q in engines if q.n]

        misc = {}

        def load(q, name, out, in_, *after):
            misc[name] = q.dma(out, in_, sem("d_" + name), 1, *after)
            return misc[name]

        banks = Ring(list(range(8)))

        units = []
        where = {}

        def plan(key, src):
            where[key] = len(units)
            units.append(src)

        nd = [0]

        def dense(key):
            plan(key, wd[nd[0], :, :])
            nd[0] += 1

        for key in [("in", i) for i in range(8)]:
            dense(key)
        for i in range(2):
            dense(("ao", i))
            dense(("po", i))
        for i in range(4):
            dense(("ga", i))
            dense(("gb", i))
        for i in range(4):
            dense(("wo", i))
        u = 0
        dn = 0
        for n in CHUNKS:
            for _ in range(n // 2):
                dense(("uv", u))
                dense(("ug", u))
                u += 1
            for _ in range(n // 2):
                dense(("dn", dn))
                dn += 1
        for i in range(12):
            dense(("in2", i))
        for i in range(4):
            dense(("out2", i))
        ND1 = len(units)

        def expert(w, e, kh):
            if w == 2:
                src = w2_d[e, kh * 256:(kh + 1) * 256, :].rearrange("(k p) n -> p k n", p=128)
            else:
                src = (w1_d if w == 1 else w3_d)[e, kh * 512:(kh + 1) * 512, :].rearrange("(k p) n -> p k n", p=128)
            plan(("e", w, e, kh), src)

        for p in range(NPAIR + 1):
            for w in (1, 3):
                if p < NPAIR:
                    for kh in range(2):
                        for e in (2 * p, 2 * p + 1):
                            expert(w, e, kh)
            if p >= 1:
                for kh in range(2):
                    for e in (2 * p - 2, 2 * p - 1):
                        expert(2, e, kh)
        dense(("ple", 0))
        for i in range(4):
            dense(("plg", i))

        slots = [ring_t[:, i * UNIT:(i + 1) * UNIT] for i in range(NS)]
        slot_sem = [sem(f"d_w{i}") for i in range(NS_MOE)]
        slot_n = [0] * NS_MOE
        slot_of = {}
        ready = {}
        free_slots = deque((i, None) for i in range(NS))
        issued = [0]
        limit = [ND1]

        def issue():
            while free_slots and issued[0] < limit[0]:
                i, tok = free_slots.popleft()
                n = issued[0]
                src = units[n]
                dst = slots[i]
                if len(src.shape) == 3:
                    dst = dst.rearrange("p (k n) -> p k n", k=src.shape[1])
                slot_n[i] += 1
                slot_of[n] = i
                ready[n] = sp.dma(dst, src, slot_sem[i], slot_n[i], tok)
                issued[0] += 1

        def W(key, k):
            n = where[key]
            return slots[slot_of[n]].rearrange("p (k n) -> p k n", k=k), ready[n]

        def Wdone(key, tok):
            free_slots.append((slot_of[where[key]], tok))
            issue()

        for t in range(TT):
            load(pool, f"x{t}", X[:, t, :], x_d[t * 128:(t + 1) * 128, :])
        load(pool, "cst", cst[:, :], cst_d)
        load(pool, "cols", cols[:, :], cols_d)
        issue()

        o_st = [0]

        def stat(n=1):
            a = st[:, o_st[0]:o_st[0] + n]
            o_st[0] += n
            assert o_st[0] <= 1600
            return a

        def rstd_of(ss, n, div, *after):
            ms, sq, r = stat(n), stat(n), stat(n)
            a = dve(lambda e: e.tensor_scalar(ms, ss, 1.0 / div, EPS, ALU.mult, ALU.add), *after)
            b = act(lambda e: e.activation(sq, ms, ACT.Sqrt), a)
            return r, dve(lambda e: e.reciprocal(r, sq), b)

        junk = sb("junk", [128, 4, D // 2], mybir.dt.bfloat16)
        junk_r = Ring([junk[:, i, :] for i in range(4)])

        def sumsq(src, ss, *after):
            out = []
            for i in range(ss.shape[1]):
                j, jf = junk_r.take()
                a = act(lambda e, i=i, j=j: e.activation(j, src(i), ACT.Square, accum_out=ss[:, i:i + 1]), jf, *after)
                junk_r.give(j, a)
                out.append(a)
            return out

        def norm_to_T(gname, xt, xs, dst, dst_after, keep=None):
            ss2, ss = stat(2 * TT), stat(TT)
            toks = [sumsq(lambda i, t=t: X[:, t, i * 512:(i + 1) * 512], ss2[:, 2 * t:2 * t + 2], xt[t])
                    for t in range(TT)]
            a = dve(lambda e: e.tensor_reduce(ss, ss2.rearrange("p (t h) -> p t h", h=2), AX, ALU.add), toks)
            r, rt = rstd_of(ss, TT, D, a)
            out, kept = [], []
            for t in range(TT):
                buf, free = (keep[:, t, :], dst_after) if keep is not None else xs.take()
                a = dve(lambda e, t=t, buf=buf: e.tensor_scalar(buf, X[:, t, :], r[:, t:t + 1], None, ALU.mult),
                        rt, free)
                kept.append(a)
                for h in range(2):
                    b, bf = banks.take()
                    for k in range(4):
                        m = pe(lambda e, k=k, b=b, h=h, buf=buf: e.transpose(
                            bank[b][:, k * 128:(k + 1) * 128], buf[:, (4 * h + k) * 128:(4 * h + k + 1) * 128], ident),
                            a, bf, misc["cst"], sig=(k == 3))
                    g = col(gname, 4 * h, 4).unsqueeze(2).to_broadcast([128, 4, 128])
                    d = dve(lambda e, b=b, h=h, t=t, g=g: e.tensor_tensor(
                        dst[:, 4 * h:4 * h + 4, t * 128:(t + 1) * 128],
                        bank[b][:, :].rearrange("p (k n) -> p k n", k=4), g, ALU.mult),
                        m, misc["cols"], dst_after)
                    banks.give(b, d)
                    out.append(d)
                if keep is None:
                    xs.give(buf, m)
            return (out, kept) if keep is not None else out

        def gemm_T(key, nk, n0, src, after, b, bf, mcols=128):
            w, wt = W(key, nk)
            for k in range(nk):
                m = pe(lambda e, k=k: e.matmul(bank[b][:, :], w[:, k, n0:n0 + mcols], src[:, k, :],
                                               start=(k == 0), stop=(k == nk - 1)),
                       wt, after, bf, sig=(k == nk - 1))
            return m

        def gemm_tok(keys, src, after, t, b, bf):
            for j, key in enumerate(keys):
                w, wt = W(key, KD)
                for k in range(KD):
                    m = pe(lambda e, k=k, w=w, j=j: e.matmul(
                        bank[b][:, j * 256:(j + 1) * 256], src[:, k, t * 128:(t + 1) * 128], w[:, k, :],
                        start=(k == 0), stop=(k == KD - 1)), wt, after, bf, sig=(k == KD - 1))
            return m

        flip = [0]

        def evac(dst, src, after, scale=None):
            flip[0] ^= 1
            if flip[0]:
                if scale is None:
                    return act(lambda e: e.activation(dst, src, ACT.Copy), after)
                return act(lambda e: e.activation(dst, src, ACT.Copy, scale=scale), after)
            if scale is None:
                return dve(lambda e: e.tensor_copy(dst, src), after)
            return dve(lambda e: e.tensor_scalar(dst, src, scale, None, ALU.mult), after)

        qT = region(0, 4, 512)
        kT = region(2048, 4, 512)
        V = region(4096, 4, 512)
        U = region(6144, 4, 528)
        TB = region(8256, 8, 512)
        sc_r = [region(12352 + 512 * i, 512) for i in range(2)]
        P_r = [region(13376 + 512 * i, 512) for i in range(3)]
        PT_r = [region(14912 + 512 * i, 512) for i in range(3)]
        attnT = region(16448, 4, 512)
        mixedT = region(18496, 4, 512)
        ps_r = [region(20544 + 528 * i, 528) for i in range(3)]
        load(pool, "wpg", wpg[:, :, :], wpg_d)
        load(pool, "tb", TB, tb_d)
        load(pool, "rows", rows[:, :], rows_d.to_broadcast([128, NROWS]))
        load(pool, "wr", wr[:, :, :], wr_d)

        xs_ring = Ring([region(12352 + 1024 * i, 1024) for i in range(3)])
        xt = [misc[f"x{t}"] for t in range(TT)]
        hT_t = norm_to_T("mix_pre", xt, xs_ring, HT, None)
        free1 = everything()

        zu = pool(lambda e: e.memset(U[:, :, 0:16], 0.0))
        qk_t = {}
        for i in range(4):
            for j in range(2):
                n = 2 * i + j
                b, bf = banks.take()
                m = gemm_T(("in", i), KD, j * 128, HT, hT_t, b, bf)
                dst = qT[:, n, :] if n < 4 else kT[:, n - 4, :]
                qk_t[n] = evac(dst, bank[b][:, :], m, 0.125 if n < 4 else None)
                banks.give(b, qk_t[n])
            Wdone(("in", i), m)
        v_t = []
        for t in range(TT):
            b, bf = banks.take()
            m = gemm_tok([("in", 4), ("in", 5)], HT, hT_t, t, b, bf)
            v_t.append(evac(V[:, t, :], bank[b][:, :], m))
            banks.give(b, v_t[-1])
        Wdone(("in", 4), m)
        Wdone(("in", 5), m)
        u_t = []
        for i in range(2):
            for j in range(2):
                g = 2 * i + j
                b, bf = banks.take()
                m = gemm_T(("in", 6 + i), KD, j * 128, HT, hT_t, b, bf)
                u_t.append(evac(U[:, g, 16:528], bank[b][:, :], m))
                banks.give(b, u_t[-1])
            Wdone(("in", 6 + i), m)

        def pool_group(g):
            cur, cur_t = U[:, g, :], [u_t[g], zu]
            lo = 0
            for s in range(g + 1):
                d = 1 << s
                nxt = ps_r[s % 2]
                lo2 = lo + d
                cur_t = [pool(lambda e, cur=cur, nxt=nxt, d=d, lo2=lo2: e.tensor_tensor(
                    nxt[:, lo2:528], cur[:, lo2:528], cur[:, lo2 - d:528 - d], ALU.add), cur_t, free1)]
                cur, lo = nxt, lo2
            w = 2 << g
            pl = ps_r[2][:, 0:512]
            mean = pool(lambda e: e.tensor_scalar(pl, cur[:, 16:528], 1.0 / w, None, ALU.mult), cur_t, pg_free[0])
            cn = con("cnt")[:, 16 * g:16 * g + w - 1]
            fix = pool(lambda e: e.tensor_tensor(pl[:, 0:w - 1], cur[:, 16:16 + w - 1], cn, ALU.mult),
                       mean, misc["cst"])
            sub = pool(lambda e: e.tensor_tensor(pl, pl, U[:, g, 16:528], ALU.subtract), fix)
            b, bf = banks.take()
            m = pe(lambda e: e.matmul(bank[b][:, :], wpg[:, g, :], pl, start=True, stop=True), sub, bf, misc["wpg"])
            pg_free[0] = m
            d = act(lambda e: e.activation(mixedT[:, g, :], bank[b][:, :], ACT.Copy, scale=col("pool_scale", g)),
                    m, misc["cols"])
            banks.give(b, d)
            return d

        pg_free = [None]
        mixed_t = []

        sc_ring, P_ring, PT_ring = (Ring(r, free1) for r in (sc_r, P_r, PT_r))
        items = [(h, qt) for h in range(8) for qt in range(4)]
        ob = {}
        state = {}
        attn_t = []

        def a0(i):
            h, qt = items[i]
            nk, pr, hp = 128 * (qt + 1), 64 * (h % 2), h // 2
            b, bf = banks.take()
            m = pe(lambda e: e.matmul(bank[b][:, 0:nk], qT[pr:pr + 64, hp, qt * 128:(qt + 1) * 128],
                                      kT[pr:pr + 64, hp, 0:nk], start=True, stop=True),
                   bf, qk_t[hp], qk_t[4 + hp])
            sc, sf = sc_ring.take()
            P, pf = P_ring.take()
            mx, nm, rs, rr = stat(), stat(), stat(), stat()
            a = dve(lambda e: e.tensor_tensor_reduce(sc[:, 0:nk], bank[b][:, 0:nk], TB[:, h, 384 - 128 * qt:512], 1.0,
                                                     -3e38, ALU.add, ALU.max, mx), m, sf, misc["tb"])
            banks.give(b, a)
            c = dve(lambda e: e.tensor_scalar(nm, mx, -1.0, None, ALU.mult), a)
            ex = act(lambda e: e.activation(P[:, 0:nk], sc[:, 0:nk], ACT.Exp, bias=nm, accum_out=rs), c, pf)
            sc_ring.give(sc, ex)
            r = dve(lambda e: e.reciprocal(rr, rs), ex)
            n = dve(lambda e: e.tensor_scalar(P[:, 0:nk], P[:, 0:nk], rr, None, ALU.mult), r)
            state[i] = (P, n)

        def a1(i):
            h, qt = items[i]
            P, n = state[i]
            b, bf = banks.take()
            for k in range(qt + 1):
                m = pe(lambda e, k=k: e.transpose(bank[b][:, k * 128:(k + 1) * 128], P[:, k * 128:(k + 1) * 128],
                                                  ident), n, bf, sig=(k == qt))
            P_ring.give(P, m)
            PT, pf = PT_ring.take()
            nk = 128 * (qt + 1)
            ev = act(lambda e: e.activation(PT[:, 0:nk], bank[b][:, 0:nk], ACT.Copy), m, pf)
            banks.give(b, ev)
            state[i] = (PT, ev)

        def a2(i):
            h, qt = items[i]
            PT, ev = state[i]
            pr, hp = 64 * (h % 2), h // 2
            if hp not in ob:
                ob[hp] = banks.take()
            b, bf = ob[hp]
            for k in range(qt + 1):
                m = pe(lambda e, k=k: e.matmul(bank[b][pr:pr + 64, qt * 128:(qt + 1) * 128],
                                               V[:, k, h * 64:(h + 1) * 64], PT[:, k * 128:(k + 1) * 128],
                                               start=(k == 0), stop=(k == qt)), ev, bf, v_t, sig=(k == qt))
            PT_ring.give(PT, m)
            if h % 2 and qt == 3:
                d = dve(lambda e: e.tensor_copy(attnT[:, hp, :], bank[b][:, :]), m)
                banks.give(b, d)
                attn_t.append(d)

        for i in range(len(items) + 2):
            if i < len(items):
                a0(i)
            if 1 <= i <= len(items):
                a1(i - 1)
            if i >= 2:
                a2(i - 2)
            if i % 8 == 4 and i // 8 < 4:
                mixed_t.append(pool_group(i // 8))
        free2 = everything()

        MT = region(0, 8, 512)
        g_ring = Ring([region(8256 + 512 * i, 512) for i in range(8)], free2)
        mt_t = []
        for n in range(8):
            bs = [banks.take() for _ in range(4)]
            ka, kb = ("ga", n // 2), ("gb", n // 2)
            ma = gemm_T(ka, KD, (n % 2) * 128, HT, hT_t, *bs[0])
            mb = gemm_T(kb, KD, (n % 2) * 128, HT, hT_t, *bs[1])
            mya = gemm_T(("ao", n // 4), 4, (n % 4) * 128, attnT, attn_t, *bs[2])
            myb = gemm_T(("po", n // 4), 4, (n % 4) * 128, mixedT, mixed_t, *bs[3])
            if n % 2:
                Wdone(ka, ma)
                Wdone(kb, mb)
            if n % 4 == 3:
                Wdone(("ao", n // 4), mya)
                Wdone(("po", n // 4), myb)
            (ga, fa), (gb, fb) = g_ring.take(), g_ring.take()
            sa = act(lambda e, n=n, b=bs[0][0], ga=ga: e.activation(ga, bank[b][:, :], ACT.Sigmoid,
                                                                    bias=col("b_gate", n)), ma, fa)
            banks.give(bs[0][0], sa)
            sg = act(lambda e, n=n, b=bs[1][0], gb=gb: e.activation(gb, bank[b][:, :], ACT.Sigmoid,
                                                                    bias=col("b_gate", 8 + n)), mb, fb)
            banks.give(bs[1][0], sg)
            ta = dve(lambda e, b=bs[2][0], ga=ga: e.tensor_tensor(ga, bank[b][:, :], ga, ALU.mult), sa, mya)
            banks.give(bs[2][0], ta)
            tb_ = dve(lambda e, b=bs[3][0], gb=gb: e.tensor_tensor(gb, bank[b][:, :], gb, ALU.mult), sg, myb)
            banks.give(bs[3][0], tb_)
            d = pool(lambda e, n=n, ga=ga, gb=gb: e.tensor_tensor(MT[:, n, :], ga, gb, ALU.add), ta, tb_, free2)
            g_ring.give(ga, d)
            g_ring.give(gb, d)
            mt_t.append(d)

        def residual(halves, gname, tt, scratch, *more):
            ss, s1 = stat(2), stat()
            tmp, tf = scratch
            q = sumsq(lambda i: halves[i][0], ss, halves[0][1], halves[1][1])
            a = dve(lambda e: e.tensor_tensor(s1, ss[:, 0:1], ss[:, 1:2], ALU.add), q)
            r, rt = rstd_of(s1, 1, D, a)
            o = ROWS[gname][0]
            z = [dve(lambda e, h=h: e.scalar_tensor_tensor(
                out=tmp[:, h * 512:(h + 1) * 512], in0=halves[h][0], scalar=r,
                in1=rows[:, o + h * 512:o + (h + 1) * 512], op0=ALU.mult, op1=ALU.mult),
                rt, tf, misc["rows"]) for h in range(2)]
            f = pool(lambda e: e.tensor_tensor(X[:, tt, :], X[:, tt, :], tmp, ALU.add), z, *more)
            return z, f

        free_s = everything()
        tmp_ring = Ring([region(16448 + 1024 * i, 1024) for i in range(4)], free_s)
        x_t = []
        held = {}
        for h in range(2):
            for t in range(TT):
                b, bf = banks.take()
                m = gemm_tok([("wo", 2 * h), ("wo", 2 * h + 1)], MT, mt_t, t, b, bf)
                held[t, h] = (b, m)
            Wdone(("wo", 2 * h), m)
            Wdone(("wo", 2 * h + 1), m)
        for t in range(TT):
            tmp, tf = tmp_ring.take()
            z, f = residual([(bank[held[t, h][0]][:, :], held[t, h][1]) for h in range(2)], "mix_post", t, (tmp, tf))
            for h in range(2):
                banks.give(held[t, h][0], z[h])
            tmp_ring.give(tmp, f)
            x_t.append(f)
        free3 = everything()

        xs_ring = Ring([region(12352 + 1024 * i, 1024) for i in range(3)], free3)
        hT_t = norm_to_T("ffn_pre", x_t, xs_ring, HT, free3)
        free4 = everything()
        ACTV = [region(6144 * 0 + 3072 * i, 6, 512) for i in range(2)]
        FACC = region(6144, 4, 1024)
        zv_ring = Ring([region(10240 + 512 * i, 512) for i in range(3)], free4)
        zg_ring = Ring([region(11776 + 512 * i, 512) for i in range(3)], free4)
        av_free = [free4, free4]
        facc_t = {(t, h): free4 for t in range(TT) for h in range(2)}
        pair = 0
        dn = 0

        def conv(b, m, z, zf, n):
            cw = [col("conv_w", i * 44 + n) for i in range(3)]
            a = act(lambda e: e.activation(z, bank[b][:, :], ACT.Identity, bias=col("conv_b", n), scale=cw[2]), m, zf)
            c = dve(lambda e: e.scalar_tensor_tensor(out=z[:, 2:512], in0=bank[b][:, 0:510], scalar=cw[0],
                                                     in1=z[:, 2:512], op0=ALU.mult, op1=ALU.add), a)
            d = dve(lambda e: e.scalar_tensor_tensor(out=z[:, 1:512], in0=bank[b][:, 0:511], scalar=cw[1],
                                                     in1=z[:, 1:512], op0=ALU.mult, op1=ALU.add), c)
            banks.give(b, d)
            return d

        def up(c, n):
            nonlocal pair
            A, af = ACTV[c % 2], av_free[c % 2]
            at = []
            for i in range(n):
                uu, j = pair // 2, pair % 2
                b1, f1 = banks.take()
                mv = gemm_T(("uv", uu), KD, j * 128, HT, hT_t, b1, f1)
                b2, f2 = banks.take()
                mg = gemm_T(("ug", uu), KD, j * 128, HT, hT_t, b2, f2)
                if j:
                    Wdone(("uv", uu), mv)
                    Wdone(("ug", uu), mg)
                (zv, fv), (zg, fg) = zv_ring.take(), zg_ring.take()
                dg = conv(b2, mg, zg, fg, 22 + pair)
                dv = conv(b1, mv, zv, fv, pair)
                ge = act(lambda e, zg=zg: e.activation(zg, zg, ACT.Gelu_apprx_tanh), dg)
                o = pool(lambda e, i=i, A=A, zg=zg, zv=zv: e.tensor_tensor(A[:, i, :], zg, zv, ALU.mult), ge, dv, af)
                zv_ring.give(zv, o)
                zg_ring.give(zg, o)
                at.append(o)
                pair += 1
            return at

        def down(c, n, at):
            nonlocal dn
            A = ACTV[c % 2]
            for t in range(TT):
                for h in range(2):
                    b, bf = banks.take()
                    for i in range(n):
                        w, wt = W(("dn", dn + i // 2), 2)
                        m = pe(lambda e, i=i, w=w, t=t, h=h, b=b: e.matmul(
                            bank[b][:, :], A[:, i, t * 128:(t + 1) * 128], w[:, i % 2, h * 512:(h + 1) * 512],
                            start=(i == 0), stop=(i == n - 1)), wt, bf, at[i], sig=(i == n - 1))
                    dst = FACC[:, t, h * 512:(h + 1) * 512]
                    if c == 0:
                        f = dve(lambda e, dst=dst, b=b: e.tensor_copy(dst, bank[b][:, :]), m, facc_t[t, h])
                    else:
                        f = dve(lambda e, dst=dst, b=b: e.tensor_tensor(dst, bank[b][:, :], dst, ALU.add), m,
                                facc_t[t, h])
                    banks.give(b, f)
                    facc_t[t, h] = f
            av_free[c % 2] = m
            for i in range(n // 2):
                Wdone(("dn", dn + i), m)
            dn += n // 2

        prev = None
        for c, n in enumerate(CHUNKS):
            at = up(c, n)
            if prev is not None:
                down(*prev)
            prev = (c, n, at)
        down(*prev)

        tmp_ring = Ring([region(16448 + 1024 * i, 1024) for i in range(4)], free4)
        x_t = []
        for t in range(TT):
            tmp, tf = tmp_ring.take()
            z, f = residual([(FACC[:, t, h * 512:(h + 1) * 512], facc_t[t, h]) for h in range(2)], "ffn_post", t,
                            (tmp, tf))
            tmp_ring.give(tmp, f)
            x_t.append(f)
        free5 = everything()

        xs_ring = Ring([region(12352 + 1024 * i, 1024) for i in range(3)], free5)
        aT_t = norm_to_T("mix2", x_t, xs_ring, HT, free5)
        free6 = everything()

        qaT, kaT = region(0, 4, 512), region(2048, 4, 512)
        qbT, kbT = region(4096, 4, 512), region(6144, 4, 512)
        Va = region(8192, 4, 512)
        Vj = region(10240, 8, 512)
        sqr = Ring([region(14336 + 512 * i, 512) for i in range(2)], free6)
        qnr = Ring([region(15360 + 512 * i, 512) for i in range(3)], free6)
        t1r = Ring([region(16896 + 512 * i, 512) for i in range(2)], free6)
        t2r = Ring([region(17920 + 512 * i, 512) for i in range(2)], free6)

        def qk_tok(unit, nh, gname, dstT, scale, rope, by_block=False):
            dh = 512 // nh
            outs = []
            pend = []

            def first(t):
                b, bf = banks.take()
                m = gemm_tok([("in2", unit), ("in2", unit + 1)], HT, aT_t, t, b, bf)
                sq, sf = sqr.take()
                ss = stat(nh)
                a = act(lambda e: e.activation(sq, bank[b][:, :], ACT.Square), m, sf)
                c = dve(lambda e: e.tensor_reduce(ss, sq.rearrange("p (h d) -> p h d", h=nh), AX, ALU.add), a)
                sqr.give(sq, c)
                r, rt = rstd_of(ss, nh, dh, c)
                qn, qf = qnr.take()
                q3 = qn.rearrange("p (h d) -> p h d", h=nh)
                d = dve(lambda e: e.tensor_tensor(q3, bank[b][:, :].rearrange("p (h d) -> p h d", h=nh),
                                                  r.unsqueeze(2).to_broadcast([128, nh, dh]), ALU.mult), rt, qf)
                banks.give(b, d)
                g = row(gname).unsqueeze(1).to_broadcast([128, nh, dh])
                f = pool(lambda e: e.tensor_tensor(q3, q3, g, ALU.mult), d)
                if rope:
                    (t1, f1), (t2, f2) = t1r.take(), t2r.take()
                    co = con("cos")[:, t * 32:(t + 1) * 32].unsqueeze(1).to_broadcast([128, 16, 32])
                    si = con("sin")[:, t * 32:(t + 1) * 32].unsqueeze(1).to_broadcast([128, 16, 32])
                    v16 = lambda a: a.rearrange("p (h d) -> p h d", h=16)
                    v4 = lambda a, s: a.rearrange("p (h s d) -> p h s d", s=2, d=32)[:, :, s, :]
                    c1 = dve(lambda e: e.tensor_tensor(v16(t1), v16(qn), co, ALU.mult), f, f1)
                    c2 = dve(lambda e: e.tensor_tensor(v16(t2), v16(qn), si, ALU.mult), f, f2)
                    e1 = pool(lambda e: e.tensor_tensor(v4(qn, 0), v4(t1, 0), v4(t2, 1), ALU.subtract), c1, c2)
                    f = pool(lambda e: e.tensor_tensor(v4(qn, 1), v4(t1, 1), v4(t2, 0), ALU.add), e1)
                    t1r.give(t1, f)
                    t2r.give(t2, f)
                pend.append((t, qn, f))

            def second():
                t, qn, f = pend.pop(0)
                b, bf = banks.take()
                for k in range(4):
                    m = pe(lambda e, k=k: e.transpose(bank[b][:, k * 128:(k + 1) * 128], qn[:, k * 128:(k + 1) * 128],
                                                      ident), f, bf, sig=(k == 3))
                qnr.give(qn, m)
                dst = dstT[:, :, t * 128:(t + 1) * 128]
                src = bank[b][:, :].rearrange("p (k n) -> p k n", k=4)
                if by_block:
                    for f in range(4):
                        d4 = dstT[:, f, :].rearrange("p (j r c) -> p j r c", j=4, r=8)[:, :, 2 * t:2 * t + 2, :]
                        s4 = src[:, f, :].rearrange("p (r j c) -> p j r c", r=2, j=4)
                        for rr in range(2):
                            o = act(lambda e, d4=d4, s4=s4, rr=rr: e.activation(d4[:, :, rr, :], s4[:, :, rr, :], ACT.Copy,
                                                                                scale=scale), m)
                elif scale is None:
                    o = act(lambda e: e.activation(dst, src, ACT.Copy), m)
                else:
                    o = act(lambda e: e.activation(dst, src, ACT.Copy, scale=scale), m)
                banks.give(b, o)
                outs.append(o)

            for t in range(TT):
                first(t)
                if t >= 1:
                    second()
            Wdone(("in2", unit), (s_pe, pe.n))
            Wdone(("in2", unit + 1), (s_pe, pe.n))
            second()
            return outs

        qa_t = qk_tok(0, 8, "qa", qaT, 0.125, True)
        ka_t = qk_tok(2, 8, "ka", kaT, None, True)
        va_t = []
        for t in range(TT):
            b, bf = banks.take()
            m = gemm_tok([("in2", 4), ("in2", 5)], HT, aT_t, t, b, bf)
            va_t.append(evac(Va[:, t, :], bank[b][:, :], m))
            banks.give(b, va_t[-1])
        Wdone(("in2", 4), m)
        Wdone(("in2", 5), m)
        qb_t = qk_tok(6, 16, "qb", qbT, 32.0 ** -0.5, False, by_block=True)
        kb_t = qk_tok(8, 16, "kb", kbT, None, False)
        vbJ = region(15360, 4, 4, 256)
        KB = [0, 8, 24, 32]
        vb_t = [[] for _ in range(4)]
        free_v = everything()
        for i in range(2):
            for jj in range(2):
                f = 2 * i + jj
                b, bf = banks.take()
                m = gemm_T(("in2", 10 + i), KD, jj * 128, HT, aT_t, b, bf)
                b4 = bank[b][:, :].rearrange("p (r c) -> p r c", c=64)
                for j in range(4):
                    o = act(lambda e, f=f, j=j, b4=b4: e.activation(
                        vbJ[:, f, j, :].rearrange("p (r c) -> p r c", c=32), b4[:, :, KB[j]:KB[j] + 32], ACT.Copy),
                        m, free_v)
                    vb_t[j].append(o)
                banks.give(b, o)
            Wdone(("in2", 10 + i), m)
        vj_t = []
        for j in range(4):
            for half in range(2):
                b, bf = banks.take()
                for f in range(4):
                    m = pe(lambda e, f=f, j=j, half=half, b=b: e.transpose(
                        bank[b][:, f * 128:(f + 1) * 128], vbJ[:, f, j, half * 128:(half + 1) * 128], ident),
                        vb_t[j], bf, sig=(f == 3))
                vj_t.append(evac(Vj[:, 2 * j + half, :], bank[b][:, :], m))
                banks.give(b, vj_t[-1])
        free7 = everything()

        lam = stat(6)
        lt = [route[:, 0:64], route[:, 64:128]]
        lp = []
        for i, (a_, b_) in enumerate((("lq1", "lk1"), ("lq2", "lk2"))):
            lp.append(dve(lambda e, i=i, a_=a_, b_=b_: e.tensor_tensor_reduce(
                lt[i], row(a_), row(b_), 1.0, 0.0, ALU.mult, ALU.add, lam[:, i:i + 1]), misc["rows"]))
        le = act(lambda e: e.activation(lam[:, 2:4], lam[:, 0:2], ACT.Exp), lp)
        lm0 = dve(lambda e: e.tensor_tensor(lam[:, 4:5], lam[:, 2:3], lam[:, 3:4], ALU.subtract), le)
        LAM0 = 0.8 - 0.6 * float(np.exp(0.0))
        lm = dve(lambda e: e.tensor_scalar(lam[:, 5:6], lam[:, 4:5], LAM0, None, ALU.add), lm0)

        e1r = Ring([region(14336 + 512 * i, 512) for i in range(2)], free7)
        e2r = Ring([region(15360 + 512 * i, 512) for i in range(2)], free7)
        wTr = Ring([region(16384 + 512 * i, 512) for i in range(3)], free7)
        OR = region(17920, 4, 512)
        catT = HT
        items = [(h, qt) for h in range(4) for qt in range(4)]
        state = {}
        ob = {}
        or_t = {}

        def d0(i):
            h, qt = items[i]
            ms = []
            bs = []
            for s in range(2):
                b, bf = banks.take()
                bs.append(b)
                ms.append(pe(lambda e, s=s, b=b: e.matmul(
                    bank[b][:, :], qaT[64 * s:64 * s + 64, h, qt * 128:(qt + 1) * 128],
                    kaT[64 * s:64 * s + 64, h, :], start=True, stop=True), bf, qa_t, ka_t))
            nm, rs, rr = stat(2), stat(2), stat(3)
            E = [e1r.take(), e2r.take()]
            ex = []
            for s in range(2):
                a = dve(lambda e, s=s: e.tensor_reduce(nm[:, s:s + 1], bank[bs[s]][:, :], AX, ALU.max, negate=True), ms[s])
                x_ = act(lambda e, s=s: e.activation(E[s][0], bank[bs[s]][:, :], ACT.Exp, bias=nm[:, s:s + 1],
                                                     accum_out=rs[:, s:s + 1]), a, E[s][1])
                banks.give(bs[s], x_)
                ex.append(x_)
            r = dve(lambda e: e.reciprocal(rr[:, 0:2], rs), ex)
            l = dve(lambda e: e.tensor_tensor(rr[:, 2:3], rr[:, 1:2], lam[:, 5:6], ALU.mult), r, lm)
            t = dve(lambda e: e.tensor_scalar(E[1][0], E[1][0], rr[:, 2:3], None, ALU.mult), l)
            w = dve(lambda e: e.scalar_tensor_tensor(out=E[0][0], in0=E[0][0], scalar=rr[:, 0:1], in1=E[1][0],
                                                     op0=ALU.mult, op1=ALU.subtract), t)
            e2r.give(E[1][0], w)
            state[i] = (E[0][0], w)

        def d1(i):
            Wt, w = state[i]
            b, bf = banks.take()
            for k in range(4):
                m = pe(lambda e, k=k: e.transpose(bank[b][:, k * 128:(k + 1) * 128], Wt[:, k * 128:(k + 1) * 128], ident),
                       w, bf, sig=(k == 3))
            e1r.give(Wt, m)
            wT, wf = wTr.take()
            ev = act(lambda e: e.activation(wT, bank[b][:, :], ACT.Copy), m, wf)
            banks.give(b, ev)
            state[i] = (wT, ev)

        def d2(i):
            h, qt = items[i]
            wT, ev = state[i]
            if h not in ob:
                ob[h] = banks.take()
            b, bf = ob[h]
            for k in range(4):
                m = pe(lambda e, k=k: e.matmul(bank[b][:, qt * 128:(qt + 1) * 128], wT[:, k * 128:(k + 1) * 128],
                                               Va[:, k, h * 128:(h + 1) * 128], start=(k == 0), stop=(k == 3)),
                       ev, bf, va_t, sig=(k == 3))
            wTr.give(wT, m)
            if qt == 3:
                d = dve(lambda e: e.tensor_copy(OR[:, :, h * 128:(h + 1) * 128],
                                                bank[b][:, :].rearrange("p (q d) -> p q d", q=4)), m, free7)
                banks.give(b, d)
                or_t[h] = d

        n = len(items)
        for i in range(n + 2):
            if i < n:
                d0(i)
            if 1 <= i <= n:
                d1(i - 1)
            if i >= 2:
                d2(i - 2)

        free8 = everything()
        nbr = Ring([region(3072 * 0, 4, 3, 256)], free8)
        nb2 = region(14336, 4, 3, 256)
        nbr.give(nb2, free8)
        nb_sem = [sem("d_nb0"), sem("d_nb1")]
        nb_n = [0, 0]

        def nb_load(hg):
            buf, bf = nbr.take()
            i = hg % 2
            nb_n[i] += 1
            return buf, sp.dma(buf, nb_d[hg, :, :].rearrange("p (h j k) -> p h j k", h=4, j=3), nb_sem[i], nb_n[i], bf)

        nbs = [nb_load(0), nb_load(1)]
        OFF = 20480
        scr = Ring([region(OFF - 512 - 2560 + 1024 * 0, 4, 256)], free8)
        scr = Ring([region(8192, 4, 256), region(9216, 4, 256)], free8)
        Pr = Ring([region(3072, 4, 256), region(19968, 4, 256)], free8)
        PTr = Ring([region(20992, 8, 128)], free8)
        items = [(hg, j) for hg in range(4) for j in range(4)]
        state = {}
        ob = {}
        cat_t = []
        k4 = kbT.rearrange("p f (r c) -> p f r c", c=64)
        catR = catT[:, :, :].rearrange("p f (r c) -> p f r c", c=64)

        def n0(i):
            hg, j = items[i]
            nb, nt = nbs[hg]
            jt = (0, 1, 1, 2)[j]
            sc, sf = scr.take()
            P, pf = Pr.take()
            mx, nm, rs, rr = stat(4), stat(4), stat(4), stat(4)
            tt = []
            for hh in range(4):
                b, bf = banks.take()
                m = pe(lambda e, hh=hh, b=b: e.matmul(
                    bank[b][:, 0:256], qbT[32 * hh:32 * hh + 32, hg, 128 * j:128 * j + 128],
                    k4[32 * hh:32 * hh + 32, hg, :, KB[j]:KB[j] + 32], start=True, stop=True,
                    tile_position=(32 * hh, 0)), bf, qb_t, kb_t)
                a = dve(lambda e, hh=hh, b=b: e.tensor_tensor_reduce(
                    sc[:, hh, :], bank[b][:, 0:256], nb[:, hh, jt, :], 1.0, -3e38,
                    ALU.add, ALU.max, mx[:, hh:hh + 1]), m, sf, nt)
                tt.append(a)
                banks.give(b, a)
            c = dve(lambda e: e.tensor_scalar(nm, mx, -1.0, None, ALU.mult), tt)
            for g in range(4):
                ex = act(lambda e, g=g: e.activation(P[:, g, :], sc[:, g, :], ACT.Exp, bias=nm[:, g:g + 1],
                                                     accum_out=rs[:, g:g + 1]), c, pf)
            scr.give(sc, ex)
            r = dve(lambda e: e.reciprocal(rr, rs), ex)
            d = dve(lambda e: e.tensor_tensor(P, P, rr.unsqueeze(2).to_broadcast([128, 4, 256]), ALU.mult), r)
            state[i] = (P, d)
            if j == 3:
                nbr.give(nb, tt[-1])
                if hg + 2 < 4:
                    nbs.append(nb_load(hg + 2))

        def n1(i):
            P, d = state[i]
            PT, pf = PTr.take()
            evs = []
            for half in range(2):
                b, bf = banks.take()
                for g in range(4):
                    m = pe(lambda e, g=g, b=b, half=half: e.transpose(
                        bank[b][:, g * 128:(g + 1) * 128], P[:, g, half * 128:(half + 1) * 128], ident),
                        d, bf, sig=(g == 3))
                src = bank[b][:, :].rearrange("p (g q) -> p g q", g=4)
                ev = evac(PT[:, 4 * half:4 * half + 4, :], src, [m, pf])
                banks.give(b, ev)
                evs.append(ev)
            Pr.give(P, m)
            state[i] = (PT, evs)

        def n2(i):
            hg, j = items[i]
            PT, evs = state[i]
            if hg not in ob:
                ob[hg] = banks.take()
            b, bf = ob[hg]
            for g in range(4):
                for half in range(2):
                    m = pe(lambda e, g=g, half=half: e.matmul(
                        bank[b][32 * g:32 * g + 32, j * 128:(j + 1) * 128],
                        Vj[:, 2 * j + half, hg * 128 + 32 * g:hg * 128 + 32 * g + 32], PT[:, 4 * half + g, :],
                        start=(half == 0), stop=(half == 1), tile_position=(0, 32 * g)),
                        evs, bf, vj_t, sig=(g == 3 and half == 1))
            PTr.give(PT, m)
            if j == 3:
                for jj in range(4):
                    o = dve(lambda e, jj=jj: e.tensor_copy(
                        catR[:, 4 + hg, :, 16 * jj:16 * jj + 16],
                        bank[b][:, jj * 128:(jj + 1) * 128].rearrange("p (r c) -> p r c", c=16)), m)
                banks.give(b, o)
                cat_t.append(o)

        for i in range(len(items) + 2):
            if i < len(items):
                n0(i)
            if i >= 2:
                n2(i - 2)
            if 1 <= i <= len(items):
                n1(i - 1)

        sqr = Ring([region(8192 + 512 * i, 512) for i in range(2)], everything())
        for t in range(TT):
            ss = stat(4)
            sq, sf = sqr.take()
            o3 = OR[:, t, :].rearrange("p (h d) -> p h d", h=4)
            a = act(lambda e, t=t, sq=sq: e.activation(sq, OR[:, t, :], ACT.Square), list(or_t.values()), sf)
            c = dve(lambda e, ss=ss, sq=sq: e.tensor_reduce(ss, sq.rearrange("p (h d) -> p h d", h=4), AX, ALU.add), a)
            sqr.give(sq, c)
            r, rt = rstd_of(ss, 4, 128, c)
            d = dve(lambda e, o3=o3, r=r: e.tensor_tensor(o3, o3, r.unsqueeze(2).to_broadcast([128, 4, 128]), ALU.mult), rt)
            b, bf = banks.take()
            for k in range(4):
                m = pe(lambda e, k=k, b=b, t=t: e.transpose(bank[b][:, k * 128:(k + 1) * 128],
                                                            OR[:, t, k * 128:(k + 1) * 128], ident), d, bf, sig=(k == 3))
            f = dve(lambda e, t=t, b=b: e.tensor_scalar(
                catT[:, 0:4, t * 128:(t + 1) * 128], bank[b][:, :].rearrange("p (k n) -> p k n", k=4),
                col("g_sub"), 1.0 - LAM0, ALU.mult, ALU.mult), m)
            banks.give(b, f)
            cat_t.append(f)

        x_t = []
        for h in range(2):
            for t in range(TT):
                b, bf = banks.take()
                m = gemm_tok([("out2", 2 * h), ("out2", 2 * h + 1)], catT, cat_t, t, b, bf)
                dst = X[:, t, h * 512:(h + 1) * 512]
                f = dve(lambda e, dst=dst, b=b: e.tensor_tensor(dst, bank[b][:, :], dst, ALU.add), m)
                banks.give(b, f)
                x_t.append(f)
            Wdone(("out2", 2 * h), m)
            Wdone(("out2", 2 * h + 1), m)
        x2_t = [[x_t[t], x_t[4 + t]] for t in range(TT)]

        free9 = everything()
        XS = region(0, 4, 1024)
        XNT = region(4096, 8, 512)
        xnT_t, xs_t = norm_to_T("ffn2", x2_t, None, XNT, free9, keep=XS)

        L = route[:, 0:144].rearrange("p (t n) -> p t n", t=4)
        RK = route[:, 144:272].rearrange("p (t e) -> p t e", t=4)
        W32 = route[:, 272:400].rearrange("p (t e) -> p t e", t=4)
        SEL = route[:, 400:528].rearrange("p (t e) -> p t e", t=4)
        ro = [528]

        def rt4(*shape):
            n = int(np.prod(shape))
            a = route[:, ro[0]:ro[0] + n]
            ro[0] += n
            if len(shape) == 2:
                a = a.rearrange("p (a b) -> p a b", a=shape[0])
            if len(shape) == 3:
                a = a.rearrange("p (a b c) -> p a b c", a=shape[0], b=shape[1])
            return a

        b, bf = banks.take()
        for t in range(TT):
            for k in range(KD):
                m = pe(lambda e, t=t, k=k, b=b: e.matmul(bank[b][:, t * 36:(t + 1) * 36],
                                                         XNT[:, k, t * 128:(t + 1) * 128], wr[:, k, :],
                                                         start=(k == 0), stop=(k == KD - 1)),
                       xnT_t, bf, misc["wr"], sig=(k == KD - 1))
        lt_ = dve(lambda e, b=b: e.tensor_copy(route[:, 0:144], bank[b][:, 0:144]), m)
        banks.give(b, lt_)
        GL = L[:, :, 0:4]
        iota = con("iota")

        def first_max(src, n, after):
            mx, t, mn, oh = rt4(4), rt4(4, n), rt4(4), rt4(4, n)
            bc = lambda a: a.unsqueeze(2).to_broadcast([128, 4, n])
            a = dve(lambda e: e.tensor_reduce(mx, src, AX, ALU.max), after)
            c = dve(lambda e: e.tensor_tensor(t, src, bc(mx), ALU.is_equal), a)
            io = iota[:, 0:n].unsqueeze(1).to_broadcast([128, 4, n])
            d = dve(lambda e: e.scalar_tensor_tensor(out=t, in0=t, scalar=-100.0, in1=io, op0=ALU.mult, op1=ALU.add), c)
            f = dve(lambda e: e.tensor_reduce(mn, t, AX, ALU.min), d)
            return mx, oh, dve(lambda e: e.tensor_tensor(oh, t, bc(mn), ALU.is_equal), f)

        gm, goh, gt = first_max(GL, 4, lt_)
        ge_, gs, gg = rt4(4, 4), rt4(4), rt4(4)
        a = dve(lambda e: e.tensor_tensor(ge_, GL, gm.unsqueeze(2).to_broadcast([128, 4, 4]), ALU.subtract), gt)
        a = act(lambda e: e.activation(ge_, ge_, ACT.Exp), a)
        a = dve(lambda e: e.tensor_reduce(gs, ge_, AX, ALU.add), a)
        gg_t = dve(lambda e: e.reciprocal(gg, gs), a)
        prod, el = rt4(4, 32), rt4(4, 8)
        for t in range(TT):
            a = dve(lambda e, t=t: e.tensor_tensor(
                prod[:, t, :].rearrange("p (g e) -> p g e", g=4), L[:, t, 4:36].rearrange("p (g e) -> p g e", g=4),
                goh[:, t, :].unsqueeze(2).to_broadcast([128, 4, 8]), ALU.mult), gt)
        for t in range(TT):
            c = dve(lambda e, t=t: e.tensor_reduce(el[:, t, :], prod[:, t, :].rearrange("p (g e) -> p e g", g=4), AX,
                                                   ALU.add), a)
        m1, oh1, o1 = first_max(el, 8, c)
        el2 = rt4(4, 8)
        a = dve(lambda e: e.scalar_tensor_tensor(out=el2, in0=oh1, scalar=-3e38, in1=el, op0=ALU.mult, op1=ALU.add), o1)
        m2, oh2, o2 = first_max(el2, 8, a)
        df, e2_, wa, wb = rt4(4), rt4(4), rt4(4), rt4(4)
        a = dve(lambda e: e.tensor_tensor(df, m2, m1, ALU.subtract), o2)
        x_ = act(lambda e: e.activation(e2_, df, ACT.Exp), a)
        a = dve(lambda e: e.tensor_scalar(wa, e2_, 1.0, None, ALU.add), x_)
        a = dve(lambda e: e.reciprocal(wa, wa), a)
        a = dve(lambda e: e.tensor_tensor(wa, wa, gg, ALU.mult), a, gg_t)
        a = dve(lambda e: e.tensor_tensor(wb, wa, e2_, ALU.mult), a)
        w8, s8, w8b = rt4(4, 8), rt4(4, 8), rt4(4, 8)
        bc8 = lambda v: v.unsqueeze(2).to_broadcast([128, 4, 8])
        a = dve(lambda e: e.tensor_tensor(w8, oh1, bc8(wa), ALU.mult), a)
        c = dve(lambda e: e.tensor_tensor(w8b, oh2, bc8(wb), ALU.mult), a)
        a = dve(lambda e: e.tensor_tensor(w8, w8, w8b, ALU.add), c)
        c = dve(lambda e: e.tensor_tensor(s8, oh1, oh2, ALU.add), a)
        for t in range(TT):
            gb_ = goh[:, t, :].unsqueeze(2).to_broadcast([128, 4, 8])
            dve(lambda e, t=t, gb_=gb_: e.tensor_tensor(
                W32[:, t, :].rearrange("p (g e) -> p g e", g=4), w8[:, t, :].unsqueeze(1).to_broadcast([128, 4, 8]),
                gb_, ALU.mult), c)
            sel_t = dve(lambda e, t=t, gb_=gb_: e.tensor_tensor(
                SEL[:, t, :].rearrange("p (g e) -> p g e", g=4), s8[:, t, :].unsqueeze(1).to_broadcast([128, 4, 8]),
                gb_, ALU.mult), c)
        b, bf = banks.take()
        for t in range(TT):
            for j in range(t + 1):
                m = pe(lambda e, t=t, j=j, b=b: e.matmul(bank[b][:, t * 32:(t + 1) * 32],
                                                         con("tri") if j == t else con("ones"), SEL[:, j, :],
                                                         start=(j == 0), stop=(j == t)), sel_t, bf, sig=(j == t))
        for j in range(TT):
            m = pe(lambda e, j=j, b=b: e.matmul(bank[b][:, 128:160], con("ones"), SEL[:, j, :], start=(j == 0),
                                                stop=(j == 3)), sig=(j == 3))
        flat = lambda v: v.rearrange("p t e -> p (t e)")
        a = dve(lambda e, b=b: e.scalar_tensor_tensor(out=flat(RK), in0=bank[b][:, 0:128], scalar=1.0, in1=flat(SEL),
                                                      op0=ALU.add, op1=ALU.mult), m)
        mc, cm, nx = rt4(1), rt4(7), rt4(1)
        c = dve(lambda e, b=b: e.tensor_reduce(mc, bank[b][:, 128:160], AX, ALU.max), a)
        banks.give(b, c)
        rk_t = dve(lambda e: e.tensor_scalar(flat(RK), flat(RK), -1.0, None, ALU.add), c)
        c = dve(lambda e: e.tensor_scalar(cm, con("thr")[:, 0:7], mc, None, ALU.is_lt), c)
        c = dve(lambda e: e.tensor_reduce(nx, cm, AX, ALU.add), c)
        nx_t = dve(lambda e: e.tensor_copy(nex_i[:, :], nx[0:1, :]), c)

        XET = [HT[:, 0:4, :].rearrange("p a b -> p (a b)").rearrange("p (k s) -> p k s", k=8),
               HT[:, 4:8, :].rearrange("p a b -> p (a b)").rearrange("p (k s) -> p k s", k=8)]
        free10 = everything()
        S_r = Ring([region(4096, 4, 4 * C), region(5120, 4, 4 * C)], free10)
        Sw_r = Ring([region(6144, 4, 4 * C)], free10)
        SwT_r = Ring([region(7168 + 512 * i, 512) for i in range(8)], free10)
        Y_r = Ring([region(11264 + 1024 * i, 1024) for i in range(4)], free10)
        sg_r = Ring([region(15360 + 512 * i, 512) for i in range(2)], free10)
        hd_r = Ring([region(16384 + 512 * i, 512) for i in range(2)], free10)
        hT_r = Ring([region(17408 + 512 * i, 512) for i in range(2)], free10)
        xet_free = [free10, free10]
        for i in range(NS, NS_MOE):
            slots.append(region(18432 + (i - NS) * UNIT, UNIT))
            free_slots.append((i, free10))
        limit[0] = len(units)
        issue()
        gath, swT = {}, {}

        def gather(g):
            S, sf = S_r.take()
            Sw, wf = Sw_r.take()
            for t in range(TT):
                ib = iota.unsqueeze(1).to_broadcast([128, 4, C])
                rb = RK[:, t, 4 * g:4 * g + 4].unsqueeze(2).to_broadcast([128, 4, C])
                a = dve(lambda e, t=t, ib=ib, rb=rb: e.tensor_tensor(
                    S[:, t, :].rearrange("p (e s) -> p e s", e=4), ib, rb, ALU.is_equal), rk_t, sf)
            for t in range(TT):
                wb_ = W32[:, t, 4 * g:4 * g + 4].unsqueeze(2).to_broadcast([128, 4, C])
                w_ = pool(lambda e, t=t, wb_=wb_: e.tensor_tensor(
                    Sw[:, t, :].rearrange("p (e s) -> p e s", e=4), S[:, t, :].rearrange("p (e s) -> p e s", e=4),
                    wb_, ALU.mult), a, wf)
            Xe = XET[g % 2]
            out = []
            for kp in range(4):
                b, bf = banks.take()
                for kk in range(2):
                    k = 2 * kp + kk
                    for t in range(TT):
                        m = pe(lambda e, k=k, kk=kk, t=t, b=b: e.matmul(
                            bank[b][:, kk * 256:(kk + 1) * 256], XS[:, t, k * 128:(k + 1) * 128], S[:, t, :],
                            start=(t == 0), stop=(t == 3)), a, bf, xs_t, sig=(t == 3))
                for kk in range(2):
                    k = 2 * kp + kk
                    d = act(lambda e, k=k, kk=kk, b=b: e.activation(Xe[:, k, :], bank[b][:, kk * 256:(kk + 1) * 256],
                                                                    ACT.Copy, scale=col("ffn2", k)), m, xet_free[g % 2])
                banks.give(b, d)
                out.append(d)
            for q in range(2):
                b, bf = banks.take()
                for t in range(TT):
                    m2_ = pe(lambda e, t=t, q=q, b=b: e.transpose(bank[b][:, t * 128:(t + 1) * 128],
                                                                  Sw[:, t, q * 128:(q + 1) * 128], ident),
                             w_, bf, sig=(t == 3))
                T_, tf = SwT_r.take()
                d = act(lambda e, T_=T_, b=b: e.activation(T_, bank[b][:, :], ACT.Copy), m2_, tf)
                banks.give(b, d)
                swT[2 * g + q] = (T_, d)
            S_r.give(S, [m, w_])
            Sw_r.give(Sw, m2_)
            gath[g] = out

        hid = {}

        def hidden(p):
            Xe, xt_ = XET[(p // 2) % 2], gath[p // 2]
            o = (p % 2) * 2 * C
            ms = []
            for w in (1, 3):
                b, bf = banks.take()
                for kh in range(2):
                    us = [W(("e", w, 2 * p + s, kh), 4) for s in range(2)]
                    for k in range(4):
                        for s in range(2):
                            m = pe(lambda e, s=s, k=k, kh=kh, b=b, us=us: e.matmul(
                                bank[b][64 * s:64 * s + 64, :], Xe[:, 4 * kh + k, o + C * s:o + C * s + C],
                                us[s][0][:, k, :], start=(kh == 0 and k == 0), stop=(kh == 1 and k == 3)),
                                us[s][1], bf, xt_, sig=(k == 3 and s == 1))
                    for s in range(2):
                        Wdone(("e", w, 2 * p + s, kh), m)
                ms.append((b, m))
            if p % 2:
                xet_free[(p // 2) % 2] = m
            sg, sf = sg_r.take()
            hd, hf = hd_r.take()
            a = act(lambda e: e.activation(sg, bank[ms[0][0]][:, :], ACT.Silu), ms[0][1], sf)
            banks.give(ms[0][0], a)
            d = dve(lambda e: e.tensor_tensor(hd, sg, bank[ms[1][0]][:, :], ALU.mult), a, ms[1][1], hf)
            banks.give(ms[1][0], d)
            sg_r.give(sg, d)
            hid[p] = (hd, d)

        def turn(p):
            hd, d = hid[p]
            b, bf = banks.take()
            for k in range(4):
                m = pe(lambda e, k=k: e.transpose(bank[b][:, k * 128:(k + 1) * 128], hd[:, k * 128:(k + 1) * 128], ident),
                       d, bf, sig=(k == 3))
            hd_r.give(hd, m)
            hT, hf = hT_r.take()
            ev = dve(lambda e: e.tensor_copy(hT, bank[b][:, :]), m, hf)
            banks.give(b, ev)
            hid[p] = (hT, ev)

        ys = {}

        def second(p):
            hT, ev = hid[p]
            bs = [banks.take() for _ in range(2)]
            for kh in range(2):
                us = [W(("e", 2, 2 * p + s, kh), 2) for s in range(2)]
                for k in range(2):
                    for h in range(2):
                        for s in range(2):
                            kk = 2 * kh + k
                            m = pe(lambda e, s=s, k=k, kk=kk, h=h, us=us: e.matmul(
                                bank[bs[h][0]][64 * s:64 * s + 64, :], hT[:, kk * 128 + 64 * s:kk * 128 + 64 * s + 64],
                                us[s][0][:, k, h * 512:(h + 1) * 512], start=(kk == 0), stop=(kk == 3)),
                                us[s][1], bs[h][1], ev, sig=(s == 1 and h == 1 and k == 1))
                for s in range(2):
                    Wdone(("e", 2, 2 * p + s, kh), m)
            hT_r.give(hT, m)
            Y, yf = Y_r.take()
            ev = [act(lambda e: e.activation(Y[:, 0:512], bank[bs[0][0]][:, :], ACT.Copy), m, yf),
                  dve(lambda e: e.tensor_copy(Y[:, 512:1024], bank[bs[1][0]][:, :]), m, yf)]
            for h in range(2):
                banks.give(bs[h][0], ev[h])
            ys[p] = (Y, ev)

        acc_t = {(t, h): [xs_t[t]] for t in range(TT) for h in range(2)}

        def scatter(ps):
            for t in range(TT):
                for h in range(2):
                    b, bf = banks.take()
                    for i, p in enumerate(ps):
                        m = pe(lambda e, i=i, p=p, t=t, h=h, b=b: e.matmul(
                            bank[b][:, :], swT[p][0][:, t * 128:(t + 1) * 128], ys[p][0][:, h * 512:(h + 1) * 512],
                            start=(i == 0), stop=(i == len(ps) - 1)), swT[p][1], ys[p][1], bf, sig=(i == len(ps) - 1))
                    dst = X[:, t, h * 512:(h + 1) * 512]
                    f = dve(lambda e, dst=dst, b=b: e.tensor_tensor(dst, bank[b][:, :], dst, ALU.add), m, acc_t[t, h])
                    banks.give(b, f)
                    acc_t[t, h] = f
            for p in ps:
                SwT_r.give(swT[p][0], m)
                Y_r.give(ys[p][0], m)

        gather(0)
        for p in range(NPAIR + 1):
            if p < NPAIR:
                hidden(p)
                if p % 2 == 0 and p // 2 + 1 < NE // 4:
                    gather(p // 2 + 1)
            if p >= 1:
                second(p - 1)
                if p % 4 == 0:
                    scatter(list(range(p - 4, p)))
            if p < NPAIR:
                turn(p)

        with nc.Block() as block:
            @block.sync
            def _(e):
                sp.run(e)

            @block.gpsimd
            def _(e):
                pool.run(e)

            @block.scalar
            def _(e):
                act.run(e)

            @block.vector
            def _(e):
                dve.run(e)

            @block.tensor
            def _(e):
                pe.run(e)
        for q in (pe, act, dve, pool, sp):
            q.items.clear()

        overflow(nc, ctx, sem, dict(nex_i=nex_i, w1=w1_d, w3=w3_d, w2=w2_d, arena=arena, HT=HT, X=X, XS=XS, RK=RK,
                                    W32=W32, con=con, col=col, bank=bank, ident=ident))

        everything_done = everything()
        for q in engines:
            for s_, v_ in everything_done:
                q.waited[s_.name] = v_
        banks = Ring(list(range(8)))
        hT2 = region(4096, 8, 512)
        xs_ring = Ring([region(8192 + 1024 * i, 1024) for i in range(2)])
        pT = region(10240, 2, 512)
        PN = region(11264, 4, 1024)
        tmp_ring = Ring([region(15360 + 1024 * i, 1024) for i in range(3)])
        load(pool, "pT", pT, pT_d)
        w, wt = W(("ple", 0), 2)
        pn_t = []
        for t in range(TT):
            hs = []
            for h in range(2):
                b, bf = banks.take()
                for k in range(2):
                    m = pe(lambda e, k=k, t=t, h=h, b=b: e.matmul(
                        bank[b][:, :], pT[:, k, t * 128:(t + 1) * 128], w[:, k, h * 512:(h + 1) * 512],
                        start=(k == 0), stop=(k == 1)), wt, misc["pT"], bf, sig=(k == 1))
                hs.append((bank[b][:, :], m, b))
            ss, s1 = stat(2), stat()
            q = sumsq(lambda i, hs=hs: hs[i][0], ss, hs[0][1], hs[1][1])
            a = dve(lambda e, s1=s1, ss=ss: e.tensor_tensor(s1, ss[:, 0:1], ss[:, 1:2], ALU.add), q)
            r, rt = rstd_of(s1, 1, D, a)
            o = ROWS["ple"][0]
            for h in range(2):
                z = dve(lambda e, h=h, t=t, hs=hs, r=r: e.scalar_tensor_tensor(
                    out=PN[:, t, h * 512:(h + 1) * 512], in0=hs[h][0], scalar=r,
                    in1=rows[:, o + h * 512:o + (h + 1) * 512], op0=ALU.mult, op1=ALU.mult), rt)
                banks.give(hs[h][2], z)
            pn_t.append(z)
        hT_t = norm_to_T("plg", [None] * TT, xs_ring, hT2, None)
        d_out = sem("d_out")
        fin = {}
        nout = 0
        for h in range(2):
            for t in range(TT):
                b, bf = banks.take()
                m = gemm_tok([("plg", 2 * h), ("plg", 2 * h + 1)], hT2, hT_t, t, b, bf)
                tmp, tf = tmp_ring.take()
                s = act(lambda e, b=b, tmp=tmp: e.activation(tmp[:, 0:512], bank[b][:, :], ACT.Sigmoid), m, tf)
                banks.give(b, s)
                z = pool(lambda e, h=h, t=t, tmp=tmp: e.tensor_tensor(
                    tmp[:, 0:512], tmp[:, 0:512], PN[:, t, h * 512:(h + 1) * 512], ALU.mult), s, pn_t[t])
                f = dve(lambda e, h=h, t=t, tmp=tmp: e.tensor_tensor(
                    tmp[:, 512:1024], tmp[:, 0:512], X[:, t, h * 512:(h + 1) * 512], ALU.add), z)
                nout += 1
                od = sp.dma(out_d[t * 128:(t + 1) * 128, h * 512:(h + 1) * 512], tmp[:, 512:1024],
                            sem(f"d_out{nout}"), 1, f)
                tmp_ring.give(tmp, od)
                fin[t, h] = od
        sp.wait(list(fin.values()))

        with nc.Block() as block:
            @block.sync
            def _(e):
                sp.run(e)

            @block.gpsimd
            def _(e):
                pool.run(e)

            @block.scalar
            def _(e):
                act.run(e)

            @block.vector
            def _(e):
                dve.run(e)

            @block.tensor
            def _(e):
                pe.run(e)


def overflow(nc, ctx, sem, v):
    con, bank, ident, X, XS, HT = v["con"], v["bank"], v["ident"], v["X"], v["XS"], v["HT"]
    arena = v["arena"]
    iota = con("iota")

    def reg(o, *shape):
        n = int(np.prod(shape))
        a = arena[:, o:o + n]
        return a if len(shape) == 1 else a.rearrange("p (a b) -> p a b", a=shape[0])

    wA, wB, wC = (reg(4096 + 4096 * i, 4096) for i in range(3))
    oh = reg(16384, 32)
    pr = reg(16416, 4, 32)
    rc, wc = reg(16544, 4), reg(16548, 4)
    cnt = reg(16552, 1)
    rnd = reg(16553, 1)
    S, Sw = reg(16640, 4, C), reg(16896, 4, C)
    SwT, sg, hd = reg(17152, 512), reg(17664, 512), reg(18176, 512)
    hT = reg(18688, 4, C)
    Y = reg(18944, 1024)
    Xe = HT[:, 0, :].rearrange("p (k s) -> p k s", k=8)
    s_d, s_p, s_a, s_v, s_i = sem("o_d"), sem("o_p"), sem("o_a"), sem("o_v"), sem("o_i")

    with nc.Block() as block:
        @block.vector
        def _(e):
            e.memset(rnd, float(C)).then_inc(s_i, 1)
            e.wait_ge(s_i, 1)

    n = nc.values_load(v["nex_i"][0:1, 0:1], min_val=0, max_val=NTOK // C - 1)
    with nc.If(n > 0):
        with nc.Fori(0, n):
            with nc.Block() as block:
                @block.vector
                def _(e):
                    e.memset(cnt, 0.0).then_inc(s_v, 1)
                    e.wait_ge(s_v, 1)
            nc.all_engine_barrier()
            nc.gpsimd.sem_clear(s_v)
            nc.all_engine_barrier()
            with nc.Fori(0, NE) as ei:
                pe, act, dve, sp = Queue(s_p), Queue(s_a), Queue(s_v), Queue(s_d)
                for i, (w, src, k) in enumerate(((wA, v["w1"], 8), (wB, v["w3"], 8), (wC, v["w2"], 4))):
                    s = src[bass.ds(ei, 1), :, :].rearrange("a (k p) n -> p (a k) n", p=128)
                    d_t = sp.dma(w.rearrange("p (k n) -> p k n", k=k), s, s_d, i + 1)
                a = dve(lambda e: e.tensor_scalar(oh, iota[:, 0:32], cnt, None, ALU.is_equal))
                a = dve(lambda e: e.tensor_scalar(cnt, cnt, 1.0, None, ALU.add), a)
                ohb = oh.unsqueeze(1).to_broadcast([128, 4, 32])
                for src, dst in ((v["RK"], rc), (v["W32"], wc)):
                    a = dve(lambda e, src=src: e.tensor_tensor(pr, src, ohb, ALU.mult), a)
                    a = dve(lambda e, dst=dst: e.tensor_reduce(dst, pr, AX, ALU.add), a)
                a = dve(lambda e: e.tensor_scalar(rc, rc, rnd, None, ALU.subtract), a)
                ib = iota.unsqueeze(1).to_broadcast([128, 4, C])
                a = dve(lambda e: e.tensor_tensor(S, ib, rc.unsqueeze(2).to_broadcast([128, 4, C]), ALU.is_equal), a)
                sw = dve(lambda e: e.tensor_tensor(Sw, S, wc.unsqueeze(2).to_broadcast([128, 4, C]), ALU.mult), a)
                for k in range(KD):
                    for t in range(TT):
                        m = pe(lambda e, k=k, t=t: e.matmul(bank[0][:, k * C:(k + 1) * C],
                                                            XS[:, t, k * 128:(k + 1) * 128], S[:, t, :],
                                                            start=(t == 0), stop=(t == 3)), a, sig=(t == 3))
                for t in range(TT):
                    m2 = pe(lambda e, t=t: e.transpose(bank[1][0:C, t * 128:(t + 1) * 128], Sw[:, t, :], ident),
                            sw, sig=(t == 3))
                for k in range(KD):
                    x = act(lambda e, k=k: e.activation(Xe[:, k, :], bank[0][:, k * C:(k + 1) * C], ACT.Copy,
                                                        scale=v["col"]("ffn2", k)), m)
                x2 = act(lambda e: e.activation(SwT[0:C, :], bank[1][0:C, :], ACT.Copy), m2)
                for w, b in ((wA, 2), (wB, 3)):
                    for k in range(KD):
                        m = pe(lambda e, w=w, b=b, k=k: e.matmul(bank[b][0:C, :], Xe[:, k, :],
                                                                 w[:, k * 512:(k + 1) * 512], start=(k == 0),
                                                                 stop=(k == 7)), x, d_t, sig=(k == 7))
                g = act(lambda e: e.activation(sg[0:C, :], bank[2][0:C, :], ACT.Silu), m)
                h = dve(lambda e: e.tensor_tensor(hd[0:C, :], sg[0:C, :], bank[3][0:C, :], ALU.mult), g)
                for k in range(4):
                    m = pe(lambda e, k=k: e.transpose(bank[4][:, k * C:(k + 1) * C], hd[0:C, k * 128:(k + 1) * 128],
                                                      ident[0:C, 0:C]), h, sig=(k == 3))
                c = dve(lambda e: e.tensor_copy(hT.rearrange("p a b -> p (a b)"), bank[4][:, 0:4 * C]), m)
                for hh in range(2):
                    for k in range(4):
                        m = pe(lambda e, hh=hh, k=k: e.matmul(
                            bank[5 + hh][0:C, :], hT[:, k, :], wC[:, k * 1024 + hh * 512:k * 1024 + hh * 512 + 512],
                            start=(k == 0), stop=(k == 3)), c, sig=(k == 3))
                    y = dve(lambda e, hh=hh: e.tensor_copy(Y[0:C, hh * 512:(hh + 1) * 512], bank[5 + hh][0:C, :]), m)
                f = None
                for t in range(TT):
                    for hh in range(2):
                        m = pe(lambda e, t=t, hh=hh: e.matmul(bank[7][:, :], SwT[0:C, t * 128:(t + 1) * 128],
                                                              Y[0:C, hh * 512:(hh + 1) * 512], start=True, stop=True),
                               y, x2, f)
                        dst = X[:, t, hh * 512:(hh + 1) * 512]
                        f = dve(lambda e, dst=dst: e.tensor_tensor(dst, bank[7][:, :], dst, ALU.add), m)
                dve.wait(f)
                with nc.Block() as block:
                    @block.sync
                    def _(e):
                        sp.run(e)

                    @block.scalar
                    def _(e):
                        act.run(e)

                    @block.vector
                    def _(e):
                        dve.run(e)

                    @block.tensor
                    def _(e):
                        pe.run(e)
                nc.all_engine_barrier()
                for s in (s_d, s_p, s_a, s_v):
                    nc.gpsimd.sem_clear(s)
                nc.all_engine_barrier()
            with nc.Block() as block:
                @block.vector
                def _(e):
                    e.tensor_scalar(rnd, rnd, float(C), None, ALU.add).then_inc(s_v, 1)
                    e.wait_ge(s_v, 1)
            nc.all_engine_barrier()
            nc.gpsimd.sem_clear(s_v)
            nc.all_engine_barrier()


def _by_cols(w, width=256):
    k, n = w.shape
    return w.reshape(k // 128, 128, n // width, width).transpose(2, 1, 0, 3).reshape(n // width, 128, -1)


def _by_rows(w):
    return w.reshape(-1, 2, 128, 1024).transpose(0, 2, 1, 3).reshape(-1, 128, 2048)


def _tiles(v):
    return v.reshape(-1, 128).T


def _layout(i):
    w_in, w_up = _by_cols(i["w_in"][0]), _by_cols(i["w_up"][0])
    ao, po = _by_cols(i["w_attn_out"][0], 512), _by_cols(i["w_pool_out"][0], 512)
    dn = _by_rows(i["w_down"][0])
    seq = [w_in[n] for n in range(8)]
    for n in range(2):
        seq += [ao[n], po[n]]
    for n in range(4):
        seq += [w_in[8 + n], w_in[12 + n]]
    seq += list(_by_cols(i["w_o"][0]))
    u = d = 0
    for n in CHUNKS:
        for _ in range(n // 2):
            seq += [w_up[u], w_up[11 + u]]
            u += 1
        for _ in range(n // 2):
            seq.append(dn[d])
            d += 1
    seq += list(_by_cols(i["w_in_2"][0])) + list(_by_cols(i["w_out_2"][0]))
    seq += list(_by_rows(i["w_ple_2"][0])) + list(_by_cols(i["w_plg_2"][0]))

    cols = np.concatenate([_tiles(i[n].reshape(-1)) for n in (
        "norm_mix_pre", "norm_ffn_pre", "g_mix_2", "g_ffn_2", "g_plg_2", "b_gate", "pool_scale", "conv_w", "conv_b",
        "g_sub_2")], axis=1)
    rows = np.concatenate([i[n].reshape(-1) for n in (
        "norm_mix_post", "norm_ffn_post", "g_ple_2", "g_qa_2", "g_ka_2", "g_qb_2", "g_kb_2", "lam_q1_2", "lam_k1_2",
        "lam_q2_2", "lam_k2_2")])[None, :]

    p = np.arange(128)
    dist = p[:, None] + 384 - np.arange(512)[None, :]
    tb = i["rel_bias"][0][:, np.clip(dist, -256, 256) + 256]
    tb = np.where((p[:, None] < 64) & (np.arange(512)[None, :] >= 448), np.float32(NEG), tb).transpose(1, 0, 2)

    r, c = p // 16, p % 16
    kr, kc = np.arange(256) // 32, np.arange(256) % 32
    nb = np.empty((4, 128, 4, 3, 256), np.float32)
    for jt, (q0, k0) in enumerate(((0, 0), (16, 8), (48, 32))):
        qc, kcol = q0 + c, k0 + kc
        cs = np.clip(qc - 8, 0, 48)
        ok = (kcol[None, :] >= cs[:, None]) & (kcol[None, :] < cs[:, None] + 16)
        off = np.clip(kcol[None, :] - qc[:, None] + 15, 0, 30)
        ro = kr[None, :] - r[:, None] + 7
        t = np.where(ok, i["rpb_2"][0][:, ro, off], np.float32(NEG))
        nb[:, :, :, jt, :] = t.reshape(4, 4, 128, 256).transpose(0, 2, 1, 3)

    t = np.arange(NTOK, dtype=np.float32)
    inv = (np.float32(10000.0) ** (-np.arange(0, 64, 2, dtype=np.float32) / np.float32(64))).astype(np.float32)
    ang = (t[:, None] * inv[None, :]).astype(np.float32)
    by_tok = lambda a: a.reshape(4, 128, 32).transpose(1, 0, 2).reshape(128, 128)
    cnt = np.stack([1.0 / np.minimum(np.arange(16) + 1, 2 << g) for g in range(4)]).reshape(1, 64)
    one = np.ones((128, 1))
    cst = np.concatenate([np.eye(128), np.triu(np.ones((128, 128)), 1), np.ones((128, 128)),
                          one * np.arange(64)[None, :], one * (C * (1 + np.arange(8)))[None, :], one * cnt,
                          by_tok(np.cos(ang)), by_tok(np.sin(ang))], axis=1).astype(np.float32)
    wr = np.concatenate([i["w_rg_2"][0], i["w_re_2"][0]], axis=1).reshape(8, 128, 36).transpose(1, 0, 2)
    return {
        "x": i["x"][0], "wd": np.stack(seq), "w1": i["w1_2"][0], "w3": i["w3_2"][0], "w2": i["w2_2"][0],
        "cols": cols, "rows": rows, "cst": cst, "wr": wr, "wpg": i["w_pool_group"][0].transpose(1, 0, 2),
        "pT": i["p_2"][0, 0].T.reshape(2, 128, 512).transpose(1, 0, 2), "tb": tb, "nb": nb.reshape(4, 128, 3072),
    }


def kernel(**inputs):
    import concourse.bacc as bacc
    from concourse.bass_utils import run_bass_kernel_spmd

    nc = bacc.Bacc("TRN2", target_bir_lowering=False, num_devices=1)
    arrays, args = {}, []
    for name, a in _layout({k: np.asarray(v) for k, v in inputs.items()}).items():
        a = np.ascontiguousarray(a)
        arrays[f"in_{name}"] = a
        args.append(nc.dram_tensor(f"in_{name}", a.shape, mybir.dt.from_np(a.dtype), kind="ExternalInput").ap())
    out = nc.dram_tensor("out_0", (NTOK, D), F32, kind="ExternalOutput").ap()
    build(nc, *args, out)
    r = run_bass_kernel_spmd(nc, [arrays], core_ids=[0])
    return r.results[0]["out_0"].reshape(1, NTOK, D)
```

```python
from collections import deque
from contextlib import ExitStack

import numpy as np

import concourse.bass as bass
from concourse import mybir

F32 = mybir.dt.float32
F32R = mybir.dt.float32r
I32 = mybir.dt.int32
ACT = mybir.ActivationFunctionType
ALU = mybir.AluOpType
AX = mybir.AxisListType.X

NTOK, D = 512, 1024
TT, KD = 4, 8
FF = 2816
UNIT = 2048
NS = 4
NSPLIT = 3
M_SZ = 42560
SPLIT0 = NS * UNIT
HT0 = SPLIT0 + NSPLIT * 2 * UNIT
R0 = HT0 + 8192
A0 = 14336
NATILE = 6
NS_MOE = 7
NE = 32
NPAIR = NE // 2
C = 64
EPS = 1e-6
NEG = -1e30

COLS = {}
_o = 0
for _n, _w in (("mix_pre", 8), ("ffn_pre", 8), ("mix2", 8), ("ffn2", 8), ("plg", 8), ("b_gate", 16),
               ("pool_scale", 4), ("conv_w", 132), ("conv_b", 44), ("g_sub", 1)):
    COLS[_n] = (_o, _w)
    _o += _w
NCOLS = _o
ROWS = {}
_o = 0
for _n, _w in (("qa", 64), ("ka", 64), ("qb", 32),
               ("kb", 32), ("lq1", 64), ("lk1", 64), ("lq2", 64), ("lk2", 64)):
    ROWS[_n] = (_o, _w)
    _o += _w
NROWS = _o
BIG = {"mix_post": 0, "ffn_post": 1024, "ple": 2048}
CST = {}
_o = 0
for _n, _w in (("ident", 128), ("tri", 128), ("ones", 128), ("iota", 64), ("thr", 8), ("cnt", 64),
               ("cos", 128), ("sin", 128)):
    CST[_n] = (_o, _w)
    _o += _w
NCST = _o


def ffn_order():
    steps = [([0, 1, 2], [0, 1])]
    for n in range(1, 5):
        steps.append(([2 * n + 1, 2 * n + 2], [2 * n, 2 * n + 1]))
    return steps + [([], [10])]


class Queue:

    def __init__(self, sem):
        self.sem, self.n, self.items, self.waited = sem, 0, [], {}

    def wait(self, *after):
        for t in after:
            if t is None:
                continue
            if isinstance(t, list):
                self.wait(*t)
                continue
            sem, v = t
            if self.waited.get(sem.name, 0) < v:
                self.waited[sem.name] = v
                self.items.append(lambda e, sem=sem, v=v: e.wait_ge(sem, v))

    def __call__(self, fn, *after, sig=True):
        self.wait(*after)
        if not sig:
            self.items.append(fn)
            return None
        self.n += 1
        self.items.append(lambda e: fn(e).then_inc(self.sem, 1))
        return (self.sem, self.n)

    def dma(self, out, in_, sem, n, *after):
        self.wait(*after)
        self.items.append(lambda e: e.dma_start(out, in_).then_inc(sem, 16))
        return (sem, 16 * n)

    def run(self, e):
        for f in self.items:
            f(e)


class Ring:

    def __init__(self, bufs, after=None):
        self.free = deque((b, after) for b in bufs)

    def take(self):
        return self.free.popleft()

    def give(self, b, tok):
        self.free.append((b, tok))


def build(nc, x_d, wd, w1_d, w3_d, w2_d, cols_d, rows_d, cst_d, wr_d, wpg_d, pT_d, tb_d, nb_d, out_d):
    with ExitStack() as ctx:
        def sb(name, shape, dt=F32):
            return ctx.enter_context(nc.sbuf_tensor(name, shape, dt))

        def sem(name):
            return ctx.enter_context(nc.semaphore(name))

        X = sb("X", [128, TT, D])
        cols = sb("cols", [128, NCOLS])
        rows = sb("rows", [128, NROWS])
        rowb = sb("rowb", [128, D])
        cst = sb("cst", [128, NCST])
        wr = sb("wr", [128, KD, 36])
        wpg = sb("wpg", [128, 4, 128])
        st = sb("st", [128, 1760])
        nex_i = sb("nex_i", [1, 1], I32)
        junk = sb("junk", [128, 4, D // 2], mybir.dt.bfloat16)

        def overlay(name, o, *shape, dt=F32R):
            with ExitStack() as s:
                if o:
                    s.enter_context(nc.sbuf_tensor(name + "_before", [128, o], F32))
                return s.enter_context(nc.sbuf_tensor(name, [128, *shape], dt))

        HTH, HTL = overlay("HTH", HT0, KD, NTOK), overlay("HTL", HT0 + 4096, KD, NTOK)
        w_hi = [overlay(f"w_hi{i}", SPLIT0 + 2 * UNIT * i, UNIT) for i in range(NSPLIT)]
        w_lo = [overlay(f"w_lo{i}", SPLIT0 + 2 * UNIT * i + UNIT, UNIT) for i in range(NSPLIT)]
        AH, AL = overlay("AH", R0, NATILE, NTOK), overlay("AL", R0 + NATILE * NTOK, NATILE, NTOK)
        XSH, XSL = overlay("XSH", A0, TT, D), overlay("XSL", A0 + 4096, TT, D)
        S = overlay("S", A0 + 8192, TT, 4 * C)
        ST = [overlay(f"ST{i}", A0 + 10240 + 512 * i, NTOK) for i in range(6)]
        YH, YL = ([overlay(f"{n}{i}", A0 + 13312 + o + 2048 * i, D) for i in range(3)] for n, o in (("YH", 0), ("YL", 1024)))
        OS = overlay("OS", A0 + 20736, TT, C)
        M = sb("M", [128, M_SZ])
        bank = [ctx.enter_context(nc.psum_tensor(f"bank{i}", [128, 512], F32)) for i in range(8)]

        def col(name, i=0, n=1):
            o = COLS[name][0]
            return cols[:, o + i:o + i + n]

        def row(name):
            o, w = ROWS[name]
            return rows[:, o:o + w]

        def con(name):
            o, w = CST[name]
            return cst[:, o:o + w]

        ident = con("ident")

        def mem(o, *shape):
            n = int(np.prod(shape))
            assert o + n <= M_SZ, (o, shape)
            v = M[:, o:o + n]
            if len(shape) == 2:
                v = v.rearrange("p (a b) -> p a b", a=shape[0])
            if len(shape) == 3:
                v = v.rearrange("p (a b c) -> p a b c", a=shape[0], b=shape[1])
            return v

        def region(o, *shape):
            return mem(R0 + o, *shape)

        def area(o, *shape):
            return mem(A0 + o, *shape)

        s_pe, s_act, s_dve, s_pool, s_sp = (sem(n) for n in ("s_pe", "s_act", "s_dve", "s_pool", "s_sp"))
        pe, act, dve, pool, sp = Queue(s_pe), Queue(s_act), Queue(s_dve), Queue(s_pool), Queue(s_sp)
        engines = (pe, act, dve, pool)

        def everything():
            return [(q.sem, q.n) for q in engines if q.n]

        misc = {}

        def load(q, name, out, in_, *after):
            misc[name] = q.dma(out, in_, sem("d_" + name), 1, *after)
            return misc[name]

        banks = Ring(list(range(8)))

        units = []
        where = {}

        def plan(key, src):
            where[key] = len(units)
            units.append(src)

        nd = [0]

        def dense(key):
            plan(key, wd[nd[0], :, :])
            nd[0] += 1

        for key in [("in", i) for i in range(8)]:
            dense(key)
        for i in range(4):
            if i % 2 == 0:
                dense(("ao", i // 2))
                dense(("po", i // 2))
            dense(("ga", i))
            dense(("gb", i))
        for i in range(4):
            dense(("wo", i))
        for n, (us, ds) in enumerate(ffn_order()):
            for u in us:
                dense(("uv", u))
                dense(("ug", u))
            for d in ds:
                dense(("dn", d))
        for i in range(12):
            dense(("in2", i))
        for i in range(4):
            dense(("out2", i))
        to_split = deque(k for k in where if k[0] not in ("ao", "po", "wo"))

        def expert(w, e, kh):
            if w == 2:
                src = w2_d[e, kh * 256:(kh + 1) * 256, :].rearrange("(k p) n -> p k n", p=128)
            else:
                src = (w1_d if w == 1 else w3_d)[e, kh * 512:(kh + 1) * 512, :].rearrange("(k p) n -> p k n", p=128)
            plan(("e", w, e, kh), src)

        for p in range(NPAIR + 1):
            for w in (1, 3):
                if p < NPAIR:
                    for kh in range(2):
                        for e in (2 * p, 2 * p + 1):
                            expert(w, e, kh)
            if p >= 1:
                for kh in range(2):
                    for e in (2 * p - 2, 2 * p - 1):
                        expert(2, e, kh)
        dense(("ple", 0))
        for i in range(4):
            dense(("plg", i))

        slots = [M[:, i * UNIT:(i + 1) * UNIT] for i in range(NS)]
        slot_sem = [sem(f"d_w{i}") for i in range(NS_MOE)]
        slot_n = [0] * NS_MOE
        slot_of = {}
        ready = {}
        free_slots = deque((i, None) for i in range(NS))
        issued = [0]
        split_free = deque((i, None) for i in range(NSPLIT))
        split_of = {}
        split_limit = [8]

        def issue():
            while free_slots and issued[0] < len(units):
                i, tok = free_slots.popleft()
                n = issued[0]
                src = units[n]
                dst = slots[i]
                if len(src.shape) == 3:
                    dst = dst.rearrange("p (k n) -> p k n", k=src.shape[1])
                slot_n[i] += 1
                slot_of[n] = i
                ready[n] = sp.dma(dst, src, slot_sem[i], slot_n[i], tok)
                issued[0] += 1

        def W(key, k):
            n = where[key]
            return slots[slot_of[n]].rearrange("p (k n) -> p k n", k=k), ready[n]

        def Wdone(key, tok):
            free_slots.append((slot_of[where[key]], tok))
            issue()
            ahead()

        def ahead():
            while split_free and to_split and split_limit[0] and where[to_split[0]] < issued[0]:
                key = to_split.popleft()
                split_limit[0] -= 1
                i, tok = split_free.popleft()
                n = where[key]
                raw = slots[slot_of[n]]
                a = act(lambda e, i=i, raw=raw: e.activation(w_hi[i][:, :], raw, ACT.Copy), ready[n], tok)
                d = dve(lambda e, i=i, raw=raw: e.tensor_tensor(w_lo[i][:, :], raw, w_hi[i][:, :], ALU.subtract), a)
                split_of[key] = (i, d)
                free_slots.append((slot_of[n], d))
                issue()

        def split_W(key, k):
            i, tok = split_of[key]
            return (*(v[i][:, :].rearrange("p (k n) -> p k n", k=k) for v in (w_hi, w_lo)), tok)

        def split_done(key, tok):
            split_free.append((split_of[key][0], tok))
            ahead()

        def allow(n, after):
            split_limit[0] += n
            assert len(split_free) == NSPLIT
            for _ in range(NSPLIT):
                i, tok = split_free.popleft()
                split_free.append((i, after))
            ahead()

        for t in range(TT):
            load(pool, f"x{t}", X[:, t, :], x_d[t * 128:(t + 1) * 128, :])
        load(pool, "cst", cst[:, :], cst_d)
        load(pool, "cols", cols[:, :], cols_d)
        issue()

        o_st = [0]

        def stat(n=1):
            a = st[:, o_st[0]:o_st[0] + n]
            o_st[0] += n
            assert o_st[0] <= 1760
            return a

        def rstd_of(ss, n, div, *after):
            ms, sq, r = stat(n), stat(n), stat(n)
            a = dve(lambda e: e.tensor_scalar(ms, ss, 1.0 / div, EPS, ALU.mult, ALU.add), *after)
            b = act(lambda e: e.activation(sq, ms, ACT.Sqrt), a)
            return r, dve(lambda e: e.reciprocal(r, sq), b)

        junk_r = Ring([junk[:, i, :] for i in range(4)])

        def sumsq(src, ss, *after):
            out = []
            for i in range(ss.shape[1]):
                j, jf = junk_r.take()
                a = act(lambda e, i=i, j=j: e.activation(j, src(i), ACT.Square, accum_out=ss[:, i:i + 1]), jf, *after)
                junk_r.give(j, a)
                out.append(a)
            return out

        def norm_to_T(gname, xt, xs, dst, dst_after, keep=None, y_r=None):
            ss2, ss = stat(2 * TT), stat(TT)
            toks = [sumsq(lambda i, t=t: X[:, t, i * 512:(i + 1) * 512], ss2[:, 2 * t:2 * t + 2], xt[t])
                    for t in range(TT)]
            a = dve(lambda e: e.tensor_reduce(ss, ss2.rearrange("p (t h) -> p t h", h=2), AX, ALU.add), toks)
            r, rt = rstd_of(ss, TT, D, a)
            out, kept = [], []
            for t in range(TT):
                buf, free = xs.take()
                a = dve(lambda e, t=t, buf=buf: e.tensor_scalar(buf, X[:, t, :], r[:, t:t + 1], None, ALU.mult),
                        rt, free)
                own = []
                if keep is not None:
                    c = act(lambda e, t=t, buf=buf: e.activation(keep[0][:, t, :], buf, ACT.Copy), a, dst_after)
                    own.append(pool(lambda e, t=t, buf=buf: e.tensor_tensor(keep[1][:, t, :], buf, keep[0][:, t, :],
                                                                            ALU.subtract), c))
                    kept.append(own[0])
                for h in range(2):
                    b, bf = banks.take()
                    for k in range(4):
                        m = pe(lambda e, k=k, b=b, h=h, buf=buf: e.transpose(
                            bank[b][:, k * 128:(k + 1) * 128], buf[:, (4 * h + k) * 128:(4 * h + k + 1) * 128], ident),
                            a, bf, misc["cst"], sig=(k == 3))
                    g = col(gname, 4 * h, 4).unsqueeze(2).to_broadcast([128, 4, 128])
                    place = (slice(None), slice(4 * h, 4 * h + 4), slice(t * 128, (t + 1) * 128))
                    if y_r is None:
                        y, yf = dst[place], dst_after
                    else:
                        y, yf = y_r.take()
                        y = y.rearrange("p (k n) -> p k n", k=4)
                    d = dve(lambda e, b=b, y=y, g=g: e.tensor_tensor(
                        y, bank[b][:, :].rearrange("p (k n) -> p k n", k=4), g, ALU.mult), m, misc["cols"], yf)
                    banks.give(b, d)
                    if y_r is not None:
                        c = act(lambda e, y=y, place=place: e.activation(HTH[place], y, ACT.Copy), d, dst_after)
                        d = pool(lambda e, y=y, place=place: e.tensor_tensor(HTL[place], y, HTH[place], ALU.subtract), c)
                        y_r.give(y.rearrange("p k n -> p (k n)"), d)
                    out.append(d)
                xs.give(buf, [m] + own)
            return (out, kept) if keep is not None else out

        def gemm_T(key, nk, n0, src, after, b, bf, mcols=128):
            w, wt = W(key, nk)
            for k in range(nk):
                m = pe(lambda e, k=k: e.matmul(bank[b][:, :], w[:, k, n0:n0 + mcols], src[:, k, :],
                                               start=(k == 0), stop=(k == nk - 1)),
                       wt, after, bf, sig=(k == nk - 1))
            return m

        def gemm_tok(keys, src, after, t, b, bf):
            for j, key in enumerate(keys):
                w, wt = W(key, KD)
                for k in range(KD):
                    m = pe(lambda e, k=k, w=w, j=j: e.matmul(
                        bank[b][:, j * 256:(j + 1) * 256], src[:, k, t * 128:(t + 1) * 128], w[:, k, :],
                        start=(k == 0), stop=(k == KD - 1)), wt, after, bf, sig=(k == KD - 1))
            return m

        def gemm3_T(key, n0, after, b, bf):
            wh, wl, wt = split_W(key, KD)
            for k in range(KD):
                for i, (w, src) in enumerate(((wh, HTH), (wh, HTL), (wl, HTH))):
                    last = k == KD - 1 and i == 2
                    m = pe(lambda e, k=k, w=w, src=src, i=i, last=last: e.matmul(
                        bank[b][:, :], w[:, k, n0:n0 + 128], src[:, k, :], start=(k == 0 and i == 0), stop=last),
                        wt, after, bf, sig=last)
            return m

        def gemm3_tok(keys, after, t, b, bf):
            for j, key in enumerate(keys):
                wh, wl, wt = split_W(key, 4)
                for k in range(4):
                    for i, (src, w) in enumerate(((HTH, wh), (HTH, wl), (HTL, wh))):
                        first, last = j == k == i == 0, j == 1 and k == 3 and i == 2
                        m = pe(lambda e, k=k, w=w, j=j, src=src, first=first, last=last: e.matmul(
                            bank[b][:, :], src[:, 4 * j + k, t * 128:(t + 1) * 128], w[:, k, :],
                            start=first, stop=last), wt, after, bf, sig=(k == 3 and i == 2))
            return m

        flip = [0]

        def evac(dst, src, after, scale=None):
            flip[0] ^= 1
            if flip[0]:
                if scale is None:
                    return act(lambda e: e.activation(dst, src, ACT.Copy), after)
                return act(lambda e: e.activation(dst, src, ACT.Copy, scale=scale), after)
            if scale is None:
                return dve(lambda e: e.tensor_copy(dst, src), after)
            return dve(lambda e: e.tensor_scalar(dst, src, scale, None, ALU.mult), after)

        qT = region(0, 4, 512)
        kT = region(2048, 4, 512)
        V = region(4096, 4, 512)
        U = region(6144, 4, 528)
        attnT = region(8256, 4, 512)
        mixedT = region(10304, 4, 512)
        TB = [region(12352 + 512 * i, 512) for i in range(3)] + [mem(SPLIT0 + 512 * i, 512) for i in range(5)]
        sc_r = [mem(SPLIT0 + 2560 + 512 * i, 512) for i in range(3)]
        P_r = [mem(SPLIT0 + 4096 + 512 * i, 512) for i in range(4)]
        PT_r = [mem(SPLIT0 + 6144 + 512 * i, 512) for i in range(4)]
        ps_r = [mem(SPLIT0 + 8192 + 528 * i, 528) for i in range(3)]
        load(pool, "wpg", wpg[:, :, :], wpg_d)
        for h in range(3):
            load(pool, f"tb{h}", TB[h], tb_d[:, h, :])
        load(pool, "rows", rows[:, :], rows_d[:, 3072:3072 + NROWS].to_broadcast([128, NROWS]))

        def load_row(name, *after):
            o = BIG[name]
            load(pool, "row_" + name, rowb[:, :], rows_d[:, o:o + D].to_broadcast([128, D]), *after)

        load_row("mix_post")
        load(pool, "wr", wr[:, :, :], wr_d)

        xs_ring = Ring([region(8256 + 1024 * i, 1024) for i in range(3)])
        y_ring = Ring([region(11328 + 512 * i, 512) for i in range(2)])
        xt = [misc[f"x{t}"] for t in range(TT)]
        hT_t = norm_to_T("mix_pre", xt, xs_ring, None, None, y_r=y_ring)
        ahead()

        zu = pool(lambda e: e.memset(U[:, :, 0:16], 0.0))
        qk_t = {}
        for i in range(4):
            for j in range(2):
                n = 2 * i + j
                b, bf = banks.take()
                m = gemm3_T(("in", i), j * 128, hT_t, b, bf)
                dst = qT[:, n, :] if n < 4 else kT[:, n - 4, :]
                qk_t[n] = evac(dst, bank[b][:, :], m, 0.125 if n < 4 else None)
                banks.give(b, qk_t[n])
            split_done(("in", i), m)
        v_t = []
        for t in range(TT):
            b, bf = banks.take()
            m = gemm3_tok([("in", 4), ("in", 5)], hT_t, t, b, bf)
            v_t.append(evac(V[:, t, :], bank[b][:, :], m))
            banks.give(b, v_t[-1])
        split_done(("in", 4), m)
        split_done(("in", 5), m)
        u_t = []
        for i in range(2):
            for j in range(2):
                g = 2 * i + j
                b, bf = banks.take()
                m = gemm3_T(("in", 6 + i), j * 128, hT_t, b, bf)
                u_t.append(evac(U[:, g, 16:528], bank[b][:, :], m))
                banks.give(b, u_t[-1])
            split_done(("in", 6 + i), m)
        free1 = everything()
        for h in range(3, 8):
            load(pool, f"tb{h}", TB[h], tb_d[:, h, :], free1)

        def pool_group(g):
            cur, cur_t = U[:, g, :], [u_t[g], zu]
            lo = 0
            for s in range(g + 1):
                d = 1 << s
                nxt = ps_r[s % 2]
                lo2 = lo + d
                cur_t = [pool(lambda e, cur=cur, nxt=nxt, d=d, lo2=lo2: e.tensor_tensor(
                    nxt[:, lo2:528], cur[:, lo2:528], cur[:, lo2 - d:528 - d], ALU.add), cur_t, free1)]
                cur, lo = nxt, lo2
            w = 2 << g
            pl = ps_r[2][:, 0:512]
            mean = pool(lambda e: e.tensor_scalar(pl, cur[:, 16:528], 1.0 / w, None, ALU.mult), cur_t, pg_free[0])
            cn = con("cnt")[:, 16 * g:16 * g + w - 1]
            fix = pool(lambda e: e.tensor_tensor(pl[:, 0:w - 1], cur[:, 16:16 + w - 1], cn, ALU.mult),
                       mean, misc["cst"])
            sub = pool(lambda e: e.tensor_tensor(pl, pl, U[:, g, 16:528], ALU.subtract), fix)
            b, bf = banks.take()
            m = pe(lambda e: e.matmul(bank[b][:, :], wpg[:, g, :], pl, start=True, stop=True), sub, bf, misc["wpg"])
            pg_free[0] = m
            d = act(lambda e: e.activation(mixedT[:, g, :], bank[b][:, :], ACT.Copy, scale=col("pool_scale", g)),
                    m, misc["cols"])
            banks.give(b, d)
            return d

        pg_free = [None]
        mixed_t = []

        sc_ring, P_ring, PT_ring = (Ring(r, free1) for r in (sc_r, P_r, PT_r))
        items = [(h, qt) for h in range(8) for qt in range(4)]
        ob = {}
        state = {}
        attn_t = []

        def a0(i):
            h, qt = items[i]
            nk, pr, hp = 128 * (qt + 1), 64 * (h % 2), h // 2
            b, bf = banks.take()
            m = pe(lambda e: e.matmul(bank[b][:, 0:nk], qT[pr:pr + 64, hp, qt * 128:(qt + 1) * 128],
                                      kT[pr:pr + 64, hp, 0:nk], start=True, stop=True),
                   bf, qk_t[hp], qk_t[4 + hp])
            sc, sf = sc_ring.take()
            P, pf = P_ring.take()
            mx, nm, rs, rr = stat(), stat(), stat(), stat()
            a = dve(lambda e: e.tensor_tensor_reduce(sc[:, 0:nk], bank[b][:, 0:nk], TB[h][:, 384 - 128 * qt:512], 1.0,
                                                     -3e38, ALU.add, ALU.max, mx), m, sf, misc[f"tb{h}"])
            banks.give(b, a)
            c = dve(lambda e: e.tensor_scalar(nm, mx, -1.0, None, ALU.mult), a)
            ex = act(lambda e: e.activation(P[:, 0:nk], sc[:, 0:nk], ACT.Exp, bias=nm, accum_out=rs), c, pf)
            sc_ring.give(sc, ex)
            r = dve(lambda e: e.reciprocal(rr, rs), ex)
            n = dve(lambda e: e.tensor_scalar(P[:, 0:nk], P[:, 0:nk], rr, None, ALU.mult), r)
            state[i] = (P, n)

        def a1(i):
            h, qt = items[i]
            P, n = state[i]
            b, bf = banks.take()
            for k in range(qt + 1):
                m = pe(lambda e, k=k: e.transpose(bank[b][:, k * 128:(k + 1) * 128], P[:, k * 128:(k + 1) * 128],
                                                  ident), n, bf, sig=(k == qt))
            P_ring.give(P, m)
            PT, pf = PT_ring.take()
            nk = 128 * (qt + 1)
            ev = act(lambda e: e.activation(PT[:, 0:nk], bank[b][:, 0:nk], ACT.Copy), m, pf)
            banks.give(b, ev)
            state[i] = (PT, ev)

        def a2(i):
            h, qt = items[i]
            PT, ev = state[i]
            pr, hp = 64 * (h % 2), h // 2
            if hp not in ob:
                ob[hp] = banks.take()
            b, bf = ob[hp]
            for k in range(qt + 1):
                m = pe(lambda e, k=k: e.matmul(bank[b][pr:pr + 64, qt * 128:(qt + 1) * 128],
                                               V[:, k, h * 64:(h + 1) * 64], PT[:, k * 128:(k + 1) * 128],
                                               start=(k == 0), stop=(k == qt)), ev, bf, v_t, sig=(k == qt))
            PT_ring.give(PT, m)
            if h % 2 and qt == 3:
                d = dve(lambda e: e.tensor_copy(attnT[:, hp, :], bank[b][:, :]), m)
                banks.give(b, d)
                attn_t.append(d)

        for i in range(len(items) + 2):
            if i < len(items):
                a0(i)
            if 1 <= i <= len(items):
                a1(i - 1)
            if i >= 2:
                a2(i - 2)
            if i % 8 == 4 and i // 8 < 4:
                mixed_t.append(pool_group(i // 8))
        free2 = everything()

        MT = region(0, 8, 512)
        g_ring = Ring([region(4096 + 512 * i, 512) for i in range(8)], free2)
        allow(8 + 33 + 12, free2)
        mt_t = []
        for n in range(8):
            bs = [banks.take() for _ in range(4)]
            ka, kb = ("ga", n // 2), ("gb", n // 2)
            ma = gemm3_T(ka, (n % 2) * 128, hT_t, *bs[0])
            mb = gemm3_T(kb, (n % 2) * 128, hT_t, *bs[1])
            mya = gemm_T(("ao", n // 4), 4, (n % 4) * 128, attnT, attn_t, *bs[2])
            myb = gemm_T(("po", n // 4), 4, (n % 4) * 128, mixedT, mixed_t, *bs[3])
            if n % 2:
                split_done(ka, ma)
                split_done(kb, mb)
            if n % 4 == 3:
                Wdone(("ao", n // 4), mya)
                Wdone(("po", n // 4), myb)
            (ga, fa), (gb, fb) = g_ring.take(), g_ring.take()
            sa = act(lambda e, n=n, b=bs[0][0], ga=ga: e.activation(ga, bank[b][:, :], ACT.Sigmoid,
                                                                    bias=col("b_gate", n)), ma, fa)
            banks.give(bs[0][0], sa)
            sg = act(lambda e, n=n, b=bs[1][0], gb=gb: e.activation(gb, bank[b][:, :], ACT.Sigmoid,
                                                                    bias=col("b_gate", 8 + n)), mb, fb)
            banks.give(bs[1][0], sg)
            ta = dve(lambda e, b=bs[2][0], ga=ga: e.tensor_tensor(ga, bank[b][:, :], ga, ALU.mult), sa, mya)
            banks.give(bs[2][0], ta)
            tb_ = dve(lambda e, b=bs[3][0], gb=gb: e.tensor_tensor(gb, bank[b][:, :], gb, ALU.mult), sg, myb)
            banks.give(bs[3][0], tb_)
            d = pool(lambda e, n=n, ga=ga, gb=gb: e.tensor_tensor(MT[:, n, :], ga, gb, ALU.add), ta, tb_, free2)
            g_ring.give(ga, d)
            g_ring.give(gb, d)
            mt_t.append(d)

        def residual(halves, gname, tt, scratch, *more):
            ss, s1 = stat(2), stat()
            tmp, tf = scratch
            q = sumsq(lambda i: halves[i][0], ss, halves[0][1], halves[1][1])
            a = dve(lambda e: e.tensor_tensor(s1, ss[:, 0:1], ss[:, 1:2], ALU.add), q)
            r, rt = rstd_of(s1, 1, D, a)
            z = [dve(lambda e, h=h: e.scalar_tensor_tensor(
                out=tmp[:, h * 512:(h + 1) * 512], in0=halves[h][0], scalar=r,
                in1=rowb[:, h * 512:(h + 1) * 512], op0=ALU.mult, op1=ALU.mult),
                rt, tf, misc["row_" + gname]) for h in range(2)]
            f = pool(lambda e: e.tensor_tensor(X[:, tt, :], X[:, tt, :], tmp, ALU.add), z, *more)
            return z, f

        free_s = everything()
        tmp_ring = Ring([region(8256 + 1024 * i, 1024) for i in range(4)], free_s)
        x_t = []
        held = {}
        for h in range(2):
            for t in range(TT):
                b, bf = banks.take()
                m = gemm_tok([("wo", 2 * h), ("wo", 2 * h + 1)], MT, mt_t, t, b, bf)
                held[t, h] = (b, m)
            Wdone(("wo", 2 * h), m)
            Wdone(("wo", 2 * h + 1), m)
        for t in range(TT):
            tmp, tf = tmp_ring.take()
            z, f = residual([(bank[held[t, h][0]][:, :], held[t, h][1]) for h in range(2)], "mix_post", t, (tmp, tf))
            for h in range(2):
                banks.give(held[t, h][0], z[h])
            tmp_ring.give(tmp, f)
            x_t.append(f)
        free3 = everything()
        load_row("ffn_post", free3)

        xs_ring = Ring([region(1024 * i, 1024) for i in range(3)], free3)
        y_ring = Ring([region(3072 + 512 * i, 512) for i in range(4)], free3)
        hT_t = norm_to_T("ffn_pre", x_t, xs_ring, None, free3, y_r=y_ring)
        free4 = everything()
        FACC = region(6144, 4, 1024)
        zv_ring = Ring([region(10240 + 512 * i, 512) for i in range(3)], free4)
        zg_ring = Ring([region(11776 + 512 * i, 512) for i in range(4)], free4)
        tile_ring = Ring(list(range(NATILE)), free4)
        facc_t = {(t, h): free4 for t in range(TT) for h in range(2)}

        def conv(b, m, z, zf, n):
            cw = [col("conv_w", i * 44 + n) for i in range(3)]
            a = act(lambda e: e.activation(z, bank[b][:, :], ACT.Identity, bias=col("conv_b", n), scale=cw[2]), m, zf)
            c = dve(lambda e: e.scalar_tensor_tensor(out=z[:, 2:512], in0=bank[b][:, 0:510], scalar=cw[0],
                                                     in1=z[:, 2:512], op0=ALU.mult, op1=ALU.add), a)
            d = dve(lambda e: e.scalar_tensor_tensor(out=z[:, 1:512], in0=bank[b][:, 0:511], scalar=cw[1],
                                                     in1=z[:, 1:512], op0=ALU.mult, op1=ALU.add), c)
            banks.give(b, d)
            return d

        made = deque()

        def up(uu):
            for j in range(2):
                n = 2 * uu + j
                b1, f1 = banks.take()
                mv = gemm3_T(("uv", uu), j * 128, hT_t, b1, f1)
                b2, f2 = banks.take()
                mg = gemm3_T(("ug", uu), j * 128, hT_t, b2, f2)
                if j:
                    split_done(("uv", uu), mv)
                    split_done(("ug", uu), mg)
                (zv, fv), (zg, fg) = zv_ring.take(), zg_ring.take()
                i, af = tile_ring.take()
                dg = conv(b2, mg, zg, fg, 22 + n)
                dv = conv(b1, mv, zv, fv, n)
                ge = act(lambda e, zg=zg: e.activation(zg, zg, ACT.Gelu_apprx_tanh), dg)
                o = pool(lambda e, zg=zg, zv=zv: e.tensor_tensor(zg, zg, zv, ALU.mult), ge, dv)
                zv_ring.give(zv, o)
                hi = act(lambda e, i=i, zg=zg: e.activation(AH[:, i, :], zg, ACT.Copy), o, af)
                lo = pool(lambda e, i=i, zg=zg: e.tensor_tensor(AL[:, i, :], zg, AH[:, i, :], ALU.subtract), hi)
                zg_ring.give(zg, lo)
                made.append((i, lo))

        def down(ds, first):
            tiles = [made.popleft() for _ in range(2 * len(ds))]
            for t in range(TT):
                for h in range(2):
                    b, bf = banks.take()
                    for i, (a, at) in enumerate(tiles):
                        wh, wl, wt = split_W(("dn", ds[i // 2]), 2)
                        for q, (src, w) in enumerate(((AH, wh), (AH, wl), (AL, wh))):
                            last = i == len(tiles) - 1 and q == 2
                            m = pe(lambda e, i=i, a=a, q=q, src=src, w=w, t=t, h=h, b=b, last=last: e.matmul(
                                bank[b][:, :], src[:, a, t * 128:(t + 1) * 128], w[:, i % 2, h * 512:(h + 1) * 512],
                                start=(i == 0 and q == 0), stop=last), wt, bf, at, sig=last)
                    dst = FACC[:, t, h * 512:(h + 1) * 512]
                    if first:
                        f = dve(lambda e, dst=dst, b=b: e.tensor_copy(dst, bank[b][:, :]), m, facc_t[t, h])
                    else:
                        f = dve(lambda e, dst=dst, b=b: e.tensor_tensor(dst, bank[b][:, :], dst, ALU.add), m,
                                facc_t[t, h])
                    banks.give(b, f)
                    facc_t[t, h] = f
            for a, _ in tiles:
                tile_ring.give(a, m)
            for d in ds:
                split_done(("dn", d), m)
            return m

        for n, (us, ds) in enumerate(ffn_order()):
            for uu in us:
                up(uu)
            m = down(ds, n == 0)

        tmp_ring = Ring([region(1024 * i, 1024) for i in range(4)], m)
        x_t = []
        for t in range(TT):
            tmp, tf = tmp_ring.take()
            z, f = residual([(FACC[:, t, h * 512:(h + 1) * 512], facc_t[t, h]) for h in range(2)], "ffn_post", t,
                            (tmp, tf))
            tmp_ring.give(tmp, f)
            x_t.append(f)
        free5 = everything()
        load_row("ple", free5)

        xs_ring = Ring([region(1024 * i, 1024) for i in range(3)], free5)
        y_ring = Ring([region(4096 + 512 * i, 512) for i in range(4)], free5)
        aT_t = norm_to_T("mix2", x_t, xs_ring, None, free5, y_r=y_ring)
        free6 = everything()

        qaT, kaT = region(0, 4, 512), region(2048, 4, 512)
        qbT, kbT = region(4096, 4, 512), region(6144, 4, 512)
        Va = region(8192, 4, 512)
        sqr = Ring([region(10240 + 512 * i, 512) for i in range(2)], free6)
        qnr = Ring([region(11264 + 512 * i, 512) for i in range(5)], free6)
        t1r = Ring([region(6144 + 512 * i, 512) for i in range(2)], free6)
        t2r = Ring([region(7168 + 512 * i, 512) for i in range(2)], free6)

        def qk_tok(unit, nh, gname, dstT, scale, rope, by_block=False):
            dh = 512 // nh
            outs = []
            pend = []

            def first(t):
                b, bf = banks.take()
                m = gemm3_tok([("in2", unit), ("in2", unit + 1)], aT_t, t, b, bf)
                sq, sf = sqr.take()
                ss = stat(nh)
                a = act(lambda e: e.activation(sq, bank[b][:, :], ACT.Square), m, sf)
                c = dve(lambda e: e.tensor_reduce(ss, sq.rearrange("p (h d) -> p h d", h=nh), AX, ALU.add), a)
                sqr.give(sq, c)
                r, rt = rstd_of(ss, nh, dh, c)
                qn, qf = qnr.take()
                q3 = qn.rearrange("p (h d) -> p h d", h=nh)
                d = dve(lambda e: e.tensor_tensor(q3, bank[b][:, :].rearrange("p (h d) -> p h d", h=nh),
                                                  r.unsqueeze(2).to_broadcast([128, nh, dh]), ALU.mult), rt, qf)
                banks.give(b, d)
                g = row(gname).unsqueeze(1).to_broadcast([128, nh, dh])
                f = pool(lambda e: e.tensor_tensor(q3, q3, g, ALU.mult), d)
                if rope:
                    (t1, f1), (t2, f2) = t1r.take(), t2r.take()
                    co = con("cos")[:, t * 32:(t + 1) * 32].unsqueeze(1).to_broadcast([128, 16, 32])
                    si = con("sin")[:, t * 32:(t + 1) * 32].unsqueeze(1).to_broadcast([128, 16, 32])
                    v16 = lambda a: a.rearrange("p (h d) -> p h d", h=16)
                    v4 = lambda a, s: a.rearrange("p (h s d) -> p h s d", s=2, d=32)[:, :, s, :]
                    c1 = dve(lambda e: e.tensor_tensor(v16(t1), v16(qn), co, ALU.mult), f, f1)
                    c2 = dve(lambda e: e.tensor_tensor(v16(t2), v16(qn), si, ALU.mult), f, f2)
                    e1 = pool(lambda e: e.tensor_tensor(v4(qn, 0), v4(t1, 0), v4(t2, 1), ALU.subtract), c1, c2)
                    f = pool(lambda e: e.tensor_tensor(v4(qn, 1), v4(t1, 1), v4(t2, 0), ALU.add), e1)
                    t1r.give(t1, f)
                    t2r.give(t2, f)
                pend.append((t, qn, f))

            def second():
                t, qn, f = pend.pop(0)
                b, bf = banks.take()
                for k in range(4):
                    m = pe(lambda e, k=k: e.transpose(bank[b][:, k * 128:(k + 1) * 128], qn[:, k * 128:(k + 1) * 128],
                                                      ident), f, bf, sig=(k == 3))
                qnr.give(qn, m)
                dst = dstT[:, :, t * 128:(t + 1) * 128]
                src = bank[b][:, :].rearrange("p (k n) -> p k n", k=4)
                if by_block:
                    for f in range(4):
                        d4 = dstT[:, f, :].rearrange("p (j r c) -> p j r c", j=4, r=8)[:, :, 2 * t:2 * t + 2, :]
                        s4 = src[:, f, :].rearrange("p (r j c) -> p j r c", r=2, j=4)
                        for rr in range(2):
                            o = act(lambda e, d4=d4, s4=s4, rr=rr: e.activation(d4[:, :, rr, :], s4[:, :, rr, :], ACT.Copy,
                                                                                scale=scale), m)
                elif scale is None:
                    o = act(lambda e: e.activation(dst, src, ACT.Copy), m)
                else:
                    o = act(lambda e: e.activation(dst, src, ACT.Copy, scale=scale), m)
                banks.give(b, o)
                outs.append(o)

            for t in range(TT):
                first(t)
                if t >= 1:
                    second()
            last = (s_pe, pe.n)
            second()
            split_done(("in2", unit), last)
            split_done(("in2", unit + 1), last)
            return outs

        qa_t = qk_tok(0, 8, "qa", qaT, 0.125, True)
        ka_t = qk_tok(2, 8, "ka", kaT, None, True)
        va_t = []
        for t in range(TT):
            b, bf = banks.take()
            m = gemm3_tok([("in2", 4), ("in2", 5)], aT_t, t, b, bf)
            va_t.append(evac(Va[:, t, :], bank[b][:, :], m))
            banks.give(b, va_t[-1])
        split_done(("in2", 4), m)
        split_done(("in2", 5), m)
        qb_t = qk_tok(6, 16, "qb", qbT, 32.0 ** -0.5, False, by_block=True)
        kb_t = qk_tok(8, 16, "kb", kbT, None, False)
        sa, sb_ = (SPLIT0 + 2 * UNIT * split_of["in2", 10 + i][0] for i in range(2))
        sc = 3 * SPLIT0 + 6 * UNIT - sa - sb_
        vbJ = mem(sc, 4, 4, 256)
        Vj = mem(sa, 8, 512)
        KB = [0, 8, 24, 32]
        vb_t = [[] for _ in range(4)]
        free_v = everything()
        for i in range(2):
            for jj in range(2):
                f = 2 * i + jj
                b, bf = banks.take()
                m = gemm3_T(("in2", 10 + i), jj * 128, aT_t, b, bf)
                b4 = bank[b][:, :].rearrange("p (r c) -> p r c", c=64)
                for j in range(4):
                    o = act(lambda e, f=f, j=j, b4=b4: e.activation(
                        vbJ[:, f, j, :].rearrange("p (r c) -> p r c", c=32), b4[:, :, KB[j]:KB[j] + 32], ACT.Copy),
                        m, free_v)
                    vb_t[j].append(o)
                banks.give(b, o)
            split_done(("in2", 10 + i), m)
        free_j = everything()
        vj_t = []
        for j in range(4):
            for half in range(2):
                b, bf = banks.take()
                for f in range(4):
                    m = pe(lambda e, f=f, j=j, half=half, b=b: e.transpose(
                        bank[b][:, f * 128:(f + 1) * 128], vbJ[:, f, j, half * 128:(half + 1) * 128], ident),
                        vb_t[j], bf, sig=(f == 3))
                vj_t.append(evac(Vj[:, 2 * j + half, :], bank[b][:, :], [m, free_j]))
                banks.give(b, vj_t[-1])
        free7 = everything()

        lam = stat(6)
        lt = [stat(64), stat(64)]
        lp = []
        for i, (a_, b_) in enumerate((("lq1", "lk1"), ("lq2", "lk2"))):
            lp.append(dve(lambda e, i=i, a_=a_, b_=b_: e.tensor_tensor_reduce(
                lt[i], row(a_), row(b_), 1.0, 0.0, ALU.mult, ALU.add, lam[:, i:i + 1]), misc["rows"]))
        le = act(lambda e: e.activation(lam[:, 2:4], lam[:, 0:2], ACT.Exp), lp)
        lm0 = dve(lambda e: e.tensor_tensor(lam[:, 4:5], lam[:, 2:3], lam[:, 3:4], ALU.subtract), le)
        LAM0 = 0.8 - 0.6 * float(np.exp(0.0))
        lm = dve(lambda e: e.tensor_scalar(lam[:, 5:6], lam[:, 4:5], LAM0, None, ALU.add), lm0)

        OR = region(10240, 4, 512)
        wTr = Ring([region(12288 + 512 * i, 512) for i in range(3)], free7)
        e1r = Ring([mem(sb_ + 512 * i, 512) for i in range(4)], free7)
        e2r = Ring([mem(sb_ + 2048 + 512 * i, 512) for i in range(4)], free7)
        nb1 = mem(sc, 4, 3, 256)
        nbr = Ring([nb1], free7)
        nb_sem = [sem("d_nb0"), sem("d_nb1")]
        nb_n = [0, 0]

        def nb_load(hg):
            buf, bf = nbr.take()
            i = hg % 2
            nb_n[i] += 1
            return buf, sp.dma(buf, nb_d[hg, :, :].rearrange("p (h j k) -> p h j k", h=4, j=3), nb_sem[i], nb_n[i], bf)

        nbs = [nb_load(0)]
        items = [(h, qt) for h in range(4) for qt in range(4)]
        state = {}
        ob = {}
        or_t = {}

        def d0(i):
            h, qt = items[i]
            ms = []
            bs = []
            for s in range(2):
                b, bf = banks.take()
                bs.append(b)
                ms.append(pe(lambda e, s=s, b=b: e.matmul(
                    bank[b][:, :], qaT[64 * s:64 * s + 64, h, qt * 128:(qt + 1) * 128],
                    kaT[64 * s:64 * s + 64, h, :], start=True, stop=True), bf, qa_t, ka_t))
            nm, rs, rr = stat(2), stat(2), stat(3)
            E = [e1r.take(), e2r.take()]
            ex = []
            for s in range(2):
                a = dve(lambda e, s=s: e.tensor_reduce(nm[:, s:s + 1], bank[bs[s]][:, :], AX, ALU.max, negate=True), ms[s])
                x_ = act(lambda e, s=s: e.activation(E[s][0], bank[bs[s]][:, :], ACT.Exp, bias=nm[:, s:s + 1],
                                                     accum_out=rs[:, s:s + 1]), a, E[s][1])
                banks.give(bs[s], x_)
                ex.append(x_)
            r = dve(lambda e: e.reciprocal(rr[:, 0:2], rs), ex)
            l = dve(lambda e: e.tensor_tensor(rr[:, 2:3], rr[:, 1:2], lam[:, 5:6], ALU.mult), r, lm)
            t = dve(lambda e: e.tensor_scalar(E[1][0], E[1][0], rr[:, 2:3], None, ALU.mult), l)
            w = dve(lambda e: e.scalar_tensor_tensor(out=E[0][0], in0=E[0][0], scalar=rr[:, 0:1], in1=E[1][0],
                                                     op0=ALU.mult, op1=ALU.subtract), t)
            e2r.give(E[1][0], w)
            state[i] = (E[0][0], w)

        def d1(i):
            Wt, w = state[i]
            b, bf = banks.take()
            for k in range(4):
                m = pe(lambda e, k=k: e.transpose(bank[b][:, k * 128:(k + 1) * 128], Wt[:, k * 128:(k + 1) * 128], ident),
                       w, bf, sig=(k == 3))
            e1r.give(Wt, m)
            wT, wf = wTr.take()
            ev = act(lambda e: e.activation(wT, bank[b][:, :], ACT.Copy), m, wf)
            banks.give(b, ev)
            state[i] = (wT, ev)

        def d2(i):
            h, qt = items[i]
            wT, ev = state[i]
            if h not in ob:
                ob[h] = banks.take()
            b, bf = ob[h]
            for k in range(4):
                m = pe(lambda e, k=k: e.matmul(bank[b][:, qt * 128:(qt + 1) * 128], wT[:, k * 128:(k + 1) * 128],
                                               Va[:, k, h * 128:(h + 1) * 128], start=(k == 0), stop=(k == 3)),
                       ev, bf, va_t, sig=(k == 3))
            wTr.give(wT, m)
            if qt == 3:
                d = dve(lambda e: e.tensor_copy(OR[:, :, h * 128:(h + 1) * 128],
                                                bank[b][:, :].rearrange("p (q d) -> p q d", q=4)), m, free7)
                banks.give(b, d)
                or_t[h] = d

        n = len(items)
        for i in range(n + 2):
            if i < n:
                d0(i)
            if 1 <= i <= n:
                d1(i - 1)
            if i >= 2:
                d2(i - 2)

        free8 = everything()
        nbr.give(region(0, 4, 3, 256), free8)
        nbs.append(nb_load(1))
        scr = Ring([region(8192, 4, 256), region(9216, 4, 256)], free8)
        Pr = Ring([region(3072, 4, 256), mem(sc + 3072, 4, 256), mem(sb_, 4, 256)], free8)
        PTr = Ring([mem(sb_ + 1024, 8, 128), mem(sb_ + 2048, 8, 128)], free8)
        items = [(hg, j) for hg in range(4) for j in range(4)]
        state = {}
        ob = {}
        cat_t = []
        k4 = kbT.rearrange("p f (r c) -> p f r c", c=64)
        catR = [v[:, :, :].rearrange("p f (r c) -> p f r c", c=64) for v in (HTH, HTL)]

        def n0(i):
            hg, j = items[i]
            nb, nt = nbs[hg]
            jt = (0, 1, 1, 2)[j]
            scb, sf = scr.take()
            P, pf = Pr.take()
            mx, nm, rs, rr = stat(4), stat(4), stat(4), stat(4)
            tt = []
            for hh in range(4):
                b, bf = banks.take()
                m = pe(lambda e, hh=hh, b=b: e.matmul(
                    bank[b][:, 0:256], qbT[32 * hh:32 * hh + 32, hg, 128 * j:128 * j + 128],
                    k4[32 * hh:32 * hh + 32, hg, :, KB[j]:KB[j] + 32], start=True, stop=True,
                    tile_position=(32 * hh, 0)), bf, qb_t, kb_t)
                a = dve(lambda e, hh=hh, b=b: e.tensor_tensor_reduce(
                    scb[:, hh, :], bank[b][:, 0:256], nb[:, hh, jt, :], 1.0, -3e38,
                    ALU.add, ALU.max, mx[:, hh:hh + 1]), m, sf, nt)
                tt.append(a)
                banks.give(b, a)
            c = dve(lambda e: e.tensor_scalar(nm, mx, -1.0, None, ALU.mult), tt)
            for g in range(4):
                ex = act(lambda e, g=g: e.activation(P[:, g, :], scb[:, g, :], ACT.Exp, bias=nm[:, g:g + 1],
                                                     accum_out=rs[:, g:g + 1]), c, pf)
            scr.give(scb, ex)
            r = dve(lambda e: e.reciprocal(rr, rs), ex)
            d = dve(lambda e: e.tensor_tensor(P, P, rr.unsqueeze(2).to_broadcast([128, 4, 256]), ALU.mult), r)
            state[i] = (P, d)
            if j == 3:
                nbr.give(nb, tt[-1])
                if hg + 2 < 4:
                    nbs.append(nb_load(hg + 2))

        def n1(i):
            P, d = state[i]
            PT, pf = PTr.take()
            evs = []
            for half in range(2):
                b, bf = banks.take()
                for g in range(4):
                    m = pe(lambda e, g=g, b=b, half=half: e.transpose(
                        bank[b][:, g * 128:(g + 1) * 128], P[:, g, half * 128:(half + 1) * 128], ident),
                        d, bf, sig=(g == 3))
                src = bank[b][:, :].rearrange("p (g q) -> p g q", g=4)
                ev = evac(PT[:, 4 * half:4 * half + 4, :], src, [m, pf])
                banks.give(b, ev)
                evs.append(ev)
            Pr.give(P, m)
            state[i] = (PT, evs)

        def n2(i):
            hg, j = items[i]
            PT, evs = state[i]
            if hg not in ob:
                ob[hg] = banks.take()
            b, bf = ob[hg]
            for g in range(4):
                for half in range(2):
                    m = pe(lambda e, g=g, half=half: e.matmul(
                        bank[b][32 * g:32 * g + 32, j * 128:(j + 1) * 128],
                        Vj[:, 2 * j + half, hg * 128 + 32 * g:hg * 128 + 32 * g + 32], PT[:, 4 * half + g, :],
                        start=(half == 0), stop=(half == 1), tile_position=(0, 32 * g)),
                        evs, bf, vj_t, sig=(g == 3 and half == 1))
            PTr.give(PT, m)
            if j == 3:
                for jj in range(4):
                    hi = catR[0][:, 4 + hg, :, 16 * jj:16 * jj + 16]
                    src = bank[b][:, jj * 128:(jj + 1) * 128].rearrange("p (r c) -> p r c", c=16)
                    c = act(lambda e, hi=hi, src=src: e.activation(hi, src, ACT.Copy), m)
                for jj in range(4):
                    hi, lo = (v[:, 4 + hg, :, 16 * jj:16 * jj + 16] for v in catR)
                    src = bank[b][:, jj * 128:(jj + 1) * 128].rearrange("p (r c) -> p r c", c=16)
                    o = dve(lambda e, hi=hi, lo=lo, src=src: e.tensor_tensor(lo, src, hi, ALU.subtract), c)
                banks.give(b, o)
                cat_t.append(o)

        for i in range(len(items) + 2):
            if i < len(items):
                n0(i)
            if i >= 2:
                n2(i - 2)
            if 1 <= i <= len(items):
                n1(i - 1)

        free_n = everything()
        allow(4, free_n)
        gs_ = stat()
        gs_t = dve(lambda e: e.tensor_scalar(gs_, col("g_sub"), 1.0 - LAM0, None, ALU.mult))
        sqr = Ring([region(8192 + 512 * i, 512) for i in range(2)], free_n)
        for t in range(TT):
            ss = stat(4)
            sq, sf = sqr.take()
            o3 = OR[:, t, :].rearrange("p (h d) -> p h d", h=4)
            a = act(lambda e, t=t, sq=sq: e.activation(sq, OR[:, t, :], ACT.Square), list(or_t.values()), sf)
            c = dve(lambda e, ss=ss, sq=sq: e.tensor_reduce(ss, sq.rearrange("p (h d) -> p h d", h=4), AX, ALU.add), a)
            sqr.give(sq, c)
            r, rt = rstd_of(ss, 4, 128, c)
            d = dve(lambda e, o3=o3, r=r: e.tensor_tensor(o3, o3, r.unsqueeze(2).to_broadcast([128, 4, 128]), ALU.mult), rt)
            b, bf = banks.take()
            for k in range(4):
                m = pe(lambda e, k=k, b=b, t=t: e.transpose(bank[b][:, k * 128:(k + 1) * 128],
                                                            OR[:, t, k * 128:(k + 1) * 128], ident), d, bf, sig=(k == 3))
            place = (slice(None), slice(0, 4), slice(t * 128, (t + 1) * 128))
            src = bank[b][:, :].rearrange("p (k n) -> p k n", k=4)
            c = act(lambda e, place=place, src=src: e.activation(HTH[place], src, ACT.Copy, scale=gs_), m, gs_t)
            f = dve(lambda e, place=place, src=src: e.scalar_tensor_tensor(
                out=HTL[place], in0=src, scalar=gs_, in1=HTH[place], op0=ALU.mult, op1=ALU.subtract), c)
            banks.give(b, f)
            cat_t.append(f)

        x_t = []
        for h in range(2):
            for t in range(TT):
                b, bf = banks.take()
                m = gemm3_tok([("out2", 2 * h), ("out2", 2 * h + 1)], cat_t, t, b, bf)
                dst = X[:, t, h * 512:(h + 1) * 512]
                f = dve(lambda e, dst=dst, b=b: e.tensor_tensor(dst, bank[b][:, :], dst, ALU.add), m)
                banks.give(b, f)
                x_t.append(f)
            split_done(("out2", 2 * h), m)
            split_done(("out2", 2 * h + 1), m)
        x2_t = [[x_t[t], x_t[4 + t]] for t in range(TT)]

        free9 = everything()
        XNT = area(8192, 8, 512)
        xs_ring = Ring([area(12288 + 1024 * i, 1024) for i in range(4)], free9)
        xnT_t, xs_t = norm_to_T("ffn2", x2_t, xs_ring, XNT, free9, keep=(XSH, XSL))

        route = area(26624, 1600)
        L = route[:, 0:144].rearrange("p (t n) -> p t n", t=4)
        RK = route[:, 144:272].rearrange("p (t e) -> p t e", t=4)
        W32 = route[:, 272:400].rearrange("p (t e) -> p t e", t=4)
        SEL = route[:, 400:528].rearrange("p (t e) -> p t e", t=4)
        ro = [528]

        def rt4(*shape):
            n = int(np.prod(shape))
            a = route[:, ro[0]:ro[0] + n]
            ro[0] += n
            if len(shape) == 2:
                a = a.rearrange("p (a b) -> p a b", a=shape[0])
            if len(shape) == 3:
                a = a.rearrange("p (a b c) -> p a b c", a=shape[0], b=shape[1])
            return a

        b, bf = banks.take()
        for t in range(TT):
            for k in range(KD):
                m = pe(lambda e, t=t, k=k, b=b: e.matmul(bank[b][:, t * 36:(t + 1) * 36],
                                                         XNT[:, k, t * 128:(t + 1) * 128], wr[:, k, :],
                                                         start=(k == 0), stop=(k == KD - 1)),
                       xnT_t, bf, misc["wr"], sig=(k == KD - 1))
        lt_ = dve(lambda e, b=b: e.tensor_copy(route[:, 0:144], bank[b][:, 0:144]), m)
        banks.give(b, lt_)
        GL = L[:, :, 0:4]
        iota = con("iota")

        def first_max(src, n, after):
            mx, t, mn, oh = rt4(4), rt4(4, n), rt4(4), rt4(4, n)
            bc = lambda a: a.unsqueeze(2).to_broadcast([128, 4, n])
            a = dve(lambda e: e.tensor_reduce(mx, src, AX, ALU.max), after)
            c = dve(lambda e: e.tensor_tensor(t, src, bc(mx), ALU.is_equal), a)
            io = iota[:, 0:n].unsqueeze(1).to_broadcast([128, 4, n])
            d = dve(lambda e: e.scalar_tensor_tensor(out=t, in0=t, scalar=-100.0, in1=io, op0=ALU.mult, op1=ALU.add), c)
            f = dve(lambda e: e.tensor_reduce(mn, t, AX, ALU.min), d)
            return mx, oh, dve(lambda e: e.tensor_tensor(oh, t, bc(mn), ALU.is_equal), f)

        gm, goh, gt = first_max(GL, 4, lt_)
        ge_, gs, gg = rt4(4, 4), rt4(4), rt4(4)
        a = dve(lambda e: e.tensor_tensor(ge_, GL, gm.unsqueeze(2).to_broadcast([128, 4, 4]), ALU.subtract), gt)
        a = act(lambda e: e.activation(ge_, ge_, ACT.Exp), a)
        a = dve(lambda e: e.tensor_reduce(gs, ge_, AX, ALU.add), a)
        gg_t = dve(lambda e: e.reciprocal(gg, gs), a)
        prod, el = rt4(4, 32), rt4(4, 8)
        for t in range(TT):
            a = dve(lambda e, t=t: e.tensor_tensor(
                prod[:, t, :].rearrange("p (g e) -> p g e", g=4), L[:, t, 4:36].rearrange("p (g e) -> p g e", g=4),
                goh[:, t, :].unsqueeze(2).to_broadcast([128, 4, 8]), ALU.mult), gt)
        for t in range(TT):
            c = dve(lambda e, t=t: e.tensor_reduce(el[:, t, :], prod[:, t, :].rearrange("p (g e) -> p e g", g=4), AX,
                                                   ALU.add), a)
        m1, oh1, o1 = first_max(el, 8, c)
        el2 = rt4(4, 8)
        a = dve(lambda e: e.scalar_tensor_tensor(out=el2, in0=oh1, scalar=-3e38, in1=el, op0=ALU.mult, op1=ALU.add), o1)
        m2, oh2, o2 = first_max(el2, 8, a)
        df, e2_, wa, wb = rt4(4), rt4(4), rt4(4), rt4(4)
        a = dve(lambda e: e.tensor_tensor(df, m2, m1, ALU.subtract), o2)
        x_ = act(lambda e: e.activation(e2_, df, ACT.Exp), a)
        a = dve(lambda e: e.tensor_scalar(wa, e2_, 1.0, None, ALU.add), x_)
        a = dve(lambda e: e.reciprocal(wa, wa), a)
        a = dve(lambda e: e.tensor_tensor(wa, wa, gg, ALU.mult), a, gg_t)
        a = dve(lambda e: e.tensor_tensor(wb, wa, e2_, ALU.mult), a)
        w8, s8, w8b = rt4(4, 8), rt4(4, 8), rt4(4, 8)
        bc8 = lambda v: v.unsqueeze(2).to_broadcast([128, 4, 8])
        a = dve(lambda e: e.tensor_tensor(w8, oh1, bc8(wa), ALU.mult), a)
        c = dve(lambda e: e.tensor_tensor(w8b, oh2, bc8(wb), ALU.mult), a)
        a = dve(lambda e: e.tensor_tensor(w8, w8, w8b, ALU.add), c)
        c = dve(lambda e: e.tensor_tensor(s8, oh1, oh2, ALU.add), a)
        for t in range(TT):
            gb_ = goh[:, t, :].unsqueeze(2).to_broadcast([128, 4, 8])
            dve(lambda e, t=t, gb_=gb_: e.tensor_tensor(
                W32[:, t, :].rearrange("p (g e) -> p g e", g=4), w8[:, t, :].unsqueeze(1).to_broadcast([128, 4, 8]),
                gb_, ALU.mult), c)
            sel_t = dve(lambda e, t=t, gb_=gb_: e.tensor_tensor(
                SEL[:, t, :].rearrange("p (g e) -> p g e", g=4), s8[:, t, :].unsqueeze(1).to_broadcast([128, 4, 8]),
                gb_, ALU.mult), c)
        b, bf = banks.take()
        for t in range(TT):
            for j in range(t + 1):
                m = pe(lambda e, t=t, j=j, b=b: e.matmul(bank[b][:, t * 32:(t + 1) * 32],
                                                         con("tri") if j == t else con("ones"), SEL[:, j, :],
                                                         start=(j == 0), stop=(j == t)), sel_t, bf, sig=(j == t))
        for j in range(TT):
            m = pe(lambda e, j=j, b=b: e.matmul(bank[b][:, 128:160], con("ones"), SEL[:, j, :], start=(j == 0),
                                                stop=(j == 3)), sig=(j == 3))
        flat = lambda v: v.rearrange("p t e -> p (t e)")
        a = dve(lambda e, b=b: e.scalar_tensor_tensor(out=flat(RK), in0=bank[b][:, 0:128], scalar=1.0, in1=flat(SEL),
                                                      op0=ALU.add, op1=ALU.mult), m)
        mc, cm, nx = rt4(1), rt4(7), rt4(1)
        c = dve(lambda e, b=b: e.tensor_reduce(mc, bank[b][:, 128:160], AX, ALU.max), a)
        banks.give(b, c)
        rk_t = dve(lambda e: e.tensor_scalar(flat(RK), flat(RK), -1.0, None, ALU.add), c)
        c = dve(lambda e: e.tensor_scalar(cm, con("thr")[:, 0:7], mc, None, ALU.is_lt), c)
        c = dve(lambda e: e.tensor_reduce(nx, cm, AX, ALU.add), c)
        nx_t = dve(lambda e: e.tensor_copy(nex_i[:, :], nx[0:1, :]), c)

        XET = [area(22528 + 2048 * i, 8, 256) for i in range(2)]
        free10 = everything()
        s_free = [free10]
        Sw_r = Ring([area(9216, 4, 4 * C)], free10)
        ST_r = Ring([v[:, :] for v in ST], free10)
        Y_r = Ring([(YH[i], YL[i]) for i in range(3)], free10)
        sg_r = Ring([area(19456 + 512 * i, 512) for i in range(2)], free10)
        hd_r = Ring([area(20480 + 512 * i, 512) for i in range(2)], free10)
        hT_r = Ring([area(21504 + 512 * i, 512) for i in range(2)], free10)
        xet_free = [free10, free10]
        for i in range(NS, NS_MOE):
            slots.append(mem(i * UNIT, UNIT))
            free_slots.append((i, free10))
        issue()
        gath, swT = {}, {}

        def gather(g):
            Sw, wf = Sw_r.take()
            for t in range(TT):
                ib = iota.unsqueeze(1).to_broadcast([128, 4, C])
                rb = RK[:, t, 4 * g:4 * g + 4].unsqueeze(2).to_broadcast([128, 4, C])
                a = dve(lambda e, t=t, ib=ib, rb=rb: e.tensor_tensor(
                    S[:, t, :].rearrange("p (e s) -> p e s", e=4), ib, rb, ALU.is_equal), rk_t, s_free[0])
            for t in range(TT):
                wb_ = W32[:, t, 4 * g:4 * g + 4].unsqueeze(2).to_broadcast([128, 4, C])
                w_ = pool(lambda e, t=t, wb_=wb_: e.tensor_tensor(
                    Sw[:, t, :].rearrange("p (e s) -> p e s", e=4), S[:, t, :].rearrange("p (e s) -> p e s", e=4),
                    wb_, ALU.mult), a, wf)
            Xe = XET[g % 2]
            out = []
            for kp in range(4):
                b, bf = banks.take()
                for kk in range(2):
                    k = 2 * kp + kk
                    for t in range(TT):
                        for i, v in enumerate((XSH, XSL)):
                            m = pe(lambda e, k=k, kk=kk, t=t, b=b, i=i, v=v: e.matmul(
                                bank[b][:, kk * 256:(kk + 1) * 256], v[:, t, k * 128:(k + 1) * 128], S[:, t, :],
                                start=(t == 0 and i == 0), stop=(t == 3 and i == 1)), a, bf, xs_t,
                                sig=(t == 3 and i == 1))
                for kk in range(2):
                    k = 2 * kp + kk
                    d = act(lambda e, k=k, kk=kk, b=b: e.activation(Xe[:, k, :], bank[b][:, kk * 256:(kk + 1) * 256],
                                                                    ACT.Copy, scale=col("ffn2", k)), m, xet_free[g % 2])
                banks.give(b, d)
                out.append(d)
            for q in range(2):
                b, bf = banks.take()
                for t in range(TT):
                    m2_ = pe(lambda e, t=t, q=q, b=b: e.transpose(bank[b][:, t * 128:(t + 1) * 128],
                                                                  Sw[:, t, q * 128:(q + 1) * 128], ident),
                             w_, bf, sig=(t == 3))
                T_, tf = ST_r.take()
                wc = stat()
                c = dve(lambda e, wc=wc, b=b: e.tensor_reduce(wc, bank[b][:, :], AX, ALU.add), m2_)
                d = dve(lambda e, T_=T_, b=b: e.tensor_scalar(T_, bank[b][:, :], 0.0, None, ALU.is_gt), m2_, tf)
                banks.give(b, d)
                swT[2 * g + q] = (T_, wc, d)
            s_free[0] = [m, w_]
            Sw_r.give(Sw, m2_)
            gath[g] = out

        hid = {}

        def hidden(p):
            Xe, xt_ = XET[(p // 2) % 2], gath[p // 2]
            o = (p % 2) * 2 * C
            ms = []
            for w in (1, 3):
                b, bf = banks.take()
                for kh in range(2):
                    us = [W(("e", w, 2 * p + s, kh), 4) for s in range(2)]
                    for k in range(4):
                        for s in range(2):
                            m = pe(lambda e, s=s, k=k, kh=kh, b=b, us=us: e.matmul(
                                bank[b][64 * s:64 * s + 64, :], Xe[:, 4 * kh + k, o + C * s:o + C * s + C],
                                us[s][0][:, k, :], start=(kh == 0 and k == 0), stop=(kh == 1 and k == 3)),
                                us[s][1], bf, xt_, sig=(k == 3 and s == 1))
                    for s in range(2):
                        Wdone(("e", w, 2 * p + s, kh), m)
                ms.append((b, m))
            if p % 2:
                xet_free[(p // 2) % 2] = m
            sg, sf = sg_r.take()
            hd, hf = hd_r.take()
            a = act(lambda e: e.activation(sg, bank[ms[0][0]][:, :], ACT.Silu), ms[0][1], sf)
            banks.give(ms[0][0], a)
            d = dve(lambda e: e.tensor_tensor(hd, sg, bank[ms[1][0]][:, :], ALU.mult), a, ms[1][1], hf)
            banks.give(ms[1][0], d)
            sg_r.give(sg, d)
            hid[p] = (hd, d)

        def turn(p):
            hd, d = hid[p]
            b, bf = banks.take()
            for k in range(4):
                m = pe(lambda e, k=k: e.transpose(bank[b][:, k * 128:(k + 1) * 128], hd[:, k * 128:(k + 1) * 128], ident),
                       d, bf, sig=(k == 3))
            hd_r.give(hd, m)
            hT, hf = hT_r.take()
            ev = dve(lambda e: e.tensor_copy(hT, bank[b][:, :]), m, hf)
            banks.give(b, ev)
            hid[p] = (hT, ev)

        ys = {}

        def second(p):
            hT, ev = hid[p]
            bs = [banks.take() for _ in range(2)]
            for kh in range(2):
                us = [W(("e", 2, 2 * p + s, kh), 2) for s in range(2)]
                for k in range(2):
                    for h in range(2):
                        for s in range(2):
                            kk = 2 * kh + k
                            m = pe(lambda e, s=s, k=k, kk=kk, h=h, us=us: e.matmul(
                                bank[bs[h][0]][64 * s:64 * s + 64, :], hT[:, kk * 128 + 64 * s:kk * 128 + 64 * s + 64],
                                us[s][0][:, k, h * 512:(h + 1) * 512], start=(kk == 0), stop=(kk == 3)),
                                us[s][1], bs[h][1], ev, sig=(s == 1 and h == 1 and k == 1))
                for s in range(2):
                    Wdone(("e", 2, 2 * p + s, kh), m)
            hT_r.give(hT, m)
            Y, yf = Y_r.take()
            wc, wt_ = swT[p][1:]
            ev = []
            for h in range(2):
                place = (slice(None), slice(h * 512, (h + 1) * 512))
                a = act(lambda e, h=h, place=place: e.activation(Y[0][place], bank[bs[h][0]][:, :], ACT.Copy, scale=wc),
                        m, yf, wt_)
                ev.append(dve(lambda e, h=h, place=place: e.scalar_tensor_tensor(
                    out=Y[1][place], in0=bank[bs[h][0]][:, :], scalar=wc, in1=Y[0][place], op0=ALU.mult,
                    op1=ALU.subtract), a))
                banks.give(bs[h][0], ev[h])
            ys[p] = (Y, ev)

        acc_t = {(t, h): [xs_t[t]] for t in range(TT) for h in range(2)}

        def scatter(ps):
            for t in range(TT):
                for h in range(2):
                    b, bf = banks.take()
                    for i, (p, q) in enumerate([(p, q) for p in ps for q in range(2)]):
                        last = i == 2 * len(ps) - 1
                        m = pe(lambda e, i=i, p=p, q=q, t=t, h=h, b=b, last=last: e.matmul(
                            bank[b][:, :], swT[p][0][:, t * 128:(t + 1) * 128], ys[p][0][q][:, h * 512:(h + 1) * 512],
                            start=(i == 0), stop=last), swT[p][2], ys[p][1], bf, sig=last)
                    dst = X[:, t, h * 512:(h + 1) * 512]
                    f = dve(lambda e, dst=dst, b=b: e.tensor_tensor(dst, bank[b][:, :], dst, ALU.add), m, acc_t[t, h])
                    banks.give(b, f)
                    acc_t[t, h] = f
            for p in ps:
                ST_r.give(swT[p][0], m)
                Y_r.give(ys[p][0], m)

        gather(0)
        for p in range(NPAIR + 1):
            if p < NPAIR:
                hidden(p)
                if p % 2 == 0 and p // 2 + 1 < NE // 4:
                    gather(p // 2 + 1)
            if p >= 1:
                second(p - 1)
                if p % 2 and p >= 3:
                    scatter([p - 3, p - 2])
            if p < NPAIR:
                turn(p)
        scatter([NPAIR - 2, NPAIR - 1])

        with nc.Block() as block:
            @block.sync
            def _(e):
                sp.run(e)

            @block.gpsimd
            def _(e):
                pool.run(e)

            @block.scalar
            def _(e):
                act.run(e)

            @block.vector
            def _(e):
                dve.run(e)

            @block.tensor
            def _(e):
                pe.run(e)
        for q in (pe, act, dve, pool, sp):
            q.items.clear()

        overflow(nc, ctx, sem, dict(nex_i=nex_i, w1=w1_d, w3=w3_d, w2=w2_d, area=area, X=X, XS=(XSH, XSL), S=OS, RK=RK,
                                    W32=W32, con=con, col=col, bank=bank, ident=ident))

        everything_done = everything()
        for q in engines:
            for s_, v_ in everything_done:
                q.waited[s_.name] = v_
        banks = Ring(list(range(8)))
        hT2 = area(4096, 8, 512)
        xs_ring = Ring([area(8192 + 1024 * i, 1024) for i in range(2)])
        pT = area(10240, 2, 512)
        PN = area(11264, 4, 1024)
        tmp_ring = Ring([area(15360 + 1024 * i, 1024) for i in range(3)])
        load(pool, "pT", pT, pT_d)
        w, wt = W(("ple", 0), 2)
        pn_t = []
        for t in range(TT):
            hs = []
            for h in range(2):
                b, bf = banks.take()
                for k in range(2):
                    m = pe(lambda e, k=k, t=t, h=h, b=b: e.matmul(
                        bank[b][:, :], pT[:, k, t * 128:(t + 1) * 128], w[:, k, h * 512:(h + 1) * 512],
                        start=(k == 0), stop=(k == 1)), wt, misc["pT"], bf, sig=(k == 1))
                hs.append((bank[b][:, :], m, b))
            ss, s1 = stat(2), stat()
            q = sumsq(lambda i, hs=hs: hs[i][0], ss, hs[0][1], hs[1][1])
            a = dve(lambda e, s1=s1, ss=ss: e.tensor_tensor(s1, ss[:, 0:1], ss[:, 1:2], ALU.add), q)
            r, rt = rstd_of(s1, 1, D, a)
            for h in range(2):
                z = dve(lambda e, h=h, t=t, hs=hs, r=r: e.scalar_tensor_tensor(
                    out=PN[:, t, h * 512:(h + 1) * 512], in0=hs[h][0], scalar=r,
                    in1=rowb[:, h * 512:(h + 1) * 512], op0=ALU.mult, op1=ALU.mult), rt,
                    misc["row_ple"])
                banks.give(hs[h][2], z)
            pn_t.append(z)
        hT_t = norm_to_T("plg", [None] * TT, xs_ring, hT2, None)
        d_out = sem("d_out")
        fin = {}
        nout = 0
        for h in range(2):
            for t in range(TT):
                b, bf = banks.take()
                m = gemm_tok([("plg", 2 * h), ("plg", 2 * h + 1)], hT2, hT_t, t, b, bf)
                tmp, tf = tmp_ring.take()
                s = act(lambda e, b=b, tmp=tmp: e.activation(tmp[:, 0:512], bank[b][:, :], ACT.Sigmoid), m, tf)
                banks.give(b, s)
                z = pool(lambda e, h=h, t=t, tmp=tmp: e.tensor_tensor(
                    tmp[:, 0:512], tmp[:, 0:512], PN[:, t, h * 512:(h + 1) * 512], ALU.mult), s, pn_t[t])
                f = dve(lambda e, h=h, t=t, tmp=tmp: e.tensor_tensor(
                    tmp[:, 512:1024], tmp[:, 0:512], X[:, t, h * 512:(h + 1) * 512], ALU.add), z)
                nout += 1
                od = sp.dma(out_d[t * 128:(t + 1) * 128, h * 512:(h + 1) * 512], tmp[:, 512:1024],
                            sem(f"d_out{nout}"), 1, f)
                tmp_ring.give(tmp, od)
                fin[t, h] = od
        sp.wait(list(fin.values()))

        with nc.Block() as block:
            @block.sync
            def _(e):
                sp.run(e)

            @block.gpsimd
            def _(e):
                pool.run(e)

            @block.scalar
            def _(e):
                act.run(e)

            @block.vector
            def _(e):
                dve.run(e)

            @block.tensor
            def _(e):
                pe.run(e)


def overflow(nc, ctx, sem, v):
    con, bank, ident, X, XS = v["con"], v["bank"], v["ident"], v["X"], v["XS"]
    reg = v["area"]
    iota = con("iota")

    wA, wB, wC = (reg(8192 + 4096 * i, 4096) for i in range(3))
    oh = reg(20480, 32)
    pr = reg(20512, 4, 32)
    rc, wc = reg(20640, 4), reg(20644, 4)
    cnt = reg(20648, 1)
    rnd = reg(20649, 1)
    S, Sw = v["S"][:, :, :], reg(20992, 4, C)
    SwT, sg, hd = reg(21248, 512), reg(21760, 512), reg(22272, 512)
    hT = reg(22784, 4, C)
    Y = reg(23040, 1024)
    Xe = reg(24064, 8, C)
    s_d, s_p, s_a, s_v, s_i = sem("o_d"), sem("o_p"), sem("o_a"), sem("o_v"), sem("o_i")

    with nc.Block() as block:
        @block.vector
        def _(e):
            e.memset(rnd, float(C)).then_inc(s_i, 1)
            e.wait_ge(s_i, 1)

    n = nc.values_load(v["nex_i"][0:1, 0:1], min_val=0, max_val=NTOK // C - 1)
    with nc.If(n > 0):
        with nc.Fori(0, n):
            with nc.Block() as block:
                @block.vector
                def _(e):
                    e.memset(cnt, 0.0).then_inc(s_v, 1)
                    e.wait_ge(s_v, 1)
            nc.all_engine_barrier()
            nc.gpsimd.sem_clear(s_v)
            nc.all_engine_barrier()
            with nc.Fori(0, NE) as ei:
                pe, act, dve, sp = Queue(s_p), Queue(s_a), Queue(s_v), Queue(s_d)
                for i, (w, src, k) in enumerate(((wA, v["w1"], 8), (wB, v["w3"], 8), (wC, v["w2"], 4))):
                    s = src[bass.ds(ei, 1), :, :].rearrange("a (k p) n -> p (a k) n", p=128)
                    d_t = sp.dma(w.rearrange("p (k n) -> p k n", k=k), s, s_d, i + 1)
                a = dve(lambda e: e.tensor_scalar(oh, iota[:, 0:32], cnt, None, ALU.is_equal))
                a = dve(lambda e: e.tensor_scalar(cnt, cnt, 1.0, None, ALU.add), a)
                ohb = oh.unsqueeze(1).to_broadcast([128, 4, 32])
                for src, dst in ((v["RK"], rc), (v["W32"], wc)):
                    a = dve(lambda e, src=src: e.tensor_tensor(pr, src, ohb, ALU.mult), a)
                    a = dve(lambda e, dst=dst: e.tensor_reduce(dst, pr, AX, ALU.add), a)
                a = dve(lambda e: e.tensor_scalar(rc, rc, rnd, None, ALU.subtract), a)
                ib = iota.unsqueeze(1).to_broadcast([128, 4, C])
                a = dve(lambda e: e.tensor_tensor(S, ib, rc.unsqueeze(2).to_broadcast([128, 4, C]), ALU.is_equal), a)
                sw = dve(lambda e: e.tensor_tensor(Sw, S, wc.unsqueeze(2).to_broadcast([128, 4, C]), ALU.mult), a)
                for k in range(KD):
                    for i, (t, x) in enumerate([(t, x) for t in range(TT) for x in XS]):
                        m = pe(lambda e, k=k, t=t, i=i, x=x: e.matmul(
                            bank[0][:, k * C:(k + 1) * C], x[:, t, k * 128:(k + 1) * 128], S[:, t, :],
                            start=(i == 0), stop=(i == 7)), a, sig=(i == 7))
                for t in range(TT):
                    m2 = pe(lambda e, t=t: e.transpose(bank[1][0:C, t * 128:(t + 1) * 128], Sw[:, t, :], ident),
                            sw, sig=(t == 3))
                for k in range(KD):
                    x = act(lambda e, k=k: e.activation(Xe[:, k, :], bank[0][:, k * C:(k + 1) * C], ACT.Copy,
                                                        scale=v["col"]("ffn2", k)), m)
                x2 = act(lambda e: e.activation(SwT[0:C, :], bank[1][0:C, :], ACT.Copy), m2)
                for w, b in ((wA, 2), (wB, 3)):
                    for k in range(KD):
                        m = pe(lambda e, w=w, b=b, k=k: e.matmul(bank[b][0:C, :], Xe[:, k, :],
                                                                 w[:, k * 512:(k + 1) * 512], start=(k == 0),
                                                                 stop=(k == 7)), x, d_t, sig=(k == 7))
                g = act(lambda e: e.activation(sg[0:C, :], bank[2][0:C, :], ACT.Silu), m)
                h = dve(lambda e: e.tensor_tensor(hd[0:C, :], sg[0:C, :], bank[3][0:C, :], ALU.mult), g)
                for k in range(4):
                    m = pe(lambda e, k=k: e.transpose(bank[4][:, k * C:(k + 1) * C], hd[0:C, k * 128:(k + 1) * 128],
                                                      ident[0:C, 0:C]), h, sig=(k == 3))
                c = dve(lambda e: e.tensor_copy(hT.rearrange("p a b -> p (a b)"), bank[4][:, 0:4 * C]), m)
                for hh in range(2):
                    for k in range(4):
                        m = pe(lambda e, hh=hh, k=k: e.matmul(
                            bank[5 + hh][0:C, :], hT[:, k, :], wC[:, k * 1024 + hh * 512:k * 1024 + hh * 512 + 512],
                            start=(k == 0), stop=(k == 3)), c, sig=(k == 3))
                    y = dve(lambda e, hh=hh: e.tensor_copy(Y[0:C, hh * 512:(hh + 1) * 512], bank[5 + hh][0:C, :]), m)
                f = None
                for t in range(TT):
                    for hh in range(2):
                        m = pe(lambda e, t=t, hh=hh: e.matmul(bank[7][:, :], SwT[0:C, t * 128:(t + 1) * 128],
                                                              Y[0:C, hh * 512:(hh + 1) * 512], start=True, stop=True),
                               y, x2, f)
                        dst = X[:, t, hh * 512:(hh + 1) * 512]
                        f = dve(lambda e, dst=dst: e.tensor_tensor(dst, bank[7][:, :], dst, ALU.add), m)
                dve.wait(f)
                with nc.Block() as block:
                    @block.sync
                    def _(e):
                        sp.run(e)

                    @block.scalar
                    def _(e):
                        act.run(e)

                    @block.vector
                    def _(e):
                        dve.run(e)

                    @block.tensor
                    def _(e):
                        pe.run(e)
                nc.all_engine_barrier()
                for s in (s_d, s_p, s_a, s_v):
                    nc.gpsimd.sem_clear(s)
                nc.all_engine_barrier()
            with nc.Block() as block:
                @block.vector
                def _(e):
                    e.tensor_scalar(rnd, rnd, float(C), None, ALU.add).then_inc(s_v, 1)
                    e.wait_ge(s_v, 1)
            nc.all_engine_barrier()
            nc.gpsimd.sem_clear(s_v)
            nc.all_engine_barrier()


def _by_cols(w, width=256):
    k, n = w.shape
    return w.reshape(k // 128, 128, n // width, width).transpose(2, 1, 0, 3).reshape(n // width, 128, -1)


def _by_half(w):
    n = w.shape[1]
    return w.reshape(2, 4, 128, n // 512, 512).transpose(3, 0, 2, 1, 4).reshape(n // 256, 128, -1)


def _by_rows(w):
    return w.reshape(-1, 2, 128, 1024).transpose(0, 2, 1, 3).reshape(-1, 128, 2048)


def _tiles(v):
    return v.reshape(-1, 128).T


def _layout(i):
    w_in, w_up = _by_cols(i["w_in"][0]), _by_cols(i["w_up"][0])
    ao, po = _by_cols(i["w_attn_out"][0], 512), _by_cols(i["w_pool_out"][0], 512)
    dn = _by_rows(i["w_down"][0])
    in_half = _by_half(i["w_in"][0])
    seq = [in_half[n] if n in (4, 5) else w_in[n] for n in range(8)]
    for n in range(4):
        if n % 2 == 0:
            seq += [ao[n // 2], po[n // 2]]
        seq += [w_in[8 + n], w_in[12 + n]]
    seq += list(_by_cols(i["w_o"][0]))
    for us, ds in ffn_order():
        for u in us:
            seq += [w_up[u], w_up[11 + u]]
        seq += [dn[d] for d in ds]
    in2, in2_half = _by_cols(i["w_in_2"][0]), _by_half(i["w_in_2"][0])
    seq += [in2_half[n] if n < 10 else in2[n] for n in range(12)] + list(_by_half(i["w_out_2"][0]))
    seq += list(_by_rows(i["w_ple_2"][0])) + list(_by_cols(i["w_plg_2"][0]))

    cols = np.concatenate([_tiles(i[n].reshape(-1)) for n in (
        "norm_mix_pre", "norm_ffn_pre", "g_mix_2", "g_ffn_2", "g_plg_2", "b_gate", "pool_scale", "conv_w", "conv_b",
        "g_sub_2")], axis=1)
    rows = np.concatenate([i[n].reshape(-1) for n in (
        "norm_mix_post", "norm_ffn_post", "g_ple_2", "g_qa_2", "g_ka_2", "g_qb_2", "g_kb_2", "lam_q1_2", "lam_k1_2",
        "lam_q2_2", "lam_k2_2")])[None, :]

    p = np.arange(128)
    dist = p[:, None] + 384 - np.arange(512)[None, :]
    tb = i["rel_bias"][0][:, np.clip(dist, -256, 256) + 256]
    tb = np.where((p[:, None] < 64) & (np.arange(512)[None, :] >= 448), np.float32(NEG), tb).transpose(1, 0, 2)

    r, c = p // 16, p % 16
    kr, kc = np.arange(256) // 32, np.arange(256) % 32
    nb = np.empty((4, 128, 4, 3, 256), np.float32)
    for jt, (q0, k0) in enumerate(((0, 0), (16, 8), (48, 32))):
        qc, kcol = q0 + c, k0 + kc
        cs = np.clip(qc - 8, 0, 48)
        ok = (kcol[None, :] >= cs[:, None]) & (kcol[None, :] < cs[:, None] + 16)
        off = np.clip(kcol[None, :] - qc[:, None] + 15, 0, 30)
        ro = kr[None, :] - r[:, None] + 7
        t = np.where(ok, i["rpb_2"][0][:, ro, off], np.float32(NEG))
        nb[:, :, :, jt, :] = t.reshape(4, 4, 128, 256).transpose(0, 2, 1, 3)

    t = np.arange(NTOK, dtype=np.float32)
    inv = (np.float32(10000.0) ** (-np.arange(0, 64, 2, dtype=np.float32) / np.float32(64))).astype(np.float32)
    ang = (t[:, None] * inv[None, :]).astype(np.float32)
    by_tok = lambda a: a.reshape(4, 128, 32).transpose(1, 0, 2).reshape(128, 128)
    cnt = np.stack([1.0 / np.minimum(np.arange(16) + 1, 2 << g) for g in range(4)]).reshape(1, 64)
    one = np.ones((128, 1))
    cst = np.concatenate([np.eye(128), np.triu(np.ones((128, 128)), 1), np.ones((128, 128)),
                          one * np.arange(64)[None, :], one * (C * (1 + np.arange(8)))[None, :], one * cnt,
                          by_tok(np.cos(ang)), by_tok(np.sin(ang))], axis=1).astype(np.float32)
    wr = np.concatenate([i["w_rg_2"][0], i["w_re_2"][0]], axis=1).reshape(8, 128, 36).transpose(1, 0, 2)
    return {
        "x": i["x"][0], "wd": np.stack(seq), "w1": i["w1_2"][0], "w3": i["w3_2"][0], "w2": i["w2_2"][0],
        "cols": cols, "rows": rows, "cst": cst, "wr": wr, "wpg": i["w_pool_group"][0].transpose(1, 0, 2),
        "pT": i["p_2"][0, 0].T.reshape(2, 128, 512).transpose(1, 0, 2), "tb": tb, "nb": nb.reshape(4, 128, 3072),
    }


def kernel(**inputs):
    import concourse.bacc as bacc
    from concourse.bass_utils import run_bass_kernel_spmd

    nc = bacc.Bacc("TRN2", target_bir_lowering=False, num_devices=1)
    arrays, args = {}, []
    for name, a in _layout({k: np.asarray(v) for k, v in inputs.items()}).items():
        a = np.ascontiguousarray(a)
        arrays[f"in_{name}"] = a
        args.append(nc.dram_tensor(f"in_{name}", a.shape, mybir.dt.from_np(a.dtype), kind="ExternalInput").ap())
    out = nc.dram_tensor("out_0", (NTOK, D), F32, kind="ExternalOutput").ap()
    build(nc, *args, out)
    r = run_bass_kernel_spmd(nc, [arrays], core_ids=[0])
    return r.results[0]["out_0"].reshape(1, NTOK, D)
```

```python
from collections import deque
from contextlib import ExitStack

import numpy as np

import concourse.bass as bass
from concourse import mybir

F32 = mybir.dt.float32
F32R = mybir.dt.float32r
I32 = mybir.dt.int32
ACT = mybir.ActivationFunctionType
ALU = mybir.AluOpType
AX = mybir.AxisListType.X

NTOK, D = 512, 1024
TT, KD = 4, 8
UNIT = 2048
NS = 4
NSPLIT = 3
M_SZ = 42560
SPLIT0 = NS * UNIT
HT0 = SPLIT0 + NSPLIT * 2 * UNIT
R0 = HT0 + 8192
A0 = 14336
NATILE = 6
NS_MOE = 7
NS_ONCE = 5
NE = 32
NPAIR = NE // 2
C = 64
EPS = 1e-6
NEG = -1e30

COLS = {}
_o = 0
for _n, _w in (("mix_pre", 8), ("ffn_pre", 8), ("mix2", 8), ("ffn2", 8), ("plg", 8), ("b_gate", 16),
               ("pool_scale", 4), ("conv_w", 132), ("conv_b", 44), ("g_sub", 1)):
    COLS[_n] = (_o, _w)
    _o += _w
NCOLS = _o
ROWS = {}
_o = 0
for _n, _w in (("qa", 64), ("ka", 64), ("qb", 32),
               ("kb", 32), ("lq1", 64), ("lk1", 64), ("lq2", 64), ("lk2", 64)):
    ROWS[_n] = (_o, _w)
    _o += _w
NROWS = _o
BIG = {"mix_post": 0, "ffn_post": 1024, "ple": 2048}
CST = {}
_o = 0
for _n, _w in (("ident", 128), ("tri", 128), ("ones", 128), ("iota", 64), ("thr", 8), ("cnt", 64),
               ("cos", 128), ("sin", 128)):
    CST[_n] = (_o, _w)
    _o += _w
NCST = _o


def ffn_order():
    steps = [([0, 1, 2], [0, 1])]
    for n in range(1, 5):
        steps.append(([2 * n + 1, 2 * n + 2], [2 * n, 2 * n + 1]))
    steps[-1][1].append(10)
    return steps


class Queue:

    def __init__(self, sem):
        self.sem, self.n, self.items, self.waited = sem, 0, [], {}

    def wait(self, *after):
        for t in after:
            if t is None:
                continue
            if isinstance(t, list):
                self.wait(*t)
                continue
            sem, v = t
            if self.waited.get(sem.name, 0) < v:
                self.waited[sem.name] = v
                self.items.append(lambda e, sem=sem, v=v: e.wait_ge(sem, v))

    def __call__(self, fn, *after, sig=True):
        self.wait(*after)
        if not sig:
            self.items.append(fn)
            return None
        self.n += 1
        self.items.append(lambda e: fn(e).then_inc(self.sem, 1))
        return (self.sem, self.n)

    def dma(self, out, in_, sem, n, *after):
        self.wait(*after)
        self.items.append(lambda e: e.dma_start(out, in_).then_inc(sem, 16))
        return (sem, 16 * n)

    def run(self, e):
        for f in self.items:
            f(e)


class Ring:

    def __init__(self, bufs, after=None):
        self.free = deque((b, after) for b in bufs)

    def take(self):
        return self.free.popleft()

    def give(self, b, tok):
        self.free.append((b, tok))


def build(nc, x_d, wd, w1_d, w3_d, w2_d, cols_d, rows_d, cst_d, wr_d, wpg_d, pT_d, tb_d, nb_d, out_d):
    with ExitStack() as ctx:
        def sb(name, shape, dt=F32):
            return ctx.enter_context(nc.sbuf_tensor(name, shape, dt))

        def sem(name):
            return ctx.enter_context(nc.semaphore(name))

        X = sb("X", [128, TT, D])
        cols = sb("cols", [128, NCOLS])
        rows = sb("rows", [128, NROWS])
        rowb = sb("rowb", [128, D])
        cst = sb("cst", [128, NCST])
        wr = sb("wr", [128, KD, 36])
        wpg = sb("wpg", [128, 4, 128])
        st = sb("st", [128, 1760])
        nex_i = sb("nex_i", [1, 1], I32)
        junk = sb("junk", [128, 4, D // 2], mybir.dt.bfloat16)

        def overlay(name, o, *shape, dt=F32R):
            with ExitStack() as s:
                if o:
                    s.enter_context(nc.sbuf_tensor(name + "_before", [128, o], F32))
                return s.enter_context(nc.sbuf_tensor(name, [128, *shape], dt))

        HTH, HTL = overlay("HTH", HT0, KD, NTOK), overlay("HTL", HT0 + 4096, KD, NTOK)
        w_hi = [overlay(f"w_hi{i}", SPLIT0 + 2 * UNIT * i, UNIT) for i in range(NSPLIT)]
        w_lo = [overlay(f"w_lo{i}", SPLIT0 + 2 * UNIT * i + UNIT, UNIT) for i in range(NSPLIT)]
        AH, AL = overlay("AH", R0, NATILE, NTOK), overlay("AL", R0 + NATILE * NTOK, NATILE, NTOK)
        XSH, XSL = overlay("XSH", A0, TT, D), overlay("XSL", A0 + 4096, TT, D)
        S = overlay("S", A0 + 8192, TT, 4 * C)
        ST = [overlay(f"ST{i}", A0 + 10240 + 512 * i, NTOK) for i in range(6)]
        YH, YL = ([overlay(f"{n}{i}", A0 + 13312 + o + 2048 * i, D) for i in range(3)] for n, o in (("YH", 0), ("YL", 1024)))
        PH, PL = ([overlay(f"{n}{i}", A0 + 14336 + o + 4096 * i, UNIT) for i in range(2)]
                  for n, o in (("PH", 0), ("PL", UNIT)))
        OS = overlay("OS", A0 + 20704, TT, C)
        YAH, YAL = overlay("YAH", R0, 4, NTOK), overlay("YAL", R0 + 8256, 4, NTOK)
        YBH, YBL = overlay("YBH", R0 + 6144, 4, NTOK + 16), overlay("YBL", R0 + 10304, 4, NTOK)
        M = sb("M", [128, M_SZ])
        bank = [ctx.enter_context(nc.psum_tensor(f"bank{i}", [128, 512], F32)) for i in range(8)]

        def col(name, i=0, n=1):
            o = COLS[name][0]
            return cols[:, o + i:o + i + n]

        def row(name):
            o, w = ROWS[name]
            return rows[:, o:o + w]

        def con(name):
            o, w = CST[name]
            return cst[:, o:o + w]

        ident = con("ident")

        def mem(o, *shape):
            n = int(np.prod(shape))
            assert o + n <= M_SZ, (o, shape)
            v = M[:, o:o + n]
            if len(shape) == 2:
                v = v.rearrange("p (a b) -> p a b", a=shape[0])
            if len(shape) == 3:
                v = v.rearrange("p (a b c) -> p a b c", a=shape[0], b=shape[1])
            return v

        def region(o, *shape):
            return mem(R0 + o, *shape)

        def area(o, *shape):
            return mem(A0 + o, *shape)

        s_pe, s_act, s_dve, s_pool, s_sp = (sem(n) for n in ("s_pe", "s_act", "s_dve", "s_pool", "s_sp"))
        pe, act, dve, pool, sp = Queue(s_pe), Queue(s_act), Queue(s_dve), Queue(s_pool), Queue(s_sp)
        engines = (pe, act, dve, pool)

        def everything():
            return [(q.sem, q.n) for q in engines if q.n]

        misc = {}

        def load(q, name, out, in_, *after):
            misc[name] = q.dma(out, in_, sem("d_" + name), 1, *after)
            return misc[name]

        banks = Ring(list(range(8)))

        units = []
        where = {}

        def plan(key, src):
            where[key] = len(units)
            units.append(src)

        nd = [0]

        def dense(key):
            plan(key, wd[nd[0], :, :])
            nd[0] += 1

        for key in [("in", i) for i in range(8)]:
            dense(key)
        for i in range(4):
            dense(("ap", i))
            dense(("ga", i))
            dense(("gb", i))
        for i in range(4):
            dense(("wo", i))
        for n, (us, ds) in enumerate(ffn_order()):
            for u in us:
                dense(("uv", u))
                dense(("ug", u))
            for d in ds:
                dense(("dn", d))
        for i in range(12):
            dense(("in2", i))
        for i in range(4):
            dense(("out2", i))
        to_split = deque(k for k in where if k[0] not in ("ple", "plg"))

        def expert(w, e, kh):
            if w == 2:
                src = w2_d[e, kh * 256:(kh + 1) * 256, :].rearrange("(k p) n -> p k n", p=128)
            else:
                src = (w1_d if w == 1 else w3_d)[e, kh * 512:(kh + 1) * 512, :].rearrange("(k p) n -> p k n", p=128)
            plan(("e", w, e, kh), src)

        for p in range(NPAIR + 1):
            for w in (1, 3):
                if p < NPAIR:
                    for kh in range(2):
                        for e in (2 * p, 2 * p + 1):
                            expert(w, e, kh)
            if p == NPAIR:
                dense(("ple", 0))
            if p >= 1:
                for kh in range(2):
                    for e in (2 * p - 2, 2 * p - 1):
                        expert(2, e, kh)
        for i in range(4):
            dense(("plg", i))

        slots = [M[:, i * UNIT:(i + 1) * UNIT] for i in range(NS)]
        slot_sem = [sem(f"d_w{i}") for i in range(NS_MOE + NS_ONCE)]
        slot_n = [0] * (NS_MOE + NS_ONCE)
        slot_of = {}
        ready = {}
        free_slots = deque((i, None) for i in range(NS))
        issued = [0]
        split_free = deque((i, None) for i in range(NSPLIT))
        split_of = {}
        resting = {}
        split_limit = [8]

        def issue():
            while free_slots and issued[0] < len(units):
                i, tok = free_slots.popleft()
                n = issued[0]
                src = units[n]
                dst = slots[i]
                if len(src.shape) == 3:
                    dst = dst.rearrange("p (k n) -> p k n", k=src.shape[1])
                slot_n[i] += 1
                slot_of[n] = i
                ready[n] = sp.dma(dst, src, slot_sem[i], slot_n[i], tok)
                issued[0] += 1

        def W(key, k):
            n = where[key]
            return slots[slot_of[n]].rearrange("p (k n) -> p k n", k=k), ready[n]

        def Wdone(key, tok):
            if slot_of[where[key]] < NS_MOE:
                free_slots.append((slot_of[where[key]], tok))
            issue()
            ahead()

        def ahead():
            while split_free and to_split and split_limit[0] and where[to_split[0]] < issued[0]:
                key = to_split.popleft()
                split_limit[0] -= 1
                i, tok = split_free.popleft()
                n = where[key]
                raw = slots[slot_of[n]]
                a = act(lambda e, i=i, raw=raw: e.activation(w_hi[i][:, :], raw, ACT.Copy), ready[n], tok)
                d = dve(lambda e, i=i, raw=raw: e.tensor_tensor(w_lo[i][:, :], raw, w_hi[i][:, :], ALU.subtract), a)
                split_of[key] = (i, d)
                free_slots.append((slot_of[n], d))
                issue()

        def split_W(key, k):
            i, tok = split_of[key]
            return (*(v[i][:, :].rearrange("p (k n) -> p k n", k=k) for v in (w_hi, w_lo)), tok)

        def split_done(key, tok):
            split_free.append((split_of[key][0], tok))
            ahead()

        def allow(n, order, after=None):
            split_limit[0] += n
            resting.update(split_free)
            split_free.clear()
            split_free.extend((i, [resting.pop(i), after]) for i in order)
            ahead()

        for t in range(TT):
            load(sp, f"x{t}", X[:, t, :], x_d[t * 128:(t + 1) * 128, :])
            if t == 1:
                load(sp, "cst", cst[:, :], cst_d)
                load(sp, "cols", cols[:, :], cols_d)
        issue()

        o_st = [0]

        def stat(n=1):
            a = st[:, o_st[0]:o_st[0] + n]
            o_st[0] += n
            assert o_st[0] <= 1760
            return a

        def rstd_of(ss, n, div, *after):
            ms, sq, r = stat(n), stat(n), stat(n)
            a = dve(lambda e: e.tensor_scalar(ms, ss, 1.0 / div, EPS, ALU.mult, ALU.add), *after)
            b = act(lambda e: e.activation(sq, ms, ACT.Sqrt), a)
            return r, dve(lambda e: e.reciprocal(r, sq), b)

        junk_r = Ring([junk[:, i, :] for i in range(4)])

        def sumsq(src, ss, *after):
            out = []
            for i in range(ss.shape[1]):
                j, jf = junk_r.take()
                a = act(lambda e, i=i, j=j: e.activation(j, src(i), ACT.Square, accum_out=ss[:, i:i + 1]), jf, *after)
                junk_r.give(j, a)
                out.append(a)
            return out

        def staggered(chains, gap=3):
            chains, n = list(chains), 0
            live = []
            while chains or live:
                if chains and n % gap == 0:
                    live.append(chains.pop(0))
                live = [c for c in live if next(c, 0) is None]
                n += 1

        def rstd_stages(src, div, *after):
            ss2, ss, ms, sq, r = stat(2), stat(), stat(), stat(), stat()
            q = sumsq(src, ss2, *after)
            yield
            a = dve(lambda e: e.tensor_tensor(ss, ss2[:, 0:1], ss2[:, 1:2], ALU.add), q)
            a = dve(lambda e: e.tensor_scalar(ms, ss, 1.0 / div, EPS, ALU.mult, ALU.add), a)
            yield
            a = act(lambda e: e.activation(sq, ms, ACT.Sqrt), a)
            yield
            return r, dve(lambda e: e.reciprocal(r, sq), a)

        def norm_stages(t, gname, xt, xs, after, out, dst=None, y_r=None, keep=None, kept=None):
            r, rt = yield from rstd_stages(lambda i: X[:, t, i * 512:(i + 1) * 512], D, xt)
            buf, free = xs.take()
            a = dve(lambda e: e.tensor_scalar(buf, X[:, t, :], r, None, ALU.mult), rt, free)
            yield
            ms, bs, ds, ys = [], [], [], []
            for h in range(2):
                b, bf = banks.take()
                bs.append(b)
                for k in range(4):
                    m = pe(lambda e, k=k, b=b, h=h: e.transpose(
                        bank[b][:, k * 128:(k + 1) * 128], buf[:, (4 * h + k) * 128:(4 * h + k + 1) * 128], ident),
                        a, bf, misc["cst"], sig=(k == 3))
                ms.append(m)
            own = []
            if keep is not None:
                c = act(lambda e: e.activation(keep[0][:, t, :], buf, ACT.Copy), a, after)
                own.append(pool(lambda e: e.tensor_tensor(keep[1][:, t, :], buf, keep[0][:, t, :], ALU.subtract), c))
                kept += own
            xs.give(buf, [m] + own)
            yield
            places = [(slice(None), slice(4 * h, 4 * h + 4), slice(t * 128, (t + 1) * 128)) for h in range(2)]
            for h in range(2):
                g = col(gname, 4 * h, 4).unsqueeze(2).to_broadcast([128, 4, 128])
                if y_r is None:
                    y, yf = dst[places[h]], after
                else:
                    y, yf = y_r.take()
                    y = y.rearrange("p (k n) -> p k n", k=4)
                ys.append(y)
                ds.append(dve(lambda e, b=bs[h], y=y, g=g: e.tensor_tensor(
                    y, bank[b][:, :].rearrange("p (k n) -> p k n", k=4), g, ALU.mult), ms[h], misc["cols"], yf))
                banks.give(bs[h], ds[h])
            yield
            if y_r is None:
                out += ds
                return
            cs = [act(lambda e, h=h: e.activation(HTH[places[h]], ys[h], ACT.Copy), ds[h], after) for h in range(2)]
            yield
            for h, q in enumerate((pool, dve)):
                d = q(lambda e, h=h: e.tensor_tensor(HTL[places[h]], ys[h], HTH[places[h]], ALU.subtract), cs[h])
                y_r.give(ys[h].rearrange("p k n -> p (k n)"), d)
                out.append(d)

        def norm_to_T(gname, xt, xs, y_r, beside):
            out = [[] for _ in range(TT)]
            chains = [norm_stages(t, gname, xt[t], xs, None, out[t], y_r=y_r) for t in range(TT)]
            staggered(chains + [beside()])
            return out

        def first_split(n):
            split_limit[0] = 1
            ahead()
            split_limit[0] = n - 1
            yield

        def gemm3_T(key, n0, after, b, bf, src=None, k0=0):
            wh, wl, wt = split_W(key, KD)
            hi, lo = src or [[v[:, k, :] for k in range(KD)] for v in (HTH, HTL)]
            for k in range(len(hi)):
                for i, (w, v) in enumerate(((wh, hi), (wh, lo), (wl, hi))):
                    last = k == len(hi) - 1 and i == 2
                    m = pe(lambda e, k=k, w=w, v=v, i=i, last=last: e.matmul(
                        bank[b][:, :], w[:, k0 + k, n0:n0 + 128], v[k], start=(k == 0 and i == 0), stop=last),
                        wt, after, bf, sig=last)
            return m

        def gemm3_T_halves(key, after, bs):
            wh, wl, wt = split_W(key, KD)
            ms = [None, None]
            for half in range(2):
                ts = slice(half * 256, (half + 1) * 256)
                for j in range(2):
                    for k in range(KD):
                        for i, (w, src) in enumerate(((wh, HTH), (wh, HTL), (wl, HTH))):
                            last = k == KD - 1 and i == 2
                            m = pe(lambda e, k=k, w=w, src=src, i=i, j=j, ts=ts, last=last: e.matmul(
                                bank[bs[j][0]][:, ts], w[:, k, j * 128:(j + 1) * 128], src[:, k, ts],
                                start=(k == 0 and i == 0), stop=last),
                                wt, after[2 * half:2 * half + 2], bs[j][1], sig=last)
                    ms[j] = m
            return ms

        def gemm3_toks(keys, after, then=None, between=None, per_k=None, by_tile=False):
            bs = [banks.take() for _ in range(TT)]
            ends = []

            def half(t, j):
                wh, wl, wt = split_W(keys[j], 4)
                b, bf = bs[t]
                for k in range(4):
                    for i, (src, w) in enumerate(((HTH, wh), (HTH, wl), (HTL, wh))):
                        first, last = j == k == i == 0, k == 3 and i == 2
                        m = pe(lambda e, k=k, w=w, src=src, i=i, first=first, last=last: e.matmul(
                            bank[b][:, :], src[:, 4 * j + k, t * 128:(t + 1) * 128], w[:, k, :],
                            start=first, stop=(last and j == 1)), wt, per_k[4 * j + k] if per_k else after[t], bf,
                            sig=last)
                return b, m

            if by_tile:
                for t in range(TT):
                    half(t, 0)
                    ends.append(half(t, 1))
                return ends
            for j in range(2):
                for t in range(TT):
                    b, m = half(t, j)
                    if j:
                        ends.append((b, m))
                        if then:
                            then(t, b, m)
                    elif between:
                        between()
                split_done(keys[j], m)
            return ends

        flip = [0]

        def evac(dst, src, after, scale=None):
            flip[0] ^= 1
            if flip[0]:
                if scale is None:
                    return act(lambda e: e.activation(dst, src, ACT.Copy), after)
                return act(lambda e: e.activation(dst, src, ACT.Copy, scale=scale), after)
            if scale is None:
                return dve(lambda e: e.tensor_copy(dst, src), after)
            return dve(lambda e: e.tensor_scalar(dst, src, scale, None, ALU.mult), after)

        qT = region(0, 4, 512)
        kT = region(2048, 4, 512)
        V = region(4096, 4, 512)
        U = region(6144, 4, 528)
        ya = [[v[:, k, :] for k in range(4)] for v in (YAH, YAL)]
        yb = [[YBH[:, k, 16:528] for k in range(4)], [YBL[:, k, :] for k in range(4)]]
        TB = [region(12352 + 512 * i, 512) for i in range(3)] + [mem(SPLIT0 + 512 * i, 512) for i in range(5)]
        sc_r = [mem(SPLIT0 + 2560 + 512 * i, 512) for i in range(2)]
        P_r = [mem(SPLIT0 + 3584 + 512 * i, 512) for i in range(3)]
        PT_r = [mem(SPLIT0 + 5120 + 512 * i, 512) for i in range(3)]
        ps_r = [mem(SPLIT0 + 6656 + 528 * i, 528) for i in range(2)]
        pl = region(9792, 512)
        load(pool, "wpg", wpg[:, :, :], wpg_d)
        for h in range(3):
            load(pool, f"tb{h}", TB[h], tb_d[:, h, :])
        load(pool, "rows", rows[:, :], rows_d[:, 3072:3072 + NROWS].to_broadcast([128, NROWS]))

        def load_row(name, *after):
            o = BIG[name]
            load(pool, "row_" + name, rowb[:, :], rows_d[:, o:o + D].to_broadcast([128, D]), *after)

        load_row("mix_post")
        load(pool, "wr", wr[:, :, :], wr_d)

        xs_ring = Ring([region(8256 + 1024 * i, 1024) for i in range(3)])
        y_ring = Ring([region(4096 + 512 * i, 512) for i in range(4)])
        xt = [misc[f"x{t}"] for t in range(TT)]
        hT_t = norm_to_T("mix_pre", xt, xs_ring, y_ring, lambda: first_split(8))
        ahead()

        zu = pool(lambda e: e.memset(U[:, :, 0:16], 0.0))
        qk_t = {}
        for i in range(4):
            if i == 0:
                bs = [banks.take() for _ in range(2)]
                ms = gemm3_T_halves(("in", 0), hT_t, bs)
            for j in range(2):
                n = 2 * i + j
                if i == 0:
                    b, m = bs[j][0], ms[j]
                else:
                    b, bf = banks.take()
                    m = gemm3_T(("in", i), j * 128, hT_t, b, bf)
                dst = qT[:, n, :] if n < 4 else kT[:, n - 4, :]
                qk_t[n] = evac(dst, bank[b][:, :], m, 0.125 if n < 4 else None)
                banks.give(b, qk_t[n])
            split_done(("in", i), m)
        v_t = []

        def v_out(dst, toks):
            def then(t, b, m):
                toks.append(evac(dst[:, t, :], bank[b][:, :], m))
                banks.give(b, toks[-1])
            return then

        gemm3_toks([("in", 4), ("in", 5)], hT_t, v_out(V, v_t))
        u_t = []
        for i in range(2):
            for j in range(2):
                g = 2 * i + j
                b, bf = banks.take()
                m = gemm3_T(("in", 6 + i), j * 128, hT_t, b, bf)
                u_t.append(evac(U[:, g, 16:528], bank[b][:, :], m))
                banks.give(b, u_t[-1])
            split_done(("in", 6 + i), m)
        free1 = everything()
        for h in range(3, 8):
            load(pool, f"tb{h}", TB[h], tb_d[:, h, :], free1)

        def pool_group(g):
            cur, cur_t = U[:, g, :], [u_t[g], zu]
            lo = 0
            for s in range(g + 1):
                d = 1 << s
                nxt = ps_r[s % 2]
                lo2 = lo + d
                cur_t = [pool(lambda e, cur=cur, nxt=nxt, d=d, lo2=lo2: e.tensor_tensor(
                    nxt[:, lo2:528], cur[:, lo2:528], cur[:, lo2 - d:528 - d], ALU.add), cur_t, free1)]
                cur, lo = nxt, lo2
            w = 2 << g
            mean = pool(lambda e: e.tensor_scalar(pl, cur[:, 16:528], 1.0 / w, None, ALU.mult), cur_t, pg_free[0])
            cn = con("cnt")[:, 16 * g:16 * g + w - 1]
            fix = pool(lambda e: e.tensor_tensor(pl[:, 0:w - 1], cur[:, 16:16 + w - 1], cn, ALU.mult),
                       mean, misc["cst"])
            sub = pool(lambda e: e.tensor_tensor(pl, pl, U[:, g, 16:528], ALU.subtract), fix)
            return sub

        def pool_mix(g, sub):
            b, bf = banks.take()
            m = pe(lambda e: e.matmul(bank[b][:, :], wpg[:, g, :], pl, start=True, stop=True), sub, bf, misc["wpg"])
            pg_free[0] = m
            sc = col("pool_scale", g)
            c = act(lambda e: e.activation(yb[0][g], bank[b][:, :], ACT.Copy, scale=sc), m, misc["cols"])
            d = dve(lambda e: e.scalar_tensor_tensor(out=yb[1][g], in0=bank[b][:, :], scalar=sc, in1=yb[0][g],
                                                     op0=ALU.mult, op1=ALU.subtract), c)
            banks.give(b, d)
            return d

        pg_free = [None]
        mixed_t = []

        sc_ring, P_ring, PT_ring = (Ring(r, free1) for r in (sc_r, P_r, PT_r))
        items = [(h, qt) for h in range(8) for qt in range(4)]
        ob = {}
        state = {}
        attn_t = []

        def a0(i):
            h, qt = items[i]
            nk, pr, hp = 128 * (qt + 1), 64 * (h % 2), h // 2
            b, bf = banks.take()
            m = pe(lambda e: e.matmul(bank[b][:, 0:nk], qT[pr:pr + 64, hp, qt * 128:(qt + 1) * 128],
                                      kT[pr:pr + 64, hp, 0:nk], start=True, stop=True),
                   bf, qk_t[hp], qk_t[4 + hp])
            sc, sf = sc_ring.take()
            P, pf = P_ring.take()
            mx, nm, rs, rr = stat(), stat(), stat(), stat()
            a = dve(lambda e: e.tensor_tensor_reduce(sc[:, 0:nk], bank[b][:, 0:nk], TB[h][:, 384 - 128 * qt:512], 1.0,
                                                     -3e38, ALU.add, ALU.max, mx), m, sf, misc[f"tb{h}"])
            banks.give(b, a)
            c = dve(lambda e: e.tensor_scalar(nm, mx, -1.0, None, ALU.mult), a)
            ex = act(lambda e: e.activation(P[:, 0:nk], sc[:, 0:nk], ACT.Exp, bias=nm, accum_out=rs), c, pf)
            sc_ring.give(sc, ex)
            state[i] = (P, rr, rs, ex)

        def a0b(i):
            nk = 128 * (items[i][1] + 1)
            P, rr, rs, ex = state[i]
            r = dve(lambda e: e.reciprocal(rr, rs), ex)
            n = dve(lambda e: e.tensor_scalar(P[:, 0:nk], P[:, 0:nk], rr, None, ALU.mult), r)
            state[i] = (P, n)

        def a1(i):
            h, qt = items[i]
            P, n = state[i]
            b, bf = banks.take()
            for k in range(qt + 1):
                m = pe(lambda e, k=k: e.transpose(bank[b][:, k * 128:(k + 1) * 128], P[:, k * 128:(k + 1) * 128],
                                                  ident), n, bf, sig=(k == qt))
            P_ring.give(P, m)
            PT, pf = PT_ring.take()
            nk = 128 * (qt + 1)
            ev = act(lambda e: e.activation(PT[:, 0:nk], bank[b][:, 0:nk], ACT.Copy), m, pf)
            banks.give(b, ev)
            state[i] = (PT, ev)

        def a2(i):
            h, qt = items[i]
            PT, ev = state[i]
            pr, hp = 64 * (h % 2), h // 2
            if hp not in ob:
                ob[hp] = banks.take()
            b, bf = ob[hp]
            for k in range(qt + 1):
                m = pe(lambda e, k=k: e.matmul(bank[b][pr:pr + 64, qt * 128:(qt + 1) * 128],
                                               V[:, k, h * 64:(h + 1) * 64], PT[:, k * 128:(k + 1) * 128],
                                               start=(k == 0), stop=(k == qt)), ev, bf, v_t, sig=(k == qt))
            PT_ring.give(PT, m)
            if h % 2 and qt == 3:
                c = act(lambda e: e.activation(ya[0][hp], bank[b][:, :], ACT.Copy), m)
                d = dve(lambda e: e.tensor_tensor(ya[1][hp], bank[b][:, :], ya[0][hp], ALU.subtract), c)
                banks.give(b, d)
                attn_t.append(d)

        for i in range(len(items) + 3):
            if i < len(items):
                a0(i)
            if 1 <= i <= len(items):
                a0b(i - 1)
            if 2 <= i <= len(items) + 1:
                a1(i - 2)
            if i >= 3:
                a2(i - 3)
            if i == 20:
                allow(1, [2])
            if i % 8 == 0 and i // 8 < 4:
                pooled = pool_group(i // 8)
            if i % 8 == 5 and i // 8 < 4:
                mixed_t.append(pool_mix(i // 8, pooled))
        free2 = everything()

        MT = region(2048, 8, 512)
        g_ring = Ring([region(12352 + 512 * i, 512) for i in range(3)], free2)
        allow(11 + 4 + 33 + 12, [0, 1], free2)
        mix_t, mt_t = [], []
        def gate(bias, b_y, m_y, b_g, m_g, out):
            g, gf = g_ring.take()
            c = act(lambda e: e.activation(g, bank[b_g][:, :], ACT.Sigmoid, bias=col("b_gate", bias)), m_g, gf)
            banks.give(b_g, c)
            d = dve(lambda e: e.tensor_tensor(g if out is None else out, bank[b_y][:, :], g, ALU.mult), c, m_y, free2)
            banks.give(b_y, d)
            if out is not None:
                g_ring.give(g, d)
            return g, d

        for i in range(4):
            y_b = [[banks.take() for _ in range(2)] for _ in range(2)]
            y_m = [[gemm3_T(("ap", i), 128 * j, t_, *y_b[q][j], src=y, k0=4 * q) for j in range(2)]
                   for q, (y, t_) in enumerate(((ya, attn_t), (yb, mixed_t)))]
            split_done(("ap", i), y_m[1][1])
            firsts = []
            for q, name in enumerate(("ga", "gb")):
                gs = [banks.take() for _ in range(2)]
                ms = [gemm3_T((name, i), 128 * j, hT_t, *gs[j]) for j in range(2)]
                for j in range(2):
                    n = 2 * i + j
                    g, d = gate(8 * q + n, y_b[q][j][0], y_m[q][j], gs[j][0], ms[j], None if q else MT[:, n, :])
                    if q:
                        d = pool(lambda e, n=n, g=g: e.tensor_tensor(MT[:, n, :], MT[:, n, :], g, ALU.add), d, firsts[j])
                        g_ring.give(g, d)
                        mix_t.append(d)
                    else:
                        firsts.append(d)
                if q == 0 or i < 3:
                    split_done((name, i), ms[1])
        mb = ms[1]
        for n in range(8):
            c = act(lambda e, n=n: e.activation(HTH[:, n, :], MT[:, n, :], ACT.Copy), mix_t[n], mb)
            mt_t.append(dve(lambda e, n=n: e.tensor_tensor(HTL[:, n, :], MT[:, n, :], HTH[:, n, :], ALU.subtract), c))
        split_done(("gb", 3), mb)

        def residual_stages(halves, gname, tt, tmps, freed):
            r, rt = yield from rstd_stages(lambda i: halves[i][0], D, halves[0][1], halves[1][1])
            tmp, tf = tmps.take()
            z = [dve(lambda e, h=h: e.scalar_tensor_tensor(
                out=tmp[:, h * 512:(h + 1) * 512], in0=halves[h][0], scalar=r,
                in1=rowb[:, h * 512:(h + 1) * 512], op0=ALU.mult, op1=ALU.mult),
                rt, tf, misc["row_" + gname]) for h in range(2)]
            freed(z)
            yield
            f = []
            for h, q in enumerate((pool, dve)):
                hs = slice(h * 512, (h + 1) * 512)
                f.append(q(lambda e, hs=hs: e.tensor_tensor(X[:, tt, hs], X[:, tt, hs], tmp[:, hs], ALU.add), z))
            tmps.give(tmp, f)
            yield
            return f

        tmp_ring = Ring([region(8256 + 1024 * i, 1024) for i in range(4)], mt_t)
        xs_ring = Ring([region(1024 * i, 1024) for i in range(4)], mt_t)
        y_ring = Ring([region(4096 + 512 * i, 512) for i in range(4)], mt_t)
        x_t, hT_t = [], [[] for _ in range(TT)]
        held = {}
        for h in range(2):
            for t, e_ in enumerate(gemm3_toks([("wo", 2 * h), ("wo", 2 * h + 1)], None, per_k=mt_t, by_tile=h == 1)):
                held[t, h] = e_
        m = e_[1]

        def mix_chain(t):
            def freed(z):
                for i in range(2):
                    banks.give(held[t, i][0], z[i])

            f = yield from residual_stages([(bank[held[t, i][0]][:, :], held[t, i][1]) for i in range(2)], "mix_post", t,
                                           tmp_ring, freed)
            x_t.append(f)
            yield from norm_stages(t, "ffn_pre", f, xs_ring, m, hT_t[t], y_r=y_ring)

        staggered(mix_chain(t) for t in range(TT))
        split_done(("wo", 2), m)
        split_done(("wo", 3), m)
        load_row("ffn_post", x_t)
        free4 = [hT_t, x_t]
        FACC = region(6144, 4, 1024)
        zv_ring = Ring([region(10240 + 512 * i, 512) for i in range(3)], free4)
        zg_ring = Ring([region(11776 + 512 * i, 512) for i in range(4)], free4)
        tile_ring = Ring(list(range(NATILE)), free4)
        facc_t = {(t, h): free4 for t in range(TT) for h in range(2)}

        def conv(b, m, z, zf, n):
            cw = [col("conv_w", i * 44 + n) for i in range(3)]
            a = act(lambda e: e.activation(z, bank[b][:, :], ACT.Identity, bias=col("conv_b", n), scale=cw[2]), m, zf)
            c = dve(lambda e: e.scalar_tensor_tensor(out=z[:, 2:512], in0=bank[b][:, 0:510], scalar=cw[0],
                                                     in1=z[:, 2:512], op0=ALU.mult, op1=ALU.add), a)
            d = dve(lambda e: e.scalar_tensor_tensor(out=z[:, 1:512], in0=bank[b][:, 0:511], scalar=cw[1],
                                                     in1=z[:, 1:512], op0=ALU.mult, op1=ALU.add), c)
            banks.give(b, d)
            return d

        made = deque()
        last_lo = [None]

        def up(uu):
            if uu == 0:
                bs = [banks.take() for _ in range(2)]
                ms = gemm3_T_halves(("uv", 0), hT_t, bs)
            for j in range(2):
                n = 2 * uu + j
                if uu == 0:
                    b1, mv = bs[j][0], ms[j]
                else:
                    b1, f1 = banks.take()
                    mv = gemm3_T(("uv", uu), j * 128, hT_t, b1, f1)
                b2, f2 = banks.take()
                mg = gemm3_T(("ug", uu), j * 128, hT_t, b2, f2)
                if j:
                    split_done(("uv", uu), mv)
                    split_done(("ug", uu), mg)
                (zv, fv), (zg, fg) = zv_ring.take(), zg_ring.take()
                i, af = tile_ring.take()
                dg = conv(b2, mg, zg, fg, 22 + n)
                dv = conv(b1, mv, zv, fv, n)
                ge = act(lambda e, zg=zg: e.activation(zg, zg, ACT.Gelu_apprx_tanh), dg)
                o = pool(lambda e, zg=zg, zv=zv: e.tensor_tensor(zg, zg, zv, ALU.mult), ge, dv)
                zv_ring.give(zv, o)
                hi = act(lambda e, i=i, zg=zg: e.activation(AH[:, i, :], zg, ACT.Copy), o, af)
                lo = pool(lambda e, i=i, zg=zg: e.tensor_tensor(AL[:, i, :], zg, AH[:, i, :], ALU.subtract), hi)
                zg_ring.give(zg, lo)
                made.append((i, lo))
                last_lo[0] = lo

        def down(ds, first, last=False):
            tiles = [made.popleft() for _ in range(2 * len(ds))]
            if last:
                for ts in ((0, 1), (2, 3)):
                    places = [(t, h) for t in ts for h in range(2)]
                    bs = {p: banks.take() for p in places}
                    for part in (range(4), range(4, len(tiles))):
                        for t, h in places:
                            b, bf = bs[t, h]
                            for i in part:
                                a, at = tiles[i]
                                wh, wl, wt = split_W(("dn", ds[i // 2]), 2)
                                for q, (src, w) in enumerate(((AH, wh), (AH, wl), (AL, wh))):
                                    end = i == len(tiles) - 1 and q == 2
                                    m = pe(lambda e, i=i, a=a, q=q, src=src, w=w, t=t, h=h, b=b, end=end: e.matmul(
                                        bank[b][:, :], src[:, a, t * 128:(t + 1) * 128],
                                        w[:, i % 2, h * 512:(h + 1) * 512], start=(i == 0 and q == 0), stop=end),
                                        wt, bf, at, sig=end)
                            held[t, h] = (b, m)
                return m
            for t in range(TT):
                for h in range(2):
                    b, bf = banks.take()
                    for i, (a, at) in enumerate(tiles):
                        wh, wl, wt = split_W(("dn", ds[i // 2]), 2)
                        for q, (src, w) in enumerate(((AH, wh), (AH, wl), (AL, wh))):
                            end = i == len(tiles) - 1 and q == 2
                            m = pe(lambda e, i=i, a=a, q=q, src=src, w=w, t=t, h=h, b=b, end=end: e.matmul(
                                bank[b][:, :], src[:, a, t * 128:(t + 1) * 128], w[:, i % 2, h * 512:(h + 1) * 512],
                                start=(i == 0 and q == 0), stop=end), wt, bf, at, sig=end)
                    dst = FACC[:, t, h * 512:(h + 1) * 512]
                    if first:
                        f = dve(lambda e, dst=dst, b=b: e.tensor_copy(dst, bank[b][:, :]), m, facc_t[t, h])
                    else:
                        f = dve(lambda e, dst=dst, b=b: e.tensor_tensor(dst, bank[b][:, :], dst, ALU.add), m,
                                facc_t[t, h])
                    banks.give(b, f)
                    facc_t[t, h] = f
            for a, _ in tiles:
                tile_ring.give(a, m)
            for d in ds:
                split_done(("dn", d), m)
            return m

        order = ffn_order()
        for n, (us, ds) in enumerate(order):
            for uu in us:
                up(uu)
            m = down(ds, n == 0, n == len(order) - 1)
        x_t, aT_t = [], [[] for _ in range(TT)]
        tmp_ring = Ring([region(10240 + 1024 * i, 1024) for i in range(3)], last_lo[0])
        y_ring = Ring([region(4096 + 512 * i, 512) for i in range(4)], m)
        xs_ring = Ring([])

        def ffn_chain(t):
            fs = []
            for h in range(2):
                b, mt = held[t, h]
                dst = FACC[:, t, h * 512:(h + 1) * 512]
                fs.append(dve(lambda e, dst=dst, b=b: e.tensor_tensor(dst, bank[b][:, :], dst, ALU.add), mt, facc_t[t, h]))
                banks.give(b, fs[h])
            yield
            f = yield from residual_stages([(FACC[:, t, h * 512:(h + 1) * 512], fs[h]) for h in range(2)], "ffn_post", t,
                                           tmp_ring, lambda z: xs_ring.give(FACC[:, t, :], z))
            x_t.append(f)
            yield from norm_stages(t, "mix2", f, xs_ring, m, aT_t[t], y_r=y_ring)

        def free_first():
            split_done(("dn", order[-1][1][0]), m)
            yield

        staggered([ffn_chain(t) for t in range(TT)] + [free_first()])
        for d in order[-1][1][1:]:
            split_done(("dn", d), m)
        load_row("ple", x_t)
        free6 = [aT_t, x_t]

        qaT, kaT = region(0, 4, 512), region(2048, 4, 512)
        qbT, kbT = region(4096, 4, 512), region(6144, 4, 512)
        Va = region(8192, 4, 512)
        sqr = Ring([region(10240 + 512 * i, 512) for i in range(2)], free6)
        qnr = Ring([region(11264 + 512 * i, 512) for i in range(5)], free6)
        t1r = Ring([region(6144 + 512 * i, 512) for i in range(2)], free6)
        t2r = Ring([region(7168 + 512 * i, 512) for i in range(2)], free6)

        pend = []

        def settle():
            if pend:
                pend.pop(0)()

        def qk_tok(unit, nh, gname, dstT, scale, rope, by_block=False):
            dh = 512 // nh
            outs = []

            def first(t, b, m):
                sq, sf = sqr.take()
                ss = stat(nh)
                a = act(lambda e: e.activation(sq, bank[b][:, :], ACT.Square), m, sf)
                c = dve(lambda e: e.tensor_reduce(ss, sq.rearrange("p (h d) -> p h d", h=nh), AX, ALU.add), a)
                sqr.give(sq, c)
                r, rt = rstd_of(ss, nh, dh, c)
                qn, qf = qnr.take()
                q3 = qn.rearrange("p (h d) -> p h d", h=nh)
                d = dve(lambda e: e.tensor_tensor(q3, bank[b][:, :].rearrange("p (h d) -> p h d", h=nh),
                                                  r.unsqueeze(2).to_broadcast([128, nh, dh]), ALU.mult), rt, qf)
                banks.give(b, d)
                g = row(gname).unsqueeze(1).to_broadcast([128, nh, dh])
                f = pool(lambda e: e.tensor_tensor(q3, q3, g, ALU.mult), d)
                if rope:
                    (t1, f1), (t2, f2) = t1r.take(), t2r.take()
                    co = con("cos")[:, t * 32:(t + 1) * 32].unsqueeze(1).to_broadcast([128, 16, 32])
                    si = con("sin")[:, t * 32:(t + 1) * 32].unsqueeze(1).to_broadcast([128, 16, 32])
                    v16 = lambda a: a.rearrange("p (h d) -> p h d", h=16)
                    v4 = lambda a, s: a.rearrange("p (h s d) -> p h s d", s=2, d=32)[:, :, s, :]
                    c1 = dve(lambda e: e.tensor_tensor(v16(t1), v16(qn), co, ALU.mult), f, f1)
                    c2 = dve(lambda e: e.tensor_tensor(v16(t2), v16(qn), si, ALU.mult), f, f2)
                    e1 = pool(lambda e: e.tensor_tensor(v4(qn, 0), v4(t1, 0), v4(t2, 1), ALU.subtract), c1, c2)
                    f = pool(lambda e: e.tensor_tensor(v4(qn, 1), v4(t1, 1), v4(t2, 0), ALU.add), e1)
                    t1r.give(t1, f)
                    t2r.give(t2, f)
                pend.append(lambda: second(t, qn, f))

            def second(t, qn, f):
                b, bf = banks.take()
                for k in range(4):
                    m = pe(lambda e, k=k: e.transpose(bank[b][:, k * 128:(k + 1) * 128], qn[:, k * 128:(k + 1) * 128],
                                                      ident), f, bf, sig=(k == 3))
                qnr.give(qn, m)
                dst = dstT[:, :, t * 128:(t + 1) * 128]
                src = bank[b][:, :].rearrange("p (k n) -> p k n", k=4)
                if by_block:
                    for i in range(4):
                        d4 = dstT[:, i, :].rearrange("p (j r c) -> p j r c", j=4, r=8)[:, :, 2 * t:2 * t + 2, :]
                        s4 = src[:, i, :].rearrange("p (r j c) -> p j r c", r=2, j=4)
                        for rr in range(2):
                            o = act(lambda e, d4=d4, s4=s4, rr=rr: e.activation(d4[:, :, rr, :], s4[:, :, rr, :], ACT.Copy,
                                                                                scale=scale), m)
                elif scale is None:
                    o = act(lambda e: e.activation(dst, src, ACT.Copy), m)
                else:
                    o = act(lambda e: e.activation(dst, src, ACT.Copy, scale=scale), m)
                banks.give(b, o)
                outs.append(o)

            gemm3_toks([("in2", unit), ("in2", unit + 1)], aT_t, first, settle)
            return outs

        qa_t = qk_tok(0, 8, "qa", qaT, 0.125, True)
        ka_t = qk_tok(2, 8, "ka", kaT, None, True)
        va_t = []
        gemm3_toks([("in2", 4), ("in2", 5)], aT_t, v_out(Va, va_t), settle)
        qb_t = qk_tok(6, 16, "qb", qbT, 32.0 ** -0.5, False, by_block=True)
        kb_t = qk_tok(8, 16, "kb", kbT, None, False)
        split_left = [i for i, _ in split_free] + [split_of["in2", 10 + i][0] for i in range(2)]
        sa, sb_ = (SPLIT0 + 2 * UNIT * split_of["in2", 10 + i][0] for i in range(2))
        sc = 3 * SPLIT0 + 6 * UNIT - sa - sb_
        while pend:
            settle()
        vbJ = mem(sc, 4, 4, 256)
        Vj = mem(sa, 8, 512)
        KB = [0, 8, 24, 32]
        vb_t = [[] for _ in range(4)]
        free_v = everything()
        for i in range(2):
            for jj in range(2):
                f = 2 * i + jj
                b, bf = banks.take()
                m = gemm3_T(("in2", 10 + i), jj * 128, aT_t, b, bf)
                b4 = bank[b][:, :].rearrange("p (r c) -> p r c", c=64)
                for j in range(4):
                    o = act(lambda e, f=f, j=j, b4=b4: e.activation(
                        vbJ[:, f, j, :].rearrange("p (r c) -> p r c", c=32), b4[:, :, KB[j]:KB[j] + 32], ACT.Copy),
                        m, free_v)
                    vb_t[j].append(o)
                banks.give(b, o)
            split_done(("in2", 10 + i), m)
        free_j = everything()
        vj_t = []
        for j in range(4):
            for half in range(2):
                b, bf = banks.take()
                for f in range(4):
                    m = pe(lambda e, f=f, j=j, half=half, b=b: e.transpose(
                        bank[b][:, f * 128:(f + 1) * 128], vbJ[:, f, j, half * 128:(half + 1) * 128], ident),
                        vb_t[j], bf, sig=(f == 3))
                vj_t.append(evac(Vj[:, 2 * j + half, :], bank[b][:, :], [m, free_j]))
                banks.give(b, vj_t[-1])
        free7 = everything()

        lam = stat(6)
        lt = [stat(64), stat(64)]
        lp = []
        for i, (a_, b_) in enumerate((("lq1", "lk1"), ("lq2", "lk2"))):
            lp.append(dve(lambda e, i=i, a_=a_, b_=b_: e.tensor_tensor_reduce(
                lt[i], row(a_), row(b_), 1.0, 0.0, ALU.mult, ALU.add, lam[:, i:i + 1]), misc["rows"]))
        le = act(lambda e: e.activation(lam[:, 2:4], lam[:, 0:2], ACT.Exp), lp)
        lm0 = dve(lambda e: e.tensor_tensor(lam[:, 4:5], lam[:, 2:3], lam[:, 3:4], ALU.subtract), le)
        LAM0 = 0.8 - 0.6 * float(np.exp(0.0))
        lm = dve(lambda e: e.tensor_scalar(lam[:, 5:6], lam[:, 4:5], LAM0, None, ALU.add), lm0)

        OR = region(10240, 4, 512)
        wTr = Ring([region(12288 + 512 * i, 512) for i in range(3)], free7)
        qm_r = [mem(sb_ + UNIT * (1 - i), 4, 512) for i in range(2)]
        qz = [pool(lambda e: e.memset(qm_r[0], 0.0), free7), None]
        qm_t, qm_free = {}, [None, None]

        def spread(hg):
            v = qm_r[hg % 2]
            qm_t[hg] = [pool(lambda e, hh=hh: e.tensor_copy(v[32 * hh:32 * hh + 32, hh, :],
                                                            qbT[32 * hh:32 * hh + 32, hg, :]),
                             qz[hg % 2], qb_t, qm_free[hg % 2]) for hh in range(4)]

        spread(0)
        e1r = Ring([mem(o, 512) for o in (sb_, sb_ + 512, sc + 3072)], free7)
        e2r = Ring([mem(o, 512) for o in (sb_ + 1024, sb_ + 1536, sc + 3584)], free7)
        nb1 = mem(sc, 4, 3, 256)
        nbr = Ring([nb1], free7)
        nb_sem = [sem("d_nb0"), sem("d_nb1")]
        nb_n = [0, 0]

        def nb_load(hg):
            buf, bf = nbr.take()
            i = hg % 2
            nb_n[i] += 1
            return buf, sp.dma(buf, nb_d[hg, :, :].rearrange("p (h j k) -> p h j k", h=4, j=3), nb_sem[i], nb_n[i], bf)

        nbs = [nb_load(0)]
        items = [(h, qt) for h in range(4) for qt in range(4)]
        state = {}
        ob = {}
        or_t = {}

        def d0(i):
            h, qt = items[i]
            ms = []
            bs = []
            for s in range(2):
                b, bf = banks.take()
                bs.append(b)
                ms.append(pe(lambda e, s=s, b=b: e.matmul(
                    bank[b][:, :], qaT[64 * s:64 * s + 64, h, qt * 128:(qt + 1) * 128],
                    kaT[64 * s:64 * s + 64, h, :], start=True, stop=True), bf, qa_t, ka_t))
            nm, rs, rr = stat(2), stat(2), stat(3)
            E = [e1r.take(), e2r.take()]
            ex = []
            for s in range(2):
                a = dve(lambda e, s=s: e.tensor_reduce(nm[:, s:s + 1], bank[bs[s]][:, :], AX, ALU.max, negate=True), ms[s])
                x_ = act(lambda e, s=s: e.activation(E[s][0], bank[bs[s]][:, :], ACT.Exp, bias=nm[:, s:s + 1],
                                                     accum_out=rs[:, s:s + 1]), a, E[s][1])
                banks.give(bs[s], x_)
                ex.append(x_)
            state[i] = (E, rr, rs, ex)

        def d0b(i):
            E, rr, rs, ex = state[i]
            r = dve(lambda e: e.reciprocal(rr[:, 0:2], rs), ex)
            l = dve(lambda e: e.tensor_tensor(rr[:, 2:3], rr[:, 1:2], lam[:, 5:6], ALU.mult), r, lm)
            t = dve(lambda e: e.tensor_scalar(E[1][0], E[1][0], rr[:, 2:3], None, ALU.mult), l)
            w = dve(lambda e: e.scalar_tensor_tensor(out=E[0][0], in0=E[0][0], scalar=rr[:, 0:1], in1=E[1][0],
                                                     op0=ALU.mult, op1=ALU.subtract), t)
            e2r.give(E[1][0], w)
            state[i] = (E[0][0], w)

        def d1(i):
            Wt, w = state[i]
            b, bf = banks.take()
            for k in range(4):
                m = pe(lambda e, k=k: e.transpose(bank[b][:, k * 128:(k + 1) * 128], Wt[:, k * 128:(k + 1) * 128], ident),
                       w, bf, sig=(k == 3))
            e1r.give(Wt, m)
            wT, wf = wTr.take()
            ev = act(lambda e: e.activation(wT, bank[b][:, :], ACT.Copy), m, wf)
            banks.give(b, ev)
            state[i] = (wT, ev)

        def d2(i):
            h, qt = items[i]
            wT, ev = state[i]
            if h not in ob:
                ob[h] = banks.take()
            b, bf = ob[h]
            for k in range(4):
                m = pe(lambda e, k=k: e.matmul(bank[b][:, qt * 128:(qt + 1) * 128], wT[:, k * 128:(k + 1) * 128],
                                               Va[:, k, h * 128:(h + 1) * 128], start=(k == 0), stop=(k == 3)),
                       ev, bf, va_t, sig=(k == 3))
            wTr.give(wT, m)
            if qt == 3:
                d = dve(lambda e: e.tensor_copy(OR[:, :, h * 128:(h + 1) * 128],
                                                bank[b][:, :].rearrange("p (q d) -> p q d", q=4)), m, free7)
                banks.give(b, d)
                or_t[h] = d

        n = len(items)
        for i in range(n + 3):
            if i < n:
                d0(i)
            if 1 <= i <= n:
                d0b(i - 1)
            if 2 <= i <= n + 1:
                d1(i - 2)
            if i >= 3:
                d2(i - 3)

        free8 = everything()
        cat_t = []
        gs_ = stat()
        gs_t = dve(lambda e: e.tensor_scalar(gs_, col("g_sub"), 1.0 - LAM0, None, ALU.mult))
        sqr = Ring([region(12288 + 512 * i, 512) for i in range(3)], free8)

        def oa_chain(t):
            ss, ms, sd, r = stat(4), stat(4), stat(4), stat(4)
            sq, sf = sqr.take()
            o3 = OR[:, t, :].rearrange("p (h d) -> p h d", h=4)
            a = act(lambda e: e.activation(sq, OR[:, t, :], ACT.Square), list(or_t.values()), sf)
            yield
            c = dve(lambda e: e.tensor_reduce(ss, sq.rearrange("p (h d) -> p h d", h=4), AX, ALU.add), a)
            sqr.give(sq, c)
            c = dve(lambda e: e.tensor_scalar(ms, ss, 1.0 / 128, EPS, ALU.mult, ALU.add), c)
            yield
            a = act(lambda e: e.activation(sd, ms, ACT.Sqrt), c)
            yield
            c = dve(lambda e: e.reciprocal(r, sd), a)
            d = dve(lambda e: e.tensor_tensor(o3, o3, r.unsqueeze(2).to_broadcast([128, 4, 128]), ALU.mult), c)
            yield
            b, bf = banks.take()
            for k in range(4):
                m = pe(lambda e, k=k: e.transpose(bank[b][:, k * 128:(k + 1) * 128], OR[:, t, k * 128:(k + 1) * 128],
                                                  ident), d, bf, sig=(k == 3))
            place = (slice(None), slice(0, 4), slice(t * 128, (t + 1) * 128))
            src = bank[b][:, :].rearrange("p (k n) -> p k n", k=4)
            yield
            c = act(lambda e: e.activation(HTH[place], src, ACT.Copy, scale=gs_), m, gs_t)
            yield
            f = dve(lambda e: e.scalar_tensor_tensor(out=HTL[place], in0=src, scalar=gs_, in1=HTH[place], op0=ALU.mult,
                                                     op1=ALU.subtract), c)
            banks.give(b, f)
            cat_t.append(f)

        qz[1] = pool(lambda e: e.memset(qm_r[1], 0.0), free8)
        spread(1)
        nbr.give(region(0, 4, 3, 256), free8)
        nbs.append(nb_load(1))
        scr = Ring([region(8192, 4, 256), region(9216, 4, 256)], free8)
        Pr = Ring([region(3072, 4, 256)], free8)
        PTr = Ring([mem(sc + 3072, 8, 128)], free8)
        items = [(hg, j) for hg in range(4) for j in range(4)]
        state = {}
        ob = {}
        k4 = kbT.rearrange("p f (r c) -> p f r c", c=64)
        catR = [v[:, :, :].rearrange("p f (r c) -> p f r c", c=64) for v in (HTH, HTL)]

        def n0(i):
            hg, j = items[i]
            qm = qm_r[hg % 2]
            nb, nt = nbs[hg]
            jt = (0, 1, 1, 2)[j]
            scb, sf = scr.take()
            P, pf = Pr.take()
            mx, nm, rs, rr = stat(4), stat(4), stat(4), stat(4)
            tt = []
            for hh in range(4):
                b, bf = banks.take()
                m = pe(lambda e, hh=hh, b=b: e.matmul(
                    bank[b][:, 0:256], qm[:, hh, 128 * j:128 * j + 128], k4[:, hg, :, KB[j]:KB[j] + 32], start=True,
                    stop=True), bf, qm_t[hg], kb_t)
                a = dve(lambda e, hh=hh, b=b: e.tensor_tensor_reduce(
                    scb[:, hh, :], bank[b][:, 0:256], nb[:, hh, jt, :], 1.0, -3e38,
                    ALU.add, ALU.max, mx[:, hh:hh + 1]), m, sf, nt)
                tt.append(a)
                banks.give(b, a)
            c = dve(lambda e: e.tensor_scalar(nm, mx, -1.0, None, ALU.mult), tt)
            for g in range(4):
                ex = act(lambda e, g=g: e.activation(P[:, g, :], scb[:, g, :], ACT.Exp, bias=nm[:, g:g + 1],
                                                     accum_out=rs[:, g:g + 1]), c, pf)
            scr.give(scb, ex)
            state[i] = (P, rr, rs, ex)
            if j == 3:
                qm_free[hg % 2] = m
                if hg + 2 < 4:
                    spread(hg + 2)
                nbr.give(nb, tt[-1])
                if hg + 2 < 4:
                    nbs.append(nb_load(hg + 2))

        def n0b(i):
            P, rr, rs, ex = state[i]
            r = dve(lambda e: e.reciprocal(rr, rs), ex)
            d = dve(lambda e: e.tensor_tensor(P, P, rr.unsqueeze(2).to_broadcast([128, 4, 256]), ALU.mult), r)
            state[i] = (P, d)

        def n1(i):
            P, d = state[i]
            PT, pf = PTr.take()
            evs = []
            for half in range(2):
                b, bf = banks.take()
                for g in range(4):
                    m = pe(lambda e, g=g, b=b, half=half: e.transpose(
                        bank[b][:, g * 128:(g + 1) * 128], P[:, g, half * 128:(half + 1) * 128], ident),
                        d, bf, sig=(g == 3))
                src = bank[b][:, :].rearrange("p (g q) -> p g q", g=4)
                ev = act(lambda e, half=half, src=src: e.activation(PT[:, 4 * half:4 * half + 4, :], src, ACT.Copy), m, pf)
                banks.give(b, ev)
                evs.append(ev)
            Pr.give(P, m)
            state[i] = (PT, evs)

        def n2(i):
            hg, j = items[i]
            PT, evs = state[i]
            if hg not in ob:
                ob[hg] = banks.take()
            b, bf = ob[hg]
            for half in range(2):
                for g in range(4):
                    m = pe(lambda e, g=g, half=half: e.matmul(
                        bank[b][32 * g:32 * g + 32, j * 128:(j + 1) * 128],
                        Vj[:, 2 * j + half, hg * 128 + 32 * g:hg * 128 + 32 * g + 32], PT[:, 4 * half + g, :],
                        start=(half == 0), stop=(half == 1), tile_position=(0, 32 * g)),
                        evs, bf, vj_t, sig=(g == 3 and half == 1))
            PTr.give(PT, m)
            if j == 3:
                for jj in range(4):
                    hi = catR[0][:, 4 + hg, :, 16 * jj:16 * jj + 16]
                    src = bank[b][:, jj * 128:(jj + 1) * 128].rearrange("p (r c) -> p r c", c=16)
                    c = act(lambda e, hi=hi, src=src: e.activation(hi, src, ACT.Copy), m)
                for jj in range(4):
                    hi, lo = (v[:, 4 + hg, :, 16 * jj:16 * jj + 16] for v in catR)
                    src = bank[b][:, jj * 128:(jj + 1) * 128].rearrange("p (r c) -> p r c", c=16)
                    o = dve(lambda e, hi=hi, lo=lo, src=src: e.tensor_tensor(lo, src, hi, ALU.subtract), c)
                banks.give(b, o)
                cat_t.append(o)

        n0(0)
        staggered((oa_chain(t) for t in range(TT)), 2)
        free_o = everything()
        for o in (10240, 11264):
            Pr.give(region(o, 4, 256), free_o)
        PTr.give(region(12288, 8, 128), free_o)
        for i in range(len(items) + 3):
            if 0 < i < len(items):
                n0(i)
            if i == len(items) + 2:
                allow(1, [k for k in split_left if SPLIT0 + 2 * UNIT * k == sb_], qm_free)
            if 1 <= i <= len(items):
                n0b(i - 1)
            if i >= 3:
                n2(i - 3)
            if 2 <= i <= len(items) + 1:
                n1(i - 2)

        free_n = everything()
        allow(3, [i for i in split_left if SPLIT0 + 2 * UNIT * i != sb_], free_n)

        xs_ring = Ring([region(o, 1024) for o in (5120, 8192, 9216)], free_n)

        def out2_add(h, t, b, m):
            dst = X[:, t, h * 512:(h + 1) * 512]
            f = dve(lambda e: e.tensor_tensor(dst, bank[b][:, :], dst, ALU.add), m)
            banks.give(b, f)
            return f

        XNT = area(8192, 8, 512)
        xnT_t, xs_t = [], []
        for h in range(2):
            ends = gemm3_toks([("out2", 2 * h), ("out2", 2 * h + 1)], [cat_t] * TT, by_tile=h == 1)
            if h == 0:
                x_t = [out2_add(0, t, *ends[t]) for t in range(TT)]
        m = ends[-1][1]

        slots += [mem(i * UNIT, UNIT) for i in range(NS, NS_MOE)]
        slots += [area(o, UNIT) for o in (20480, 13312, 24576, 13312 + UNIT, 13312 + 2 * UNIT)]
        for i in (7, 8, 9, 4, 10, 11, 5, 6):
            free_slots.append((i, m))
        issue()

        def out2_chain(t):
            f = out2_add(1, t, *ends[t])
            yield
            yield from norm_stages(t, "ffn2", [x_t[t], f], xs_ring, m, xnT_t, dst=XNT, keep=(XSH, XSL), kept=xs_t)

        staggered(out2_chain(t) for t in range(TT))

        route = area(26624, 1600)
        L = route[:, 0:144].rearrange("p (t n) -> p t n", t=4)
        RK = route[:, 144:272].rearrange("p (t e) -> p t e", t=4)
        W32 = route[:, 272:400].rearrange("p (t e) -> p t e", t=4)
        SEL = route[:, 400:528].rearrange("p (t e) -> p t e", t=4)
        ro = [528]

        def rt4(*shape):
            n = int(np.prod(shape))
            a = route[:, ro[0]:ro[0] + n]
            ro[0] += n
            if len(shape) == 2:
                a = a.rearrange("p (a b) -> p a b", a=shape[0])
            if len(shape) == 3:
                a = a.rearrange("p (a b c) -> p a b c", a=shape[0], b=shape[1])
            return a

        b, bf = banks.take()
        for k in range(KD):
            m = pe(lambda e, k=k, b=b: e.matmul(bank[b][0:36, :], wr[:, k, :], XNT[:, k, :], start=(k == 0),
                                                stop=(k == KD - 1)), xnT_t, bf, misc["wr"], sig=(k == KD - 1))
        LT = area(19456, 512)
        lt_ = act(lambda e, b=b: e.activation(LT[0:36, :], bank[b][0:36, :], ACT.Copy), m, xs_t)
        banks.give(b, lt_)
        b, bf = banks.take()
        for t in range(TT):
            m = pe(lambda e, t=t, b=b: e.transpose(bank[b][:, t * 36:(t + 1) * 36], LT[0:36, t * 128:(t + 1) * 128],
                                                   ident[0:36, 0:36]), lt_, bf, sig=(t == 3))
        lt_ = dve(lambda e, b=b: e.tensor_copy(route[:, 0:144], bank[b][:, 0:144]), m)
        banks.give(b, lt_)
        GL = L[:, :, 0:4]
        iota = con("iota")

        def first_max(src, n, after):
            mx, t, mn, oh = rt4(4), rt4(4, n), rt4(4), rt4(4, n)
            bc = lambda a: a.unsqueeze(2).to_broadcast([128, 4, n])
            a = dve(lambda e: e.tensor_reduce(mx, src, AX, ALU.max), after)
            c = dve(lambda e: e.tensor_tensor(t, src, bc(mx), ALU.is_equal), a)
            io = iota[:, 0:n].unsqueeze(1).to_broadcast([128, 4, n])
            d = dve(lambda e: e.scalar_tensor_tensor(out=t, in0=t, scalar=-100.0, in1=io, op0=ALU.mult, op1=ALU.add), c)
            f = dve(lambda e: e.tensor_reduce(mn, t, AX, ALU.min), d)
            return mx, oh, dve(lambda e: e.tensor_tensor(oh, t, bc(mn), ALU.is_equal), f)

        gm, goh, gt = first_max(GL, 4, lt_)
        prod, el = rt4(4, 32), rt4(4, 8)
        for t in range(TT):
            a = dve(lambda e, t=t: e.tensor_tensor(
                prod[:, t, :].rearrange("p (g e) -> p g e", g=4), L[:, t, 4:36].rearrange("p (g e) -> p g e", g=4),
                goh[:, t, :].unsqueeze(2).to_broadcast([128, 4, 8]), ALU.mult), gt)
        for t in range(TT):
            c = dve(lambda e, t=t: e.tensor_reduce(el[:, t, :], prod[:, t, :].rearrange("p (g e) -> p e g", g=4), AX,
                                                   ALU.add), a)
        m1, oh1, o1 = first_max(el, 8, c)
        el2 = rt4(4, 8)
        a = dve(lambda e: e.scalar_tensor_tensor(out=el2, in0=oh1, scalar=-3e38, in1=el, op0=ALU.mult, op1=ALU.add), o1)
        m2, oh2, o2 = first_max(el2, 8, a)
        s8 = rt4(4, 8)
        c = dve(lambda e: e.tensor_tensor(s8, oh1, oh2, ALU.add), o2)
        for t in range(TT):
            gb_ = goh[:, t, :].unsqueeze(2).to_broadcast([128, 4, 8])
            sel_t = dve(lambda e, t=t, gb_=gb_: e.tensor_tensor(
                SEL[:, t, :].rearrange("p (g e) -> p g e", g=4), s8[:, t, :].unsqueeze(1).to_broadcast([128, 4, 8]),
                gb_, ALU.mult), c)
        PRE = rt4(4, 32)
        pre_t = dve(lambda e: e.tensor_copy(PRE[:, 0, :], SEL[:, 0, :]), sel_t)
        for t in range(1, TT):
            pre_t = dve(lambda e, t=t: e.tensor_tensor(PRE[:, t, :], PRE[:, t - 1, :], SEL[:, t, :], ALU.add), pre_t)
        b, bf = banks.take()
        pe(lambda e, b=b: e.matmul(bank[b][:, 0:128], con("tri"), route[:, 400:528], start=True, stop=False), sel_t, bf,
           sig=False)
        pe(lambda e, b=b: e.matmul(bank[b][:, 32:128], con("ones"), PRE[:, 0:3, :].rearrange("p t e -> p (t e)"),
                                   start=False, stop=True), pre_t, sig=False)
        m = pe(lambda e, b=b: e.matmul(bank[b][:, 128:160], con("ones"), PRE[:, 3, :], start=True, stop=True))
        flat = lambda v: v.rearrange("p t e -> p (t e)")
        a = dve(lambda e, b=b: e.scalar_tensor_tensor(out=flat(RK), in0=bank[b][:, 0:128], scalar=1.0, in1=flat(SEL),
                                                      op0=ALU.add, op1=ALU.mult), m)
        mc, cm, nx = rt4(1), rt4(7), rt4(1)
        c = dve(lambda e, b=b: e.tensor_reduce(mc, bank[b][:, 128:160], AX, ALU.max), a)
        banks.give(b, c)
        rk_t = dve(lambda e: e.tensor_scalar(flat(RK), flat(RK), -1.0, None, ALU.add), c)
        c = dve(lambda e: e.tensor_scalar(cm, con("thr")[:, 0:7], mc, None, ALU.is_lt), c)
        c = dve(lambda e: e.tensor_reduce(nx, cm, AX, ALU.add), c)
        dve(lambda e: e.tensor_copy(nex_i[:, :], nx[0:1, :]), c)

        def weights():
            ge_, gs, gg = rt4(4, 4), rt4(4), rt4(4)
            a = dve(lambda e: e.tensor_tensor(ge_, GL, gm.unsqueeze(2).to_broadcast([128, 4, 4]), ALU.subtract), gt)
            a = act(lambda e: e.activation(ge_, ge_, ACT.Exp), a)
            a = dve(lambda e: e.tensor_reduce(gs, ge_, AX, ALU.add), a)
            gg_t = dve(lambda e: e.reciprocal(gg, gs), a)
            df, e2_, wa, wb = rt4(4), rt4(4), rt4(4), rt4(4)
            a = dve(lambda e: e.tensor_tensor(df, m2, m1, ALU.subtract), o2)
            x_ = act(lambda e: e.activation(e2_, df, ACT.Exp), a)
            a = dve(lambda e: e.tensor_scalar(wa, e2_, 1.0, None, ALU.add), x_)
            a = dve(lambda e: e.reciprocal(wa, wa), a)
            a = dve(lambda e: e.tensor_tensor(wa, wa, gg, ALU.mult), a, gg_t)
            a = dve(lambda e: e.tensor_tensor(wb, wa, e2_, ALU.mult), a)
            w8, w8b = rt4(4, 8), rt4(4, 8)
            bc8 = lambda v: v.unsqueeze(2).to_broadcast([128, 4, 8])
            a = dve(lambda e: e.tensor_tensor(w8, oh1, bc8(wa), ALU.mult), a)
            c = dve(lambda e: e.tensor_tensor(w8b, oh2, bc8(wb), ALU.mult), a)
            a = dve(lambda e: e.tensor_tensor(w8, w8, w8b, ALU.add), c)
            for t in range(TT):
                gb_ = goh[:, t, :].unsqueeze(2).to_broadcast([128, 4, 8])
                w = dve(lambda e, t=t, gb_=gb_: e.tensor_tensor(
                    W32[:, t, :].rearrange("p (g e) -> p g e", g=4), w8[:, t, :].unsqueeze(1).to_broadcast([128, 4, 8]),
                    gb_, ALU.mult), a)
            return w

        XET = [area(22528 + 2048 * i, 8, 256) for i in range(2)]
        free10 = everything()
        s_free = [free10]
        Sw_r = Ring([area(9216, 4, 4 * C)], free10)
        ST_r = Ring([v[:, :] for v in ST], free10)
        Y_r = Ring([(YH[i], YL[i]) for i in range(3)], free10)
        sg_r = Ring([area(19456 + 512 * i, 512) for i in range(2)], free10)
        hd_r = Ring([area(20480 + 512 * i, 512) for i in range(2)], free10)
        hT_r = Ring([area(21504 + 512 * i, 512) for i in range(2)], free10)
        xet_free = [free10, free10]
        gath, swT, w32_t = {}, {}, []

        def gather(g):
            Sw, wf = Sw_r.take()
            for t in range(TT):
                ib = iota.unsqueeze(1).to_broadcast([128, 4, C])
                rb = RK[:, t, 4 * g:4 * g + 4].unsqueeze(2).to_broadcast([128, 4, C])
                a = dve(lambda e, t=t, ib=ib, rb=rb: e.tensor_tensor(
                    S[:, t, :].rearrange("p (e s) -> p e s", e=4), ib, rb, ALU.is_equal), rk_t, s_free[0])
            if g == 0:
                w32_t.append(weights())
            for t in range(TT):
                wb_ = W32[:, t, 4 * g:4 * g + 4].unsqueeze(2).to_broadcast([128, 4, C])
                w_ = pool(lambda e, t=t, wb_=wb_: e.tensor_tensor(
                    Sw[:, t, :].rearrange("p (e s) -> p e s", e=4), S[:, t, :].rearrange("p (e s) -> p e s", e=4),
                    wb_, ALU.mult), a, wf, w32_t)
            Xe = XET[g % 2]
            out = []
            for kp in range(4):
                b, bf = banks.take()
                for kk in range(2):
                    k = 2 * kp + kk
                    for t in range(TT):
                        for i, v in enumerate((XSH, XSL)):
                            m = pe(lambda e, k=k, kk=kk, t=t, b=b, i=i, v=v: e.matmul(
                                bank[b][:, kk * 256:(kk + 1) * 256], v[:, t, k * 128:(k + 1) * 128], S[:, t, :],
                                start=(t == 0 and i == 0), stop=(t == 3 and i == 1)), a, bf, xs_t,
                                sig=(t == 3 and i == 1))
                for kk in range(2):
                    k = 2 * kp + kk
                    d = act(lambda e, k=k, kk=kk, b=b: e.activation(Xe[:, k, :], bank[b][:, kk * 256:(kk + 1) * 256],
                                                                    ACT.Copy, scale=col("ffn2", k)), m, xet_free[g % 2])
                banks.give(b, d)
                out.append(d)
            for q in range(2):
                b, bf = banks.take()
                for t in range(TT):
                    m2_ = pe(lambda e, t=t, q=q, b=b: e.transpose(bank[b][:, t * 128:(t + 1) * 128],
                                                                  Sw[:, t, q * 128:(q + 1) * 128], ident),
                             w_, bf, sig=(t == 3))
                T_, tf = ST_r.take()
                wc = stat()
                c = dve(lambda e, wc=wc, b=b: e.tensor_reduce(wc, bank[b][:, :], AX, ALU.add), m2_)
                d = dve(lambda e, T_=T_, b=b: e.tensor_scalar(T_, bank[b][:, :], 0.0, None, ALU.is_gt), m2_, tf)
                banks.give(b, d)
                swT[2 * g + q] = (T_, wc, d)
            s_free[0] = [m, w_]
            Sw_r.give(Sw, m2_)
            gath[g] = out

        hid = {}

        def hidden(p):
            Xe, xt_ = XET[(p // 2) % 2], gath[p // 2]
            o = (p % 2) * 2 * C
            ms = []
            for w in (1, 3):
                b, bf = banks.take()
                for kh in range(2):
                    us = [W(("e", w, 2 * p + s, kh), 4) for s in range(2)]
                    for k in range(4):
                        for s in range(2):
                            m = pe(lambda e, s=s, k=k, kh=kh, b=b, us=us: e.matmul(
                                bank[b][64 * s:64 * s + 64, :], Xe[:, 4 * kh + k, o + C * s:o + C * s + C],
                                us[s][0][:, k, :], start=(kh == 0 and k == 0), stop=(kh == 1 and k == 3)),
                                us[s][1], bf, xt_, sig=(k == 3 and s == 1))
                    for s in range(2):
                        Wdone(("e", w, 2 * p + s, kh), m)
                ms.append((b, m))
            if p % 2:
                xet_free[(p // 2) % 2] = m
            sg, sf = sg_r.take()
            hd, hf = hd_r.take()
            a = act(lambda e: e.activation(sg, bank[ms[0][0]][:, :], ACT.Silu), ms[0][1], sf)
            banks.give(ms[0][0], a)
            d = dve(lambda e: e.tensor_tensor(hd, sg, bank[ms[1][0]][:, :], ALU.mult), a, ms[1][1], hf)
            banks.give(ms[1][0], d)
            sg_r.give(sg, d)
            hid[p] = (hd, d)

        def turn(p):
            hd, d = hid[p]
            b, bf = banks.take()
            for k in range(4):
                m = pe(lambda e, k=k: e.transpose(bank[b][:, k * 128:(k + 1) * 128], hd[:, k * 128:(k + 1) * 128], ident),
                       d, bf, sig=(k == 3))
            hd_r.give(hd, m)
            hT, hf = hT_r.take()
            ev = dve(lambda e: e.tensor_copy(hT, bank[b][:, :]), m, hf)
            banks.give(b, ev)
            hid[p] = (hT, ev)

        ys = {}

        def second(p):
            hT, ev = hid[p]
            bs = [banks.take() for _ in range(2)]
            for kh in range(2):
                us = [W(("e", 2, 2 * p + s, kh), 2) for s in range(2)]
                for k in range(2):
                    for h in range(2):
                        for s in range(2):
                            kk = 2 * kh + k
                            m = pe(lambda e, s=s, k=k, kk=kk, h=h, us=us: e.matmul(
                                bank[bs[h][0]][64 * s:64 * s + 64, :], hT[:, kk * 128 + 64 * s:kk * 128 + 64 * s + 64],
                                us[s][0][:, k, h * 512:(h + 1) * 512], start=(kk == 0), stop=(kk == 3)),
                                us[s][1], bs[h][1], ev, sig=(s == 1 and h == 1 and k == 1))
                for s in range(2):
                    Wdone(("e", 2, 2 * p + s, kh), m)
            hT_r.give(hT, m)
            Y, yf = Y_r.take()
            wc, wt_ = swT[p][1:]
            ev = []
            for h in range(2):
                place = (slice(None), slice(h * 512, (h + 1) * 512))
                a = act(lambda e, h=h, place=place: e.activation(Y[0][place], bank[bs[h][0]][:, :], ACT.Copy, scale=wc),
                        m, yf, wt_)
                ev.append(dve(lambda e, h=h, place=place: e.scalar_tensor_tensor(
                    out=Y[1][place], in0=bank[bs[h][0]][:, :], scalar=wc, in1=Y[0][place], op0=ALU.mult,
                    op1=ALU.subtract), a))
                banks.give(bs[h][0], ev[h])
            ys[p] = (Y, ev)

        acc_t = {(t, h): [xs_t[t]] for t in range(TT) for h in range(2)}

        def scatter(ps):
            for t in range(TT):
                for h in range(2):
                    b, bf = banks.take()
                    for i, (p, q) in enumerate([(p, q) for p in ps for q in range(2)]):
                        last = i == 2 * len(ps) - 1
                        m = pe(lambda e, i=i, p=p, q=q, t=t, h=h, b=b, last=last: e.matmul(
                            bank[b][:, :], swT[p][0][:, t * 128:(t + 1) * 128], ys[p][0][q][:, h * 512:(h + 1) * 512],
                            start=(i == 0), stop=last), swT[p][2], ys[p][1], bf, sig=last)
                    dst = X[:, t, h * 512:(h + 1) * 512]
                    f = dve(lambda e, dst=dst, b=b: e.tensor_tensor(dst, bank[b][:, :], dst, ALU.add), m, acc_t[t, h])
                    banks.give(b, f)
                    acc_t[t, h] = f
            for p in ps:
                ST_r.give(swT[p][0], m)
                Y_r.give(ys[p][0], m)

        pT = area(8192, 2, 512)
        PN = area(22528, 4, 1024)
        pn_t = []

        def ple():
            w, wt = W(("ple", 0), 2)
            for t in range(TT):
                hs = []
                for h in range(2):
                    b, bf = banks.take()
                    for k in range(2):
                        m = pe(lambda e, k=k, t=t, h=h, b=b: e.matmul(
                            bank[b][:, :], pT[:, k, t * 128:(t + 1) * 128], w[:, k, h * 512:(h + 1) * 512],
                            start=(k == 0), stop=(k == 1)), wt, misc["pT"], bf, sig=(k == 1))
                    hs.append((bank[b][:, :], m, b))
                ss, s1 = stat(2), stat()
                q = sumsq(lambda i, hs=hs: hs[i][0], ss, hs[0][1], hs[1][1])
                a = dve(lambda e, s1=s1, ss=ss: e.tensor_tensor(s1, ss[:, 0:1], ss[:, 1:2], ALU.add), q)
                r, rt = rstd_of(s1, 1, D, a)
                for h in range(2):
                    z = dve(lambda e, h=h, t=t, hs=hs, r=r: e.scalar_tensor_tensor(
                        out=PN[:, t, h * 512:(h + 1) * 512], in0=hs[h][0], scalar=r,
                        in1=rowb[:, h * 512:(h + 1) * 512], op0=ALU.mult, op1=ALU.mult), rt, xet_free,
                        misc["row_ple"])
                    banks.give(hs[h][2], z)
                pn_t.append(z)
            Wdone(("ple", 0), m)

        gather(0)
        for p in range(NPAIR + 1):
            if p == NPAIR:
                ple()
            if p < NPAIR:
                hidden(p)
                if p == 1 or p >= 2 and p % 2 == 0 and p // 2 + 1 < NE // 4:
                    gather((p + 1) // 2 if p == 1 else p // 2 + 1)
                if p == NPAIR - 2:
                    load(pool, "pT", pT, pT_d, s_free[0])
            if p == NPAIR:
                scatter([NPAIR - 2])
            if p >= 1:
                second(p - 1)
                if p % 2 and p >= 3:
                    scatter([p - 3, p - 2])
            if p < NPAIR:
                turn(p)
        scatter([NPAIR - 1])

        with nc.Block() as block:
            @block.sync
            def _(e):
                sp.run(e)

            @block.gpsimd
            def _(e):
                pool.run(e)

            @block.scalar
            def _(e):
                act.run(e)

            @block.vector
            def _(e):
                dve.run(e)

            @block.tensor
            def _(e):
                pe.run(e)
        for q in (pe, act, dve, pool, sp):
            q.items.clear()

        overflow(nc, ctx, sem, dict(nex_i=nex_i, w1=w1_d, w3=w3_d, w2=w2_d, area=area, X=X, XS=(XSH, XSL), S=OS, RK=RK,
                                    W32=W32, con=con, col=col, bank=bank, ident=ident))

        everything_done = everything()
        for q in engines:
            for s_, v_ in everything_done:
                q.waited[s_.name] = v_
        banks = Ring(list(range(8)))
        xs_ring = Ring([area(1024 * i, 1024) for i in range(3)])
        y_ring = Ring([area(4096 + 512 * i, 512) for i in range(4)])
        tmp_ring = Ring([area(26624 + 512 * i, 512) for i in range(3)])
        w_hi[:], w_lo[:] = PH, PL
        to_split.extend(("plg", i) for i in range(4))
        split_free.clear()
        split_free.extend((i, None) for i in range(2))
        hT_t = norm_to_T("plg", [None] * TT, xs_ring, y_ring, lambda: first_split(4))
        ahead()
        fin = []
        for n in range(4):
            wh, wl, wt = split_W(("plg", n), KD)
            cs = slice(n * 256, (n + 1) * 256)
            for t in range(TT):
                b, bf = banks.take()
                for k in range(KD):
                    for i, (src, w) in enumerate(((HTH, wh), (HTH, wl), (HTL, wh))):
                        last = k == KD - 1 and i == 2
                        m = pe(lambda e, k=k, i=i, src=src, w=w, t=t, b=b, last=last: e.matmul(
                            bank[b][:, 0:256], src[:, k, t * 128:(t + 1) * 128], w[:, k, :],
                            start=(k == 0 and i == 0), stop=last), wt, hT_t[t], bf, sig=last)
                if t == TT - 1:
                    split_done(("plg", n), m)
                tmp, tf = tmp_ring.take()
                s = act(lambda e, b=b, tmp=tmp: e.activation(tmp[:, 0:256], bank[b][:, 0:256], ACT.Sigmoid), m, tf)
                banks.give(b, s)
                z = dve(lambda e, cs=cs, t=t, tmp=tmp: e.tensor_tensor(
                    tmp[:, 0:256], tmp[:, 0:256], PN[:, t, cs], ALU.mult), s, pn_t[t])
                f = dve(lambda e, cs=cs, t=t, tmp=tmp: e.tensor_tensor(
                    tmp[:, 256:512], tmp[:, 0:256], X[:, t, cs], ALU.add), z)
                od = sp.dma(out_d[t * 128:(t + 1) * 128, cs], tmp[:, 256:512], sem(f"d_out{n}_{t}"), 1, f)
                tmp_ring.give(tmp, od)
                fin.append(od)
        sp.wait(fin)

        with nc.Block() as block:
            @block.sync
            def _(e):
                sp.run(e)

            @block.gpsimd
            def _(e):
                pool.run(e)

            @block.scalar
            def _(e):
                act.run(e)

            @block.vector
            def _(e):
                dve.run(e)

            @block.tensor
            def _(e):
                pe.run(e)


def overflow(nc, ctx, sem, v):
    con, bank, ident, X, XS = v["con"], v["bank"], v["ident"], v["X"], v["XS"]
    reg = v["area"]
    iota = con("iota")

    wA, wB, wC = (reg(8192 + 4096 * i, 4096) for i in range(3))
    oh = reg(20480, 32)
    pr = reg(20512, 4, 32)
    rc, wc = reg(20640, 4), reg(20644, 4)
    cnt = reg(20648, 1)
    rnd = reg(20649, 1)
    S, Sw = v["S"][:, :, :], reg(20960, 4, C)
    SwT, sg, hd = reg(21216, 512), reg(8192, 512), reg(8704, 512)
    hT = reg(9216, 4, C)
    Y = reg(9472, 1024)
    Xe = reg(21760, 8, C)
    s_d, s_p, s_a, s_v, s_i = sem("o_d"), sem("o_p"), sem("o_a"), sem("o_v"), sem("o_i")

    with nc.Block() as block:
        @block.vector
        def _(e):
            e.memset(rnd, float(C)).then_inc(s_i, 1)
            e.wait_ge(s_i, 1)

    n = nc.values_load(v["nex_i"][0:1, 0:1], min_val=0, max_val=NTOK // C - 1)
    with nc.If(n > 0):
        with nc.Fori(0, n):
            with nc.Block() as block:
                @block.vector
                def _(e):
                    e.memset(cnt, 0.0).then_inc(s_v, 1)
                    e.wait_ge(s_v, 1)
            nc.all_engine_barrier()
            nc.gpsimd.sem_clear(s_v)
            nc.all_engine_barrier()
            with nc.Fori(0, NE) as ei:
                pe, act, dve, sp = Queue(s_p), Queue(s_a), Queue(s_v), Queue(s_d)
                for i, (w, src, k) in enumerate(((wA, v["w1"], 8), (wB, v["w3"], 8), (wC, v["w2"], 4))):
                    s = src[bass.ds(ei, 1), :, :].rearrange("a (k p) n -> p (a k) n", p=128)
                    d_t = sp.dma(w.rearrange("p (k n) -> p k n", k=k), s, s_d, i + 1)
                a = dve(lambda e: e.tensor_scalar(oh, iota[:, 0:32], cnt, None, ALU.is_equal))
                a = dve(lambda e: e.tensor_scalar(cnt, cnt, 1.0, None, ALU.add), a)
                ohb = oh.unsqueeze(1).to_broadcast([128, 4, 32])
                for src, dst in ((v["RK"], rc), (v["W32"], wc)):
                    a = dve(lambda e, src=src: e.tensor_tensor(pr, src, ohb, ALU.mult), a)
                    a = dve(lambda e, dst=dst: e.tensor_reduce(dst, pr, AX, ALU.add), a)
                a = dve(lambda e: e.tensor_scalar(rc, rc, rnd, None, ALU.subtract), a)
                ib = iota.unsqueeze(1).to_broadcast([128, 4, C])
                a = dve(lambda e: e.tensor_tensor(S, ib, rc.unsqueeze(2).to_broadcast([128, 4, C]), ALU.is_equal), a)
                sw = dve(lambda e: e.tensor_tensor(Sw, S, wc.unsqueeze(2).to_broadcast([128, 4, C]), ALU.mult), a)
                for k in range(KD):
                    for i, (t, x) in enumerate([(t, x) for t in range(TT) for x in XS]):
                        m = pe(lambda e, k=k, t=t, i=i, x=x: e.matmul(
                            bank[0][:, k * C:(k + 1) * C], x[:, t, k * 128:(k + 1) * 128], S[:, t, :],
                            start=(i == 0), stop=(i == 7)), a, sig=(i == 7))
                for t in range(TT):
                    m2 = pe(lambda e, t=t: e.transpose(bank[1][0:C, t * 128:(t + 1) * 128], Sw[:, t, :], ident),
                            sw, sig=(t == 3))
                for k in range(KD):
                    x = act(lambda e, k=k: e.activation(Xe[:, k, :], bank[0][:, k * C:(k + 1) * C], ACT.Copy,
                                                        scale=v["col"]("ffn2", k)), m)
                x2 = act(lambda e: e.activation(SwT[0:C, :], bank[1][0:C, :], ACT.Copy), m2)
                for w, b in ((wA, 2), (wB, 3)):
                    for k in range(KD):
                        m = pe(lambda e, w=w, b=b, k=k: e.matmul(bank[b][0:C, :], Xe[:, k, :],
                                                                 w[:, k * 512:(k + 1) * 512], start=(k == 0),
                                                                 stop=(k == 7)), x, d_t, sig=(k == 7))
                g = act(lambda e: e.activation(sg[0:C, :], bank[2][0:C, :], ACT.Silu), m)
                h = dve(lambda e: e.tensor_tensor(hd[0:C, :], sg[0:C, :], bank[3][0:C, :], ALU.mult), g)
                for k in range(4):
                    m = pe(lambda e, k=k: e.transpose(bank[4][:, k * C:(k + 1) * C], hd[0:C, k * 128:(k + 1) * 128],
                                                      ident[0:C, 0:C]), h, sig=(k == 3))
                c = dve(lambda e: e.tensor_copy(hT.rearrange("p a b -> p (a b)"), bank[4][:, 0:4 * C]), m)
                for hh in range(2):
                    for k in range(4):
                        m = pe(lambda e, hh=hh, k=k: e.matmul(
                            bank[5 + hh][0:C, :], hT[:, k, :], wC[:, k * 1024 + hh * 512:k * 1024 + hh * 512 + 512],
                            start=(k == 0), stop=(k == 3)), c, sig=(k == 3))
                    y = dve(lambda e, hh=hh: e.tensor_copy(Y[0:C, hh * 512:(hh + 1) * 512], bank[5 + hh][0:C, :]), m)
                f = None
                for t in range(TT):
                    for hh in range(2):
                        m = pe(lambda e, t=t, hh=hh: e.matmul(bank[7][:, :], SwT[0:C, t * 128:(t + 1) * 128],
                                                              Y[0:C, hh * 512:(hh + 1) * 512], start=True, stop=True),
                               y, x2, f)
                        dst = X[:, t, hh * 512:(hh + 1) * 512]
                        f = dve(lambda e, dst=dst: e.tensor_tensor(dst, bank[7][:, :], dst, ALU.add), m)
                dve.wait(f)
                with nc.Block() as block:
                    @block.sync
                    def _(e):
                        sp.run(e)

                    @block.scalar
                    def _(e):
                        act.run(e)

                    @block.vector
                    def _(e):
                        dve.run(e)

                    @block.tensor
                    def _(e):
                        pe.run(e)
                nc.all_engine_barrier()
                for s in (s_d, s_p, s_a, s_v):
                    nc.gpsimd.sem_clear(s)
                nc.all_engine_barrier()
            with nc.Block() as block:
                @block.vector
                def _(e):
                    e.tensor_scalar(rnd, rnd, float(C), None, ALU.add).then_inc(s_v, 1)
                    e.wait_ge(s_v, 1)
            nc.all_engine_barrier()
            nc.gpsimd.sem_clear(s_v)
            nc.all_engine_barrier()


def _by_cols(w, width=256):
    k, n = w.shape
    return w.reshape(k // 128, 128, n // width, width).transpose(2, 1, 0, 3).reshape(n // width, 128, -1)


def _by_half(w):
    n = w.shape[1]
    return w.reshape(2, 4, 128, n // 512, 512).transpose(3, 0, 2, 1, 4).reshape(n // 256, 128, -1)


def _by_rows(w):
    return w.reshape(-1, 2, 128, 1024).transpose(0, 2, 1, 3).reshape(-1, 128, 2048)


def _tiles(v):
    return v.reshape(-1, 128).T


def _layout(i):
    w_in, w_up = _by_cols(i["w_in"][0]), _by_cols(i["w_up"][0])
    ao, po = _by_cols(i["w_attn_out"][0]), _by_cols(i["w_pool_out"][0])
    dn = _by_rows(i["w_down"][0])
    in_half = _by_half(i["w_in"][0])
    seq = [in_half[n] if n in (4, 5) else w_in[n] for n in range(8)]
    for n in range(4):
        seq += [np.concatenate([ao[n], po[n]], axis=1), w_in[8 + n], w_in[12 + n]]
    seq += list(_by_half(i["w_o"][0]))
    for us, ds in ffn_order():
        for u in us:
            seq += [w_up[u], w_up[11 + u]]
        seq += [dn[d] for d in ds]
    in2, in2_half = _by_cols(i["w_in_2"][0]), _by_half(i["w_in_2"][0])
    seq += [in2_half[n] if n < 10 else in2[n] for n in range(12)] + list(_by_half(i["w_out_2"][0]))
    seq += list(_by_rows(i["w_ple_2"][0])) + list(_by_cols(i["w_plg_2"][0]))

    cols = np.concatenate([_tiles(i[n].reshape(-1)) for n in (
        "norm_mix_pre", "norm_ffn_pre", "g_mix_2", "g_ffn_2", "g_plg_2", "b_gate", "pool_scale", "conv_w", "conv_b",
        "g_sub_2")], axis=1)
    rows = np.concatenate([i[n].reshape(-1) for n in (
        "norm_mix_post", "norm_ffn_post", "g_ple_2", "g_qa_2", "g_ka_2", "g_qb_2", "g_kb_2", "lam_q1_2", "lam_k1_2",
        "lam_q2_2", "lam_k2_2")])[None, :]

    p = np.arange(128)
    dist = p[:, None] + 384 - np.arange(512)[None, :]
    tb = i["rel_bias"][0][:, np.clip(dist, -256, 256) + 256]
    tb = np.where((p[:, None] < 64) & (np.arange(512)[None, :] >= 448), np.float32(NEG), tb).transpose(1, 0, 2)

    r, c = p // 16, p % 16
    kr, kc = np.arange(256) // 32, np.arange(256) % 32
    nb = np.empty((4, 128, 4, 3, 256), np.float32)
    for jt, (q0, k0) in enumerate(((0, 0), (16, 8), (48, 32))):
        qc, kcol = q0 + c, k0 + kc
        cs = np.clip(qc - 8, 0, 48)
        ok = (kcol[None, :] >= cs[:, None]) & (kcol[None, :] < cs[:, None] + 16)
        off = np.clip(kcol[None, :] - qc[:, None] + 15, 0, 30)
        ro = kr[None, :] - r[:, None] + 7
        t = np.where(ok, i["rpb_2"][0][:, ro, off], np.float32(NEG))
        nb[:, :, :, jt, :] = t.reshape(4, 4, 128, 256).transpose(0, 2, 1, 3)

    t = np.arange(NTOK, dtype=np.float32)
    inv = (np.float32(10000.0) ** (-np.arange(0, 64, 2, dtype=np.float32) / np.float32(64))).astype(np.float32)
    ang = (t[:, None] * inv[None, :]).astype(np.float32)
    by_tok = lambda a: a.reshape(4, 128, 32).transpose(1, 0, 2).reshape(128, 128)
    cnt = np.stack([1.0 / np.minimum(np.arange(16) + 1, 2 << g) for g in range(4)]).reshape(1, 64)
    one = np.ones((128, 1))
    cst = np.concatenate([np.eye(128), np.triu(np.ones((128, 128)), 1), np.ones((128, 128)),
                          one * np.arange(64)[None, :], one * (C * (1 + np.arange(8)))[None, :], one * cnt,
                          by_tok(np.cos(ang)), by_tok(np.sin(ang))], axis=1).astype(np.float32)
    wr = np.concatenate([i["w_rg_2"][0], i["w_re_2"][0]], axis=1).reshape(8, 128, 36).transpose(1, 0, 2)
    return {
        "x": i["x"][0], "wd": np.stack(seq), "w1": i["w1_2"][0], "w3": i["w3_2"][0], "w2": i["w2_2"][0],
        "cols": cols, "rows": rows, "cst": cst, "wr": wr, "wpg": i["w_pool_group"][0].transpose(1, 0, 2),
        "pT": i["p_2"][0, 0].T.reshape(2, 128, 512).transpose(1, 0, 2), "tb": tb, "nb": nb.reshape(4, 128, 3072),
    }


def kernel(**inputs):
    import concourse.bacc as bacc
    from concourse.bass_utils import run_bass_kernel_spmd

    nc = bacc.Bacc("TRN2", target_bir_lowering=False, num_devices=1)
    arrays, args = {}, []
    for name, a in _layout({k: np.asarray(v) for k, v in inputs.items()}).items():
        a = np.ascontiguousarray(a)
        arrays[f"in_{name}"] = a
        args.append(nc.dram_tensor(f"in_{name}", a.shape, mybir.dt.from_np(a.dtype), kind="ExternalInput").ap())
    out = nc.dram_tensor("out_0", (NTOK, D), F32, kind="ExternalOutput").ap()
    build(nc, *args, out)
    r = run_bass_kernel_spmd(nc, [arrays], core_ids=[0])
    return r.results[0]["out_0"].reshape(1, NTOK, D)
```
